# Optimizing a Trainium2 kernel written in Bass

```python
import jax, jax.numpy as jnp
from jax import lax
import numpy as np

D_MODEL = 1024
BATCH = 1
SEQ = 1024
DEPTH = 2

HEAD_DIM = 64
N_FOX_HEADS = D_MODEL // (2 * HEAD_DIM)
N_RWKV_HEADS = D_MODEL // (2 * HEAD_DIM)
FOX_WIDTH = N_FOX_HEADS * HEAD_DIM
RWKV_WIDTH = N_RWKV_HEADS * HEAD_DIM
DECAY_LORA = 64
ICLR_LORA = 64
GATE_LORA = 128
RWKV_IN = 3 * RWKV_WIDTH + DECAY_LORA + ICLR_LORA + GATE_LORA
FOX_IN = 3 * FOX_WIDTH + N_FOX_HEADS
EVEN_IN = FOX_IN + RWKV_IN
RWKV_SPLITS = [RWKV_WIDTH, 2 * RWKV_WIDTH, 3 * RWKV_WIDTH,
               3 * RWKV_WIDTH + DECAY_LORA, 3 * RWKV_WIDTH + DECAY_LORA + ICLR_LORA]
N_DIL_HEADS = D_MODEL // HEAD_DIM
DIL_WIDTH = N_DIL_HEADS * HEAD_DIM
ODD_IN = 3 * DIL_WIDTH
DILATED_GROUPS = ((128, 1), (512, 4), (2048, 16))
ROPE_THETA = 500000.0
ROPE_DIMS = HEAD_DIM // 4
D_FF = ((8 * D_MODEL // 3 + 127) // 128) * 128
CONV_WIDTH = 3
Q_BLOCK = 128
RMS_EPS = 1e-6
GN_EPS = 64e-5
NEG_INF = -1e30
N_EVEN = (DEPTH + 1) // 2
N_ODD = DEPTH // 2

kernel_name = "fox_rwkv7_dilated_hybrid"

def rms_norm(x, g):
    xf = x.astype(jnp.float32)
    y = xf * lax.rsqrt(jnp.mean(xf * xf, axis=-1, keepdims=True) + RMS_EPS)
    return (y * g.astype(jnp.float32)).astype(x.dtype)

def shift_right(t):
    return jnp.pad(t, ((0, 0), (1, 0), (0, 0)))[:, :-1]

def rotary_tables(positions):
    inv_freq = ROPE_THETA ** (-jnp.arange(0, ROPE_DIMS, 2, dtype=jnp.float32) / ROPE_DIMS)
    ang = positions.astype(jnp.float32)[..., None] * inv_freq
    return jnp.cos(ang)[:, :, None, :], jnp.sin(ang)[:, :, None, :]

def partial_rotary(t, cos, sin):
    half = ROPE_DIMS // 2
    t1, t2 = t[..., :half], t[..., half:ROPE_DIMS]
    rot = jnp.concatenate([t1 * cos - t2 * sin, t1 * sin + t2 * cos], axis=-1).astype(t.dtype)
    return jnp.concatenate([rot, t[..., ROPE_DIMS:]], axis=-1)

def forgetting_attention(q, k, v, log_f):
    B, T, H, Dh = q.shape
    nb = T // Q_BLOCK
    scale = Dh ** -0.5
    c = jnp.cumsum(log_f, axis=1)
    c_k = c.transpose(0, 2, 1)[:, :, None, :]
    k_pos = jnp.arange(T)
    qb = q.reshape(B, nb, Q_BLOCK, H, Dh).transpose(1, 0, 2, 3, 4)
    cb = c.reshape(B, nb, Q_BLOCK, H).transpose(1, 0, 2, 3)

    def block(args):
        q_blk, c_blk, i = args
        s = jnp.einsum('bqhd,bkhd->bhqk', q_blk, k, preferred_element_type=jnp.float32) * scale
        s = s + c_blk.transpose(0, 2, 1)[..., None] - c_k
        q_pos = i * Q_BLOCK + jnp.arange(Q_BLOCK)
        s = jnp.where(q_pos[:, None] >= k_pos[None, :], s, NEG_INF)
        p = jax.nn.softmax(s, axis=-1)
        return jnp.einsum('bhqk,bkhd->bqhd', p.astype(v.dtype), v)

    o = lax.map(block, (qb, cb, jnp.arange(nb)))
    return o.transpose(1, 0, 2, 3, 4).reshape(B, T, H, Dh)

def rwkv7_scan(r, w, k, v, a, b):
    B, T, H, N = r.shape

    def step(S, inp):
        r_t, w_t, k_t, v_t, a_t, b_t = inp
        sa = jnp.einsum('bhvk,bhk->bhv', S, a_t)
        S = S * w_t[:, :, None, :] + sa[..., None] * b_t[:, :, None, :] + v_t[..., None] * k_t[:, :, None, :]
        return S, jnp.einsum('bhvk,bhk->bhv', S, r_t)

    xs = tuple(t.transpose(1, 0, 2, 3) for t in (r, w, k, v, a, b))
    _, y = lax.scan(step, jnp.zeros((B, H, N, N), jnp.float32), xs)
    return y.transpose(1, 0, 2, 3)

def rwkv7_time_mix(z, mu, w0, w2, a0, a2, g2, k_k, k_a, r_k, ln_w, ln_b):
    B, T, _ = z.shape
    H, N = N_RWKV_HEADS, HEAD_DIM
    heads = lambda t: t.reshape(B, T, H, N)
    z = z.astype(jnp.float32)
    z = z + (shift_right(z) - z) * mu
    r, k, v, w_lo, a_lo, g_lo = jnp.split(z, RWKV_SPLITS, axis=-1)
    w = -jax.nn.softplus(-(w0 + jnp.tanh(w_lo) @ w2)) - 0.5
    decay = jnp.exp(-jnp.exp(w))
    a = jax.nn.sigmoid(a0 + a_lo @ a2)
    g = jax.nn.sigmoid(g_lo) @ g2
    kk = heads(k * k_k)
    kk = kk / jnp.maximum(jnp.sqrt(jnp.sum(kk * kk, axis=-1, keepdims=True)), 1e-12)
    k = k * (1 + (a - 1) * k_a)
    y = rwkv7_scan(heads(r), heads(decay), heads(k), heads(v), -kk, kk * heads(a))
    mean = jnp.mean(y, axis=-1, keepdims=True)
    var = jnp.mean(jnp.square(y - mean), axis=-1, keepdims=True)
    y = ((y - mean) * lax.rsqrt(var + GN_EPS)).reshape(B, T, RWKV_WIDTH) * ln_w + ln_b
    bonus = jnp.sum(heads(r) * heads(k) * r_k, axis=-1, keepdims=True) * heads(v)
    return (y + bonus.reshape(B, T, RWKV_WIDTH)) * g

def fox_rwkv_mixer(h, w_in, forget_bias, mu, w0, w2, a0, a2, g2, k_k, k_a, r_k, ln_w, ln_b, w_out):
    B, T, _ = h.shape
    z = h @ w_in
    fz, rz = z[..., :FOX_IN], z[..., FOX_IN:]
    q, k, v = [fz[..., i * FOX_WIDTH:(i + 1) * FOX_WIDTH].reshape(B, T, N_FOX_HEADS, HEAD_DIM)
               for i in range(3)]
    log_f = jax.nn.log_sigmoid((fz[..., 3 * FOX_WIDTH:] + forget_bias).astype(jnp.float32))
    y_fox = forgetting_attention(q, k, v, log_f).reshape(B, T, FOX_WIDTH)
    y_rwkv = rwkv7_time_mix(rz, mu, w0, w2, a0, a2, g2, k_k, k_a, r_k, ln_w, ln_b)
    y = jnp.concatenate([y_fox, y_rwkv.astype(y_fox.dtype)], axis=-1)
    return y @ w_out

def dilated_branch(q, k, v, window, dilation):
    B, T, H, Dh = q.shape
    span = window // dilation
    L = T // dilation
    nb = -(-L // span)
    Lp = nb * span
    scale = Dh ** -0.5

    def to_blocks(t):
        t = t.reshape(B, L, dilation, H, Dh).transpose(2, 0, 1, 3, 4)
        t = jnp.pad(t, ((0, 0), (0, 0), (0, Lp - L), (0, 0), (0, 0)))
        return t.reshape(dilation, B, nb, span, H, Dh)

    def band(t):
        prev = jnp.pad(t[:, :, :-1], ((0, 0), (0, 0), (1, 0), (0, 0), (0, 0), (0, 0)))
        return jnp.concatenate([prev, t], axis=3)

    def flat(t):
        t = jnp.swapaxes(t, 1, 2)
        return t.reshape((dilation * nb,) + t.shape[2:])

    qf = flat(to_blocks(q))
    kf = flat(band(to_blocks(k)))
    vf = flat(band(to_blocks(v)))
    blk_n = jnp.tile(jnp.arange(nb), dilation)
    qi = jnp.arange(span)[:, None]
    ki = jnp.arange(2 * span)[None, :]
    delta = qi - ki + span
    band_mask = (delta >= 0) & (delta <= span)

    def one(args):
        qx, kx, vx, n = args
        s = jnp.einsum('bqhd,bkhd->bhqk', qx, kx, preferred_element_type=jnp.float32) * scale
        valid = band_mask & ((ki >= span) | (n > 0))
        s = jnp.where(valid, s, NEG_INF)
        m = jnp.max(s, axis=-1, keepdims=True)
        e = jnp.exp(s - m)
        den = jnp.sum(e, axis=-1, keepdims=True)
        o = jnp.einsum('bhqk,bkhd->bqhd', (e / den).astype(vx.dtype), vx)
        return o, (m + jnp.log(den))[..., 0]

    o, lse = lax.map(one, (qf, kf, vf, blk_n))
    o = o.reshape(dilation, nb, B, span, H, Dh).transpose(2, 1, 3, 0, 4, 5)
    o = o.reshape(B, Lp, dilation, H, Dh)[:, :L].reshape(B, T, H, Dh)
    lse = lse.reshape(dilation, nb, B, H, span).transpose(2, 1, 4, 0, 3)
    lse = lse.reshape(B, Lp, dilation, H)[:, :L].reshape(B, T, H)
    return o, lse

def dilated_mixer(h, w_in, w_out, cos, sin):
    B, T, _ = h.shape
    z = h @ w_in
    q, k, v = [z[..., i * DIL_WIDTH:(i + 1) * DIL_WIDTH].reshape(B, T, N_DIL_HEADS, HEAD_DIM)
               for i in range(3)]
    q = partial_rotary(q, cos, sin)
    k = partial_rotary(k, cos, sin)
    outs, lses = zip(*[dilated_branch(q, k, v, w, d) for (w, d) in DILATED_GROUPS])
    wts = jax.nn.softmax(jnp.stack(lses, axis=0), axis=0)
    o = jnp.sum(wts[..., None] * jnp.stack(outs, axis=0).astype(jnp.float32), axis=0)
    return o.reshape(B, T, DIL_WIDTH).astype(h.dtype) @ w_out

def conv_ffn(h, w_up, conv_w, conv_b, w_down):
    T = h.shape[1]
    u = h @ w_up
    up = jnp.pad(u, ((0, 0), (CONV_WIDTH - 1, 0), (0, 0)))
    acc = conv_b
    for j in range(CONV_WIDTH):
        acc = acc + conv_w[j] * up[:, j:j + T]
    gate, val = jnp.split(acc, 2, axis=-1)
    return (jax.nn.gelu(gate, approximate=True) * val) @ w_down

def setup_inputs(seed: int = 0) -> dict:
    key = jax.random.key(seed)
    ks = iter(jax.random.split(key, 32))
    nrm = lambda shape, scale: jax.random.normal(next(ks), shape, jnp.float32) * scale
    uni = lambda shape, lo, hi: jax.random.uniform(next(ks), shape, jnp.float32, lo, hi)
    x = jax.random.normal(next(ks), (BATCH, SEQ, D_MODEL), jnp.float32)
    offsets = jax.random.randint(next(ks), (BATCH, 1), 0, 4096, dtype=jnp.int32)
    positions = (jnp.arange(SEQ, dtype=jnp.int32)[None, :] + offsets).astype(jnp.int32)
    conv_w = jnp.zeros((DEPTH, CONV_WIDTH, 2 * D_FF), jnp.float32).at[:, -1].set(1.0) \
        + nrm((DEPTH, CONV_WIDTH, 2 * D_FF), 0.1)
    return {
        "x": x,
        "positions": positions,
        "norm_mix_pre": 1.0 + nrm((DEPTH, D_MODEL), 0.02),
        "norm_mix_post": 1.0 + nrm((DEPTH, D_MODEL), 0.02),
        "norm_ffn_pre": 1.0 + nrm((DEPTH, D_MODEL), 0.02),
        "norm_ffn_post": 1.0 + nrm((DEPTH, D_MODEL), 0.02),
        "even_w_in": nrm((N_EVEN, D_MODEL, EVEN_IN), D_MODEL ** -0.5),
        "fox_forget_bias": uni((N_EVEN, N_FOX_HEADS), 2.0, 5.0),
        "rwkv_mu": uni((N_EVEN, RWKV_IN), 0.0, 1.0),
        "rwkv_w0": uni((N_EVEN, RWKV_WIDTH), -6.0, 1.0),
        "rwkv_w2": nrm((N_EVEN, DECAY_LORA, RWKV_WIDTH), 0.5 * DECAY_LORA ** -0.5),
        "rwkv_a0": nrm((N_EVEN, RWKV_WIDTH), 0.1),
        "rwkv_a2": nrm((N_EVEN, ICLR_LORA, RWKV_WIDTH), 0.5 * ICLR_LORA ** -0.5),
        "rwkv_g2": nrm((N_EVEN, GATE_LORA, RWKV_WIDTH), GATE_LORA ** -0.5),
        "rwkv_k_k": 0.85 + nrm((N_EVEN, RWKV_WIDTH), 0.05),
        "rwkv_k_a": 1.0 + nrm((N_EVEN, RWKV_WIDTH), 0.05),
        "rwkv_r_k": nrm((N_EVEN, N_RWKV_HEADS, HEAD_DIM), 0.1),
        "rwkv_ln_w": 1.0 + nrm((N_EVEN, RWKV_WIDTH), 0.02),
        "rwkv_ln_b": nrm((N_EVEN, RWKV_WIDTH), 0.02),
        "even_w_out": nrm((N_EVEN, FOX_WIDTH + RWKV_WIDTH, D_MODEL), (FOX_WIDTH + RWKV_WIDTH) ** -0.5),
        "odd_w_in": nrm((N_ODD, D_MODEL, ODD_IN), D_MODEL ** -0.5),
        "odd_w_out": nrm((N_ODD, DIL_WIDTH, D_MODEL), DIL_WIDTH ** -0.5),
        "ffn_w_up": nrm((DEPTH, D_MODEL, 2 * D_FF), D_MODEL ** -0.5),
        "ffn_conv_w": conv_w,
        "ffn_conv_b": nrm((DEPTH, 2 * D_FF), 0.02),
        "ffn_w_down": nrm((DEPTH, D_FF, D_MODEL), D_FF ** -0.5),
    }

def reference(x, positions, norm_mix_pre, norm_mix_post, norm_ffn_pre, norm_ffn_post,
              even_w_in, fox_forget_bias, rwkv_mu, rwkv_w0, rwkv_w2, rwkv_a0, rwkv_a2, rwkv_g2,
              rwkv_k_k, rwkv_k_a, rwkv_r_k, rwkv_ln_w, rwkv_ln_b, even_w_out,
              odd_w_in, odd_w_out, ffn_w_up, ffn_conv_w, ffn_conv_b, ffn_w_down):
    cos, sin = rotary_tables(positions)
    for layer in range(DEPTH):
        i = layer // 2
        h = rms_norm(x, norm_mix_pre[layer])
        if layer % 2 == 0:
            m = fox_rwkv_mixer(h, even_w_in[i], fox_forget_bias[i], rwkv_mu[i], rwkv_w0[i],
                               rwkv_w2[i], rwkv_a0[i], rwkv_a2[i], rwkv_g2[i], rwkv_k_k[i],
                               rwkv_k_a[i], rwkv_r_k[i], rwkv_ln_w[i], rwkv_ln_b[i], even_w_out[i])
        else:
            m = dilated_mixer(h, odd_w_in[i], odd_w_out[i], cos, sin)
        x = x + rms_norm(m, norm_mix_post[layer]).astype(x.dtype)
        h = rms_norm(x, norm_ffn_pre[layer])
        f = conv_ffn(h, ffn_w_up[layer], ffn_conv_w[layer], ffn_conv_b[layer], ffn_w_down[layer])
        x = x + rms_norm(f, norm_ffn_post[layer]).astype(x.dtype)
    return x


_drawn_inputs = setup_inputs


def setup_inputs(seed=0):
    import zlib

    import numpy as np

    out = dict(_drawn_inputs(seed))
    spreads = {}
    factors = {'norm_ffn_post': 3.219, 'rwkv_ln_w': 3.488, 'rwkv_ln_b': 6.662}
    for name, (base, spread) in spreads.items():
        noise = np.random.default_rng([zlib.crc32(name.encode()), seed]).standard_normal(out[name].shape)
        drawn = base * np.exp(spread * noise) if base else spread * noise
        out[name] = __import__('jax').numpy.asarray(drawn.astype(out[name].dtype))
    for name, factor in factors.items():
        out[name] = (out[name] * factor).astype(out[name].dtype)
    return out
```

```python
from contextlib import ExitStack

import numpy as np

import concourse.bass as bass
from concourse import mybir

F32 = mybir.dt.float32
F32R = mybir.dt.float32r
BF16 = mybir.dt.bfloat16
I32 = mybir.dt.int32
ACT = mybir.ActivationFunctionType
ALU = mybir.AluOpType
AX_X = mybir.AxisListType.X
ds = bass.ds

P = 128
D = 1024
T = 1024
KT = D // P
TT = T // P
HALF = 512
HD = 64
N_FOX = 8
N_RWKV = 8
FOX_W = N_FOX * HD
RWKV_W = N_RWKV * HD
RW_T = RWKV_W // P
FOX_IN = 3 * FOX_W + N_FOX
RWKV_IN = 3 * RWKV_W + 256
DIL_W = D
D_FF = ((8 * D // 3 + 127) // 128) * 128
FT = D_FF // P
CONV = 3
RMS_EPS = 1e-6
GN_EPS = 64e-5
CHUNK = 64
DECAY = float(np.exp(-0.5))
ATT_SCALE = HD ** -0.5
NEG = -1e30

BASE = 16512
A_OFF = BASE
B_OFF = A_OFF + 65536
W_OFF = B_OFF + 90112
T_OFF = W_OFF + 28672
C_OFF = T_OFF + 20608

V_PRE = 0
V_MU = 32
V_W0, V_A0, V_KK, V_KA, V_RK, V_LW, V_LB = (46 + 4 * n for n in range(7))
V_ROWS = 74

K_ID = 0
K_BLK = 128
K_AB = 256
K_L = 768
K_M1 = 896
K_LEV = 1152
K_ID64 = 1792
K_RESET = 1856
K_FREQ = 2368
K_CAUS = 2370
K_COLS = 2498


def constants():
    i, j = np.arange(P)[:, None], np.arange(P)[None, :]
    same = (i // CHUNK) == (j // CHUNK)
    c = np.zeros((P, K_COLS), np.float32)
    c[:, K_ID:K_ID + P] = i == j
    c[:, K_BLK:K_BLK + P] = same
    strict_t, incl_t = same & (i < j), same & (i <= j)
    for n, m in enumerate((strict_t, incl_t, strict_t, incl_t)):
        c[:, K_AB + n * P:K_AB + (n + 1) * P] = m
    c[:, K_L:K_L + P] = same & (i > j)

    def lower_left(b):
        return ((i // (2 * b)) == (j // (2 * b))) & (i % (2 * b) >= b) & (j % (2 * b) < b)
    c[:, K_M1:K_M1 + P] = lower_left(1)
    c[:, K_M1 + P:K_M1 + 2 * P] = lower_left(1).T
    for n in range(5):
        c[:, K_LEV + n * P:K_LEV + (n + 1) * P] = lower_left(2 << n).T
    c[:, K_ID64:K_ID64 + 64] = (i % 64) == j[:, :64]
    c[:, K_RESET:K_RESET + HALF] = (np.arange(HALF) % CHUNK != 0)[None]
    rot = HD // 4
    freq = np.float32(500000.0) ** (-np.arange(0, rot, 2, dtype=np.float32) / np.float32(rot))
    for r in range(P):
        d = r % HD
        if d < rot:
            c[r, K_FREQ] = freq[d % (rot // 2)]
            c[r, K_FREQ + 1] = -1.0 if d < rot // 2 else 1.0
    c[:, K_CAUS:K_CAUS + P] = np.where(j > i, NEG, 0.0)
    dist = i - np.arange(T)[None, :] + (TT - 1) * P
    count = sum((dist >= 0) & (dist % d == 0) & (dist <= w) for w, d in ((128, 1), (512, 4), (2048, 16)))
    dil = np.stack([np.where(count > 0, 0.0, NEG), count], 1).astype(np.float32)
    return c, dil


def build(nc, x, positions, g_post, vecs, conv, w_in0, w_out0, w_in1, w_out1, w_up, w_down,
          forget_bias, w2, a2, g2, consts, dil, out):
    top = ExitStack()

    def at(name, shape, dt, off):
        return nc.alloc_sbuf_tensor_at(name, shape, dt, offset=off)

    ident = at("ident", [P, P], F32, C_OFF)
    vec = at("vec", [P, V_ROWS], F32, C_OFF + 512)
    h_hi = at("h_hi", [P, KT, T], F32R, A_OFF)
    h_lo = at("h_lo", [P, KT, T], F32R, A_OFF + 32768)
    m_buf = at("m_buf", [P, TT, D], F32, A_OFF)
    g_buf = at("g_buf", [P, FT, T], F32, B_OFF)
    y_buf = at("y_buf", [P, KT, T], F32, B_OFF)
    cst = at("cst", [P, 8], F32, C_OFF + 832)
    convc = at("convc", [P, 2, 4, 2 * FT], F32, C_OFF + 1024)
    x_mid = [nc.dram_tensor(f"x_mid{n}", [T, D], F32, kind="Internal").ap() for n in range(3)]
    negc_dram = nc.dram_tensor("negc_dram", [N_FOX, T], F32, kind="Internal").ap()
    psum = top.enter_context(nc.psum_tensor("psum", [P, 8, HALF], F32))

    used_ids = []

    def sems(ctx, stage, names):
        got = [ctx.enter_context(nc.semaphore(f"{stage}_{n}")) for n in names.split()]
        used_ids.extend(s.num for s in got)
        return got

    def clear_semaphores():
        ids = sorted(used_ids)
        used_ids.clear()
        with nc.Block() as block:
            @block.gpsimd
            def _(pool):
                first = ids[0]
                for n, num in enumerate(ids):
                    if n + 1 == len(ids) or ids[n + 1] != num + 1:
                        pool.sem_clear(range(first, num + 1))
                        first = ids[n + 1] if n + 1 < len(ids) else 0

    def setup():
        rows = at("vec_rows", [V_ROWS, P], F32, B_OFF)
        crow = at("conv_rows", [2 * FT, 8, P], F32, B_OFF + 1024)
        with ExitStack() as ctx:
            loaded, turned, copied = sems(ctx, "set", "loaded turned copied")
            block = ctx.enter_context(nc.Block())

            @block.sync
            def _(sp):
                sp.dma_start(ident[:, :], consts[:, K_ID:K_ID + P]).then_inc(loaded, 16)
                sp.dma_start(rows[:, :], vecs).then_inc(loaded, 16)
                sp.dma_start(crow[:, :, :], conv.rearrange("l j (t p) -> t (l j) p", p=P)).then_inc(loaded, 16)

            @block.tensor
            def _(pe):
                pe.wait_ge(loaded, 48)
                for n in range(8):
                    pe.transpose(psum[:, 0, n * 2 * FT:(n + 1) * 2 * FT], crow[:, n, :],
                                 ident[0:2 * FT, 0:2 * FT])
                pe.transpose(psum[:, 1, 0:V_ROWS], rows[:, :],
                             ident[0:V_ROWS, 0:V_ROWS]).then_inc(turned, 1)

            @block.vector
            def _(dve):
                for n, value in enumerate((RMS_EPS, GN_EPS, 1.0)):
                    dve.memset(cst[:, n:n + 1], value).then_inc(copied, 1)
                dve.wait_ge(turned, 1)
                dve.tensor_copy(convc[:, :, :, :].rearrange("p l j t -> p (l j t)"),
                                psum[:, 0, 0:16 * FT]).then_inc(copied, 1)
                dve.tensor_copy(vec[:, :], psum[:, 1, 0:V_ROWS]).then_inc(copied, 1)

    def norm(tag, x_in, post_row, x_out, pre_col):
        last = pre_col is None
        m = m_buf
        xt = at(f"{tag}_x", [P, TT, D], F32, B_OFF)
        hn = at(f"{tag}_hn", [P, TT, D], F32, B_OFF + 32768)
        gp = at(f"{tag}_gp", [P, D], F32, T_OFF)
        junk = at(f"{tag}_junk", [P, 2, D], F32, T_OFF + 4096)
        st = at(f"{tag}_st", [P, 4, TT], F32, T_OFF + 12288)
        hi, lo = h_hi, h_lo
        with ExitStack() as ctx:
            (gain, m_sq, m_rms, m_rs, x_new, x_sq, x_rms, x_rs, scaled, turned, hi_done, lo_done, stored, tiny) = sems(
                ctx, tag, "gain m_sq m_rms m_rs x_new x_sq x_rms x_rs scaled turned hi_done lo_done stored tiny")
            x_in_sem = sems(ctx, tag, " ".join(f"xin{i}" for i in range(TT)))
            block = ctx.enter_context(nc.Block())

            @block.sync
            def _(sp):
                if post_row is not None:
                    sp.dma_start(gp[:, :], g_post[post_row:post_row + 1, :].broadcast_to([P, D])
                                 ).then_inc(gain, 16)
                for i in range(TT):
                    sp.dma_start(xt[:, i, :], x_in[i * P:(i + 1) * P, :]).then_inc(x_in_sem[i], 16)
                if post_row is not None:
                    for i in range(TT):
                        sp.wait_ge(x_new, i + 1)
                        sp.dma_start(x_out[i * P:(i + 1) * P, :], xt[:, i, :]).then_inc(stored, 16)
                    sp.wait_ge(stored, 16 * TT)

            @block.scalar
            def _(act):
                if post_row is not None:
                    for i in range(TT):
                        act.activation(junk[:, 0, :], m[:, i, :], ACT.Square,
                                       accum_out=st[:, 0, i:i + 1]).then_inc(m_sq, 1)
                        act.wait_ge(m_sq, i + 1)
                        act.activation(st[:, 1, i:i + 1], st[:, 0, i:i + 1], ACT.Sqrt, scale=1.0 / D,
                                       bias=cst[:, 0:1]).then_inc(m_rms, 1)
                for i in range(TT if not last else 0):
                    if post_row is not None:
                        act.wait_ge(x_new, i + 1)
                    else:
                        act.wait_ge(x_in_sem[i], 16)
                    act.activation(junk[:, 0, :], xt[:, i, :], ACT.Square,
                                   accum_out=st[:, 2, i:i + 1]).then_inc(x_sq, 1)
                    act.wait_ge(x_sq, i + 1)
                    act.activation(st[:, 3, i:i + 1], st[:, 2, i:i + 1], ACT.Sqrt, scale=1.0 / D,
                                   bias=cst[:, 0:1]).then_inc(x_rms, 1)
                    act.wait_ge(x_rs, i + 1)
                    act.activation(hn[:, i, :], xt[:, i, :], ACT.Copy, scale=st[:, 3, i:i + 1]).then_inc(scaled, 1)
                if last:
                    return
                for n in range(2 * KT):
                    k, h = n % KT, n // KT
                    act.wait_ge(turned, n + 1)
                    act.activation(hi[:, k, h * HALF:(h + 1) * HALF], psum[:, n % 8, :], ACT.Copy,
                                   scale=vec[:, pre_col + k:pre_col + k + 1]).then_inc(hi_done, 1)

            @block.vector
            def _(dve):
                n_tiny = 0
                if post_row is not None:
                    dve.wait_ge(gain, 16)
                for i in range(TT):
                    if post_row is not None:
                        dve.wait_ge(m_rms, i + 1)
                        dve.reciprocal(st[:, 1, i:i + 1], st[:, 1, i:i + 1]).then_inc(m_rs, 1)
                        dve.wait_ge(m_rs, i + 1)
                        dve.scalar_tensor_tensor(junk[:, 1, :], m[:, i, :], st[:, 1, i:i + 1], gp[:, :],
                                                 ALU.mult, ALU.mult).then_inc(tiny, 1)
                        n_tiny += 1
                        dve.wait_ge(tiny, n_tiny)
                        dve.wait_ge(x_in_sem[i], 16)
                        dve.tensor_tensor(xt[:, i, :], xt[:, i, :], junk[:, 1, :], ALU.add).then_inc(x_new, 1)
                        if not last and i == 0:
                            continue
                    if last:
                        continue
                    for b in ([i] if post_row is None else [i - 1] + ([i] if i == TT - 1 else [])):
                        dve.wait_ge(x_rms, b + 1)
                        dve.reciprocal(st[:, 3, b:b + 1], st[:, 3, b:b + 1]).then_inc(x_rs, 1)
                if last:
                    return
                for n in range(2 * KT):
                    k, h = n % KT, n // KT
                    dve.wait_ge(hi_done, n + 1)
                    dve.scalar_tensor_tensor(lo[:, k, h * HALF:(h + 1) * HALF], psum[:, n % 8, :],
                                             vec[:, pre_col + k:pre_col + k + 1],
                                             hi[:, k, h * HALF:(h + 1) * HALF],
                                             ALU.mult, ALU.subtract).then_inc(lo_done, 1)

            if not last:
                @block.tensor
                def _(pe):
                    pe.wait_ge(scaled, TT)
                    for n in range(2 * KT):
                        k, h = n % KT, n // KT
                        if n >= 8:
                            pe.wait_ge(lo_done, n - 7)
                        for i in range(4):
                            t = pe.transpose(psum[:, n % 8, i * P:(i + 1) * P],
                                             hn[:, 4 * h + i, k * P:(k + 1) * P], ident[:, :])
                        t.then_inc(turned, 1)

    def split_weights(pool, raw, whi, wlo, zero, hi_sem, hi_count, done):
        n = raw.shape[-1]
        pool.tensor_tensor(whi, raw, zero[:, 0:1].broadcast_to([P, raw.shape[1], n]) if len(raw.shape) == 3
                           else zero[:, 0:1].broadcast_to([P, n]), ALU.add).then_inc(hi_sem, 1)
        pool.wait_ge(hi_sem, hi_count)
        pool.tensor_tensor(wlo, raw, whi, ALU.subtract).then_inc(done, 1)

    def project_half(pe, bank, whi, wlo, hhi, hlo, half, ks=range(KT)):
        cols = slice(half * HALF, (half + 1) * HALF)
        for k in ks:
            pe.matmul(bank, whi[:, k, :], hhi[:, k, cols], start=(k == 0), stop=False)
            pe.matmul(bank, whi[:, k, :], hlo[:, k, cols], start=False, stop=False)
            mm = pe.matmul(bank, wlo[:, k, :], hhi[:, k, cols], start=False, stop=(k == KT - 1))
        return mm

    def ffn_up(tag, layer):
        hi, lo = h_hi, h_lo
        g = g_buf
        raw = [at(f"{tag}_raw{j}", [P, KT, P], F32, W_OFF + 4096 * j) for j in range(2)]
        whi = [at(f"{tag}_whi{j}", [P, KT, P], F32R, W_OFF + 8192 + 4096 * j) for j in range(2)]
        wlo = [at(f"{tag}_wlo{j}", [P, KT, P], F32R, W_OFF + 16384 + 4096 * j) for j in range(2)]
        zero = at(f"{tag}_zero", [P, 8], F32, W_OFF + 24576)
        u = [at(f"{tag}_u{j}", [P, T + 2], F32, T_OFF + 4128 * j) for j in range(2)]
        acc = [at(f"{tag}_acc{j}", [P, T], F32, T_OFF + 8256 + 4096 * j) for j in range(2)]
        act_g = at(f"{tag}_actg", [P, T], F32, T_OFF + 16448)
        w = w_up[layer].rearrange("(k p) n -> p k n", p=P)
        with ExitStack() as ctx:
            zeroed, pads, split_hi, gelu_done, gated = sems(ctx, tag, "zeroed pads split_hi gelu gated")
            raw_in = sems(ctx, tag, "raw0 raw1")
            w_full = sems(ctx, tag, "wfull0 wfull1")
            ps_full = sems(ctx, tag, "psfull0 psfull1")
            evac = sems(ctx, tag, "evac0 evac1")
            conv1 = sems(ctx, tag, "conv1_0 conv1_1")
            conv2 = sems(ctx, tag, "conv2_0 conv2_1")
            block = ctx.enter_context(nc.Block())

            @block.sync
            def _(sp):
                with sp.Fori(0, FT) as c:
                    for j in range(2):
                        sp.wait_ge(w_full[j], c)
                        sp.dma_start(raw[j][:, :, :], w[:, :, ds(c * P + j * D_FF, P)]).then_inc(raw_in[j], 16)

            @block.gpsimd
            def _(pool):
                pool.memset(zero[:, :], 0.0).then_inc(zeroed, 1)
                pool.wait_ge(zeroed, 1)
                with pool.Fori(0, FT) as c:
                    for j in range(2):
                        pool.wait_ge(ps_full[j], c * 2)
                        pool.wait_ge(raw_in[j], c * 16 + 16)
                        split_weights(pool, raw[j][:, :, :], whi[j][:, :, :], wlo[j][:, :, :], zero,
                                      split_hi, c * 2 + j + 1, w_full[j])

            @block.tensor
            def _(pe):
                with pe.Fori(0, FT) as c:
                    for j in range(2):
                        for h in range(2):
                            pe.wait_ge(evac[j], c * 2)
                            pe.wait_ge(w_full[j], c + 1)
                            project_half(pe, psum[:, 2 * j + h, :], whi[j], wlo[j], hi, lo, h
                                         ).then_inc(ps_full[j], 1)

            @block.scalar
            def _(act):
                cc = convc[:, layer, :, :]
                with act.Fori(0, FT) as c:
                    def take(j):
                        act.wait_ge(conv2[j], c)
                        act.wait_ge(gated if j else gelu_done, c)
                        for h in range(2):
                            bank = psum[:, 2 * j + h, :]
                            act.wait_ge(ps_full[j], c * 2 + h + 1)
                            act.activation(u[j][:, 2 + h * HALF:2 + (h + 1) * HALF], bank, ACT.Copy)
                            act.activation(acc[j][:, h * HALF:(h + 1) * HALF], bank, ACT.Identity,
                                           scale=cc[:, 2, ds(c + j * FT, 1)],
                                           bias=cc[:, 3, ds(c + j * FT, 1)]).then_inc(evac[j], 1)
                    take(0)
                    act.wait_ge(conv2[0], c + 1)
                    act.wait_ge(gated, c)
                    act.activation(act_g[:, :], acc[0][:, :], ACT.Gelu_apprx_tanh).then_inc(gelu_done, 1)
                    take(1)

            @block.vector
            def _(dve):
                cc = convc[:, layer, :, :]
                for j in range(2):
                    dve.memset(u[j][:, 0:2], 0.0).then_inc(pads, 1)
                dve.wait_ge(pads, 2)
                with dve.Fori(0, FT) as c:
                    for j in range(2):
                        dve.wait_ge(evac[j], c * 2 + 2)
                        if j == 0:
                            dve.wait_ge(gelu_done, c)
                        dve.scalar_tensor_tensor(acc[j][:, :], u[j][:, 1:T + 1], cc[:, 1, ds(c + j * FT, 1)],
                                                 acc[j][:, :], ALU.mult, ALU.add).then_inc(conv1[j], 1)
                        dve.wait_ge(conv1[j], c + 1)
                        dve.scalar_tensor_tensor(acc[j][:, :], u[j][:, 0:T], cc[:, 0, ds(c + j * FT, 1)],
                                                 acc[j][:, :], ALU.mult, ALU.add).then_inc(conv2[j], 1)
                    dve.wait_ge(gelu_done, c + 1)
                    dve.wait_ge(conv2[1], c + 1)
                    dve.tensor_tensor(g[:, c, :], act_g[:, :], acc[1][:, :], ALU.mult).then_inc(gated, 1)

    def down(tag, w, src, n_tiles):
        m = m_buf
        raw = [at(f"{tag}_raw{j}", [P, HALF], F32, W_OFF + 2048 * j) for j in range(2)]
        whi = [at(f"{tag}_whi{j}", [P, HALF], F32R, W_OFF + 4096 + 2048 * j) for j in range(2)]
        wlo = [at(f"{tag}_wlo{j}", [P, HALF], F32R, W_OFF + 8192 + 2048 * j) for j in range(2)]
        zero = at(f"{tag}_zero", [P, 8], F32, W_OFF + 24576)
        shi = [at(f"{tag}_shi{j}", [P, T], F32R, T_OFF + 4096 * j) for j in range(2)]
        slo = [at(f"{tag}_slo{j}", [P, T], F32R, T_OFF + 8192 + 4096 * j) for j in range(2)]
        pairs = n_tiles // 2
        with ExitStack() as ctx:
            zeroed, split_hi = sems(ctx, tag, "zeroed split_hi")
            raw_in = sems(ctx, tag, "raw0 raw1")
            w_full = sems(ctx, tag, "wfull0 wfull1")
            s_hi = sems(ctx, tag, "shi0 shi1")
            s_lo = sems(ctx, tag, "slo0 slo1")
            used = sems(ctx, tag, "used0 used1")
            bank_full = sems(ctx, tag, " ".join(f"bank{b}" for b in range(8)))
            bank_read = sems(ctx, tag, " ".join(f"read{b}" for b in range(8)))
            block = ctx.enter_context(nc.Block())

            @block.sync
            def _(sp):
                for nh in range(2):
                    with sp.Fori(nh * pairs, (nh + 1) * pairs) as c:
                        for j in range(2):
                            sp.wait_ge(w_full[j], c)
                            sp.dma_start(raw[j][:, :], w[ds(c * (2 * P) + (j - nh * n_tiles) * P, P),
                                                         nh * HALF:(nh + 1) * HALF]).then_inc(raw_in[j], 16)

            @block.gpsimd
            def _(pool):
                pool.memset(zero[:, :], 0.0).then_inc(zeroed, 1)
                pool.wait_ge(zeroed, 1)
                with pool.Fori(0, 2 * pairs) as c:
                    for j in range(2):
                        pool.wait_ge(used[j], c)
                        pool.wait_ge(raw_in[j], c * 16 + 16)
                        split_weights(pool, raw[j][:, :], whi[j][:, :], wlo[j][:, :], zero,
                                      split_hi, c * 2 + j + 1, w_full[j])

            @block.scalar
            def _(act):
                for nh in range(2):
                    with act.Fori(0, pairs) as c:
                        for j in range(2):
                            act.wait_ge(used[j], c + nh * pairs)
                            act.activation(shi[j][:, :], src[:, c * 2 + j, :], ACT.Copy).then_inc(s_hi[j], 1)
                    for b in range(0, 8, 2):
                        act.wait_ge(bank_full[b], nh + 1)
                        act.activation(m[:, b, nh * HALF:(nh + 1) * HALF], psum[:, b, :],
                                       ACT.Copy).then_inc(bank_read[b], 1)

            @block.vector
            def _(dve):
                for nh in range(2):
                    with dve.Fori(0, pairs) as c:
                        for j in range(2):
                            dve.wait_ge(s_hi[j], c + nh * pairs + 1)
                            dve.tensor_tensor(slo[j][:, :], src[:, c * 2 + j, :], shi[j][:, :],
                                              ALU.subtract).then_inc(s_lo[j], 1)
                    for b in range(1, 8, 2):
                        if b < 7:
                            dve.wait_ge(bank_full[b], nh + 1)
                        else:
                            dve.wait_ge(used[1], (nh + 1) * pairs)
                        dve.tensor_copy(m[:, b, nh * HALF:(nh + 1) * HALF], psum[:, b, :]).then_inc(bank_read[b], 1)

            @block.tensor
            def _(pe):
                def pair(nh, c, first=False, last=False):
                    for j in range(2):
                        pe.wait_ge(w_full[j], c + nh * pairs + 1)
                        pe.wait_ge(s_lo[j], c + nh * pairs + 1)
                        for b in range(8):
                            lhi, llo = shi[j][:, b * P:(b + 1) * P], slo[j][:, b * P:(b + 1) * P]
                            if first and j == 0 and nh:
                                pe.wait_ge(bank_read[b], nh)
                            pe.matmul(psum[:, b, :], lhi, whi[j][:, :], start=(first and j == 0), stop=False,
                                      skip_group_check=True)
                            pe.matmul(psum[:, b, :], lhi, wlo[j][:, :], start=False, stop=False,
                                      skip_group_check=True)
                            mm = pe.matmul(psum[:, b, :], llo, whi[j][:, :], start=False,
                                           stop=(last and j == 1), skip_group_check=True)
                            if last and j == 1 and b < 7:
                                mm.then_inc(bank_full[b], 1)
                        mm.then_inc(used[j], 1)
                for nh in range(2):
                    pair(nh, 0, first=True)
                    with pe.Fori(1, pairs - 1) as c:
                        pair(nh, c)
                    pair(nh, pairs - 1, last=True)

    def fox_gates(tag):
        col = 3 * FOX_W
        raw = at(f"{tag}_raw", [P, KT, P], F32, W_OFF)
        whi = at(f"{tag}_whi", [P, KT, P], F32R, W_OFF + 4096)
        wlo = at(f"{tag}_wlo", [P, KT, P], F32R, W_OFF + 8192)
        zero = at(f"{tag}_zero", [P, 8], F32, W_OFF + 12288)
        bias = at(f"{tag}_bias", [N_FOX, 8], F32, W_OFF + 12320)
        size, low, nl, cum, ones = (at(f"{tag}_{n}", [N_FOX, T], F32, B_OFF + 4096 * i)
                                    for i, n in enumerate("size low nl cum ones".split()))
        with ExitStack() as ctx:
            loaded, zeroed, split_hi, w_full, proj, act_done, dve_done, bias_in, stored = sems(
                ctx, tag, "loaded zeroed split_hi w_full proj act_done dve_done bias_in stored")
            block = ctx.enter_context(nc.Block())

            @block.sync
            def _(sp):
                sp.dma_start(raw[:, :, :], w_in0.rearrange("(k p) n -> p k n", p=P)[:, :, col:col + P]
                             ).then_inc(loaded, 16)
                sp.dma_start(bias[:, 0:1], forget_bias).then_inc(bias_in, 16)
                sp.wait_ge(dve_done, 4)
                sp.dma_start(negc_dram, cum[:, :]).then_inc(stored, 16)
                sp.wait_ge(stored, 16)

            @block.gpsimd
            def _(pool):
                pool.memset(zero[:, :], 0.0).then_inc(zeroed, 1)
                pool.wait_ge(zeroed, 1)
                pool.wait_ge(loaded, 16)
                split_weights(pool, raw[:, :, :], whi[:, :, :], wlo[:, :, :], zero, split_hi, 1, w_full)

            @block.tensor
            def _(pe):
                pe.wait_ge(w_full, 1)
                for h in range(2):
                    project_half(pe, psum[:, h, :], whi, wlo, h_hi, h_lo, h).then_inc(proj, 1)

            @block.scalar
            def _(act):
                act.wait_ge(proj, 2)
                act.wait_ge(bias_in, 16)
                z = psum[0:N_FOX, 0:2, :].rearrange("p b n -> p (b n)")
                act.activation(size[:, :], z, ACT.Abs, bias=bias[:, 0:1]).then_inc(act_done, 1)
                act.wait_ge(act_done, 1)
                act.activation(size[:, :], size[:, :], ACT.Exp, scale=-1.0).then_inc(act_done, 1)
                act.wait_ge(act_done, 2)
                act.activation(size[:, :], size[:, :], ACT.Ln, bias=cst[0:N_FOX, 2:3]).then_inc(act_done, 1)

            @block.vector
            def _(dve):
                dve.memset(ones[:, :], 1.0).then_inc(dve_done, 1)
                dve.wait_ge(act_done, 1)
                dve.wait_ge(bias_in, 16)
                z = psum[0:N_FOX, 0:2, :].rearrange("p b n -> p (b n)")
                dve.tensor_scalar(low[:, :], z, bias[:, 0:1], 0.0, ALU.add, ALU.min).then_inc(dve_done, 1)
                dve.wait_ge(act_done, 3)
                dve.wait_ge(dve_done, 2)
                dve.tensor_tensor(nl[:, :], size[:, :], low[:, :], ALU.subtract).then_inc(dve_done, 1)
                dve.wait_ge(dve_done, 3)
                dve.tensor_tensor_scan(cum[:, :], ones[:, :], nl[:, :], 0.0, ALU.mult, ALU.add
                                       ).then_inc(dve_done, 1)

    cos_t = at("cos_t", [P, T], F32, T_OFF + 8192)
    sin_t = at("sin_t", [P, T], F32, T_OFF + 12288)

    def rotary_tables(tag):
        two_pi = (6.28125, 0.00193500518798828125, 3.0199159819567e-7)
        rounder = 1.5 * 2.0 ** 23
        pos_i = at(f"{tag}_posi", [P, T], I32, B_OFF)
        ang, turns, red, half = (at(f"{tag}_{n}", [P, T], F32, B_OFF + 4096 * (i + 1))
                                 for i, n in enumerate("ang turns red half".split()))
        freq = at(f"{tag}_freq", [P, 2], F32, B_OFF + 20480)
        with ExitStack() as ctx:
            loaded, step, sines = sems(ctx, tag, "loaded step sines")
            block = ctx.enter_context(nc.Block())

            @block.sync
            def _(sp):
                sp.dma_start(pos_i[:, :], positions.broadcast_to([P, T])).then_inc(loaded, 16)
                sp.dma_start(freq[:, :], consts[:, K_FREQ:K_FREQ + 2]).then_inc(loaded, 16)

            @block.vector
            def _(dve):
                n = [0]

                def then(ins):
                    n[0] += 1
                    ins.then_inc(step, 1)
                    dve.wait_ge(step, n[0])
                dve.wait_ge(loaded, 32)
                then(dve.tensor_copy(ang[:, :], pos_i[:, :]))
                then(dve.tensor_scalar(ang[:, :], ang[:, :], freq[:, 0:1], None, ALU.mult))
                then(dve.tensor_scalar(turns[:, :], ang[:, :], 1.0 / (2 * np.pi), rounder, ALU.mult, ALU.add))
                then(dve.tensor_scalar(turns[:, :], turns[:, :], -rounder, None, ALU.add))
                then(dve.scalar_tensor_tensor(red[:, :], turns[:, :], -two_pi[0], ang[:, :], ALU.mult, ALU.add))
                then(dve.scalar_tensor_tensor(red[:, :], turns[:, :], -two_pi[1], red[:, :], ALU.mult, ALU.add))
                then(dve.scalar_tensor_tensor(red[:, :], turns[:, :], -two_pi[2], red[:, :], ALU.mult, ALU.add))
                then(dve.tensor_scalar(red[:, :], red[:, :], 3.141592, -3.141592, ALU.min, ALU.max))
                dve.wait_ge(sines, 2)
                then(dve.tensor_scalar(sin_t[:, :], sin_t[:, :], freq[:, 1:2], None, ALU.mult))
                then(dve.tensor_tensor(half[:, :], half[:, :], half[:, :], ALU.mult))
                then(dve.tensor_scalar(cos_t[:, :], half[:, :], -2.0, 1.0, ALU.mult, ALU.add))

            @block.scalar
            def _(act):
                act.wait_ge(step, 8)
                act.activation(sin_t[:, :], red[:, :], ACT.Sin).then_inc(sines, 1)
                act.activation(half[:, :], red[:, :], ACT.Sin, scale=0.5).then_inc(sines, 1)

    def attention(tag, w_in, width, n_pairs, fox):
        def b(n, name, shape=(P, T)):
            return at(f"{tag}_{name}", list(shape), F32, B_OFF + 32768 + 4096 * n)
        q = [b(0, "q0"), b(1, "q1")]
        k = [b(2, "k0"), b(3, "k1")]
        v = [b(4, "v0", (P, TT, P)), b(5, "v1", (P, TT, P))]
        stage = b(6, "stage")
        logit = [b(7, "logit0"), b(8, "logit1")]
        prob = [b(9, "prob0"), b(10, "prob1")]
        extra = b(11, "extra", (P, 2, T))
        o_sb = b(13, "o", (P, TT, P))
        probt = [at(f"{tag}_probt{n}", [P, T], F32, T_OFF + 4096 * n) for n in range(2)]
        swap = at(f"{tag}_swap", [P, T], F32, T_OFF + 16384)
        raw = at(f"{tag}_raw", [P, KT, P], F32, W_OFF)
        whi = [at(f"{tag}_whi{j}", [P, KT, P], F32R, W_OFF + 4096 + 4096 * j) for j in range(3)]
        wlo = [at(f"{tag}_wlo{j}", [P, KT, P], F32R, W_OFF + 16384 + 4096 * j) for j in range(3)]
        zero = at(f"{tag}_zero", [P, 8], F32, C_OFF + 2560)
        mask_b = at(f"{tag}_maskb", [P, P], BF16, C_OFF + 2688)
        ident_b = at(f"{tag}_identb", [P, P], BF16, C_OFF + 2944)
        mask_f = at(f"{tag}_maskf", [P, P], F32, C_OFF + 3520)
        small = at(f"{tag}_small", [P, 3, 16], F32, C_OFF + 3200)
        carrier = at(f"{tag}_carrier", [P, 16], F32, C_OFF + 3424)
        shift, den, rden = small[:, 0, :], small[:, 1, :], small[:, 2, :]
        wv = w_in.rearrange("(k p) n -> p k n", p=P)
        units = 2 * TT
        PROJ, OUT = 6, 7
        share = (3, 3, 2, 4, 4, 3, 3, 2, 4, 4, 3, 3, 2, 3, 3, 2)
        done_by = [sum(share[:u]) for u in range(units + 1)]
        ends = {u: done_by[u + 1] // KT - 1 for u in range(units) if done_by[u + 1] % KT == 0}
        rotations = {6: ("a", 0), 8: ("b", 0), 11: ("a", 1), 12: ("b", 1)}
        assert done_by[units] == 6 * KT
        q_scale = ATT_SCALE if fox else 1.0
        with ExitStack() as ctx:
            (zeroed, raw_in, split_hi, w_full, proj, proj_read, v_turn, v_new,
             s_full, biased, probs, counted, turned, turned_read, o_full, o_ready, o_turn, y_ready,
             recips, mask_in, mask_ready, swapped, rot1, rot2, rot3, rot_zero) = sems(
                ctx, tag, "zeroed raw_in split_hi w_full proj proj_read v_turn v_new "
                "s_full biased probs counted turned turned_read o_full o_ready o_turn "
                "y_ready recips mask_in mask_ready swapped rot1 rot2 rot3 rot_zero")
            gate_in = sems(ctx, tag, "gate0 gate1")
            block = ctx.enter_context(nc.Block())

            def for_pairs(engine, pair_step):
                with engine.Fori(0, n_pairs // 2 - 1) as c:
                    pair_step(c * 2, 0, c * 2 + 1)
                    pair_step(c * 2 + 1, 1, c * 2 + 2)
                pair_step(n_pairs - 2, 0, n_pairs - 1)
                pair_step(n_pairs - 1, 1, None)

            def first(pair, u=0):
                return isinstance(pair, int) and pair == 0 and u == 0

            @block.sync
            def _(sp):
                def weights(pair):
                    for t in range(3):
                        col = sp.snap(pair * P + t * width)
                        sp.compute_val(col * 4)
                        sp.wait_ge(w_full, pair * 3 + t)
                        sp.dma_start(raw[:, :, :], wv[:, :, ds(col, P)]).then_inc(raw_in, 16)

                def gates(pair, e):
                    row = sp.snap(pair * 2 + e)
                    if not first(pair):
                        sp.wait_ge(biased, pair * units + (8 * e - 8))
                    sp.dma_start(extra[:, e, :], negc_dram[ds(row, 1), :].broadcast_to([P, T])
                                 ).then_inc(gate_in[e], 16)

                weights(0)
                if fox:
                    gates(0, 0)
                    gates(0, 1)
                    sp.dma_start(mask_f[:, :], consts[:, K_CAUS:K_CAUS + P]).then_inc(mask_in, 16)
                else:
                    sp.dma_start(extra[:, :, :], dil).then_inc(mask_in, 16)
                weights(1)
                with sp.Fori(1, n_pairs - 1) as pair:
                    if fox:
                        gates(pair, 0)
                    weights(pair + 1)
                    if fox:
                        gates(pair, 1)
                if fox:
                    for e in range(2):
                        gates(n_pairs - 1, e)

            @block.gpsimd
            def _(pool):
                def split(pair, t):
                    pool.wait_ge(raw_in, (pair * 3 + t + 1) * 16)
                    split_weights(pool, raw[:, :, :], whi[t][:, :, :], wlo[t][:, :, :], zero,
                                  split_hi, pair * 3 + t + 1, w_full)
                pool.memset(zero[:, :], 0.0).then_inc(zeroed, 1)
                pool.wait_ge(zeroed, 1)
                for t in range(3):
                    split(0, t)
                with pool.Fori(1, n_pairs) as pair:
                    for t in range(3):
                        pool.wait_ge(proj, pair * 6 + (2 * t - 4))
                        split(pair, t)

            @block.tensor
            def _(pe):
                def fill(pair, lo, hi):
                    for step in range(lo, hi):
                        f, ch = step // KT, step % KT
                        t, h = f // 2, f % 2
                        if ch == 0:
                            if not h:
                                pe.wait_ge(w_full, pair * 3 + t + 1)
                            if not first(pair, f):
                                pe.wait_ge(proj_read, pair * 6 + f)
                            if f == 0 and not first(pair):
                                pe.wait_ge(y_ready, pair - 1)
                        mm = project_half(pe, psum[:, PROJ, :], whi[t], wlo[t], h_hi, h_lo, h, [ch])
                        if ch == KT - 1:
                            mm.then_inc(proj, 1)

                def turn_v(pair, before):
                    pe.wait_ge(proj_read, pair * 6 + 6)
                    if before is not None:
                        pe.wait_ge(turned_read, before * units + units)
                    for n in range(TT):
                        tr = pe.transpose(psum[:, 4 + n // 4, (n % 4) * P:(n % 4 + 1) * P],
                                          stage[:, n * P:(n + 1) * P], ident[:, :])
                    tr.then_inc(v_turn, 1)

                def scores(pair, par, u):
                    e, qt = u // TT, u % TT
                    if u == 0:
                        if fox:
                            pe.wait_ge(proj_read, pair * 6 + 4)
                        else:
                            pe.wait_ge(rot3, pair * 2 + 2)
                    if u >= 2 or not first(pair):
                        pe.wait_ge(biased, pair * units + (u - 1))
                    nk = (qt + 1) * P
                    rows = slice(e * HD, (e + 1) * HD)
                    for c in range(0, nk, HALF):
                        n = min(HALF, nk - c)
                        diag = fox and c + n == nk
                        mm = pe.matmul(psum[:, 2 * (u % 2) + c // HALF, 0:n], q[par][rows, qt * P:(qt + 1) * P],
                                       k[par][rows, c:c + n], start=True, stop=not diag)
                    if fox:
                        mm = pe.matmul(psum[:, 2 * (u % 2) + c // HALF, n - P:n], ident_b[:, :], mask_b[:, :],
                                       start=False, stop=True)
                    mm.then_inc(s_full, 1)

                def turn(pair, u):
                    pe.wait_ge(probs if fox else counted, pair * units + (u + 1))
                    pe.wait_ge(turned_read, pair * units + u)
                    if u == 0:
                        pe.wait_ge(v_new, pair + 1)
                    for n in range(u % TT + 1):
                        tr = pe.transpose(psum[:, 4 + n // 4, (n % 4) * P:(n % 4 + 1) * P],
                                          prob[u % 2][:, n * P:(n + 1) * P], ident[:, :])
                    tr.then_inc(turned, 1)

                def weigh(pair, par, u):
                    e, qt = u // TT, u % TT
                    pe.wait_ge(turned_read, pair * units + (u + 1))
                    pe.wait_ge(o_ready, pair * units + u)
                    if u == 0:
                        pe.wait_ge(y_ready, pair)
                    for n in range(qt + 1):
                        mm = pe.matmul(psum[:, OUT, 0:HD], probt[u % 2][:, n * P:(n + 1) * P],
                                       v[par][:, n, e * HD:(e + 1) * HD], start=(n == 0), stop=(n == qt))
                    mm.then_inc(o_full, 1)

                def pair_step(pair, par, following):
                    for u in range(units):
                        if u + 2 < units:
                            scores(pair, par, u + 2)
                        elif following is not None:
                            scores(following, 1 - par, u + 2 - units)
                        middle = done_by[u] + (share[u] + 1) // 2
                        if following is not None and u < units - 1:
                            fill(following, done_by[u], middle)
                        turn(pair, u)
                        if following is not None:
                            fill(following, middle if u < units - 1 else done_by[u], done_by[u + 1])
                        if u:
                            weigh(pair, par, u - 1)
                    weigh(pair, par, units - 1)
                    if following is not None:
                        turn_v(following, pair)
                    pe.wait_ge(o_ready, pair * units + units)
                    if following is not None:
                        pe.wait_ge(proj_read, following * 6 + 6)
                    for n in range(TT):
                        tr = pe.transpose(psum[:, PROJ + n // 4, (n % 4) * P:(n % 4 + 1) * P],
                                          o_sb[:, n, :], ident[:, :])
                    tr.then_inc(o_turn, 1)

                fill(0, 0, 4 * KT)
                if fox:
                    pe.wait_ge(mask_ready, 2)
                scores(0, 0, 0)
                scores(0, 0, 1)
                fill(0, 4 * KT, 6 * KT)
                turn_v(0, None)
                for_pairs(pe, pair_step)

            @block.scalar
            def _(act):
                def take(pair, par, f):
                    t, h = f // 2, f % 2
                    cols = slice(h * HALF, (h + 1) * HALF)
                    act.wait_ge(proj, pair * 6 + (f + 1))
                    dst = stage
                    if fox and t < 2:
                        dst = (q, k)[t][par]
                        if f == 0 and not first(pair):
                            act.wait_ge(s_full, (pair - 1) * units)
                    elif h == 0 and (fox or t == 0):
                        act.wait_ge(v_turn, pair)
                    elif h == 0:
                        act.wait_ge(rot1, pair * 2 + t)
                        act.wait_ge(swapped, pair * 128 + 64 * t)
                    act.activation(dst[:, cols], psum[:, PROJ, :], ACT.Copy,
                                   scale=(q_scale if t == 0 else 1.0)).then_inc(proj_read, 1)
                    if not fox and t < 2 and h:
                        act.wait_ge(proj_read, pair * 6 + (f + 1))
                        act.wait_ge(rot3, pair * 2 + t)
                        for to, of in ((0, 8), (8, 0), (64, 72), (72, 64)):
                            act.dma_start(swap[to:to + 8, :], stage[of:of + 8, :]).then_inc(swapped, 16)

                def take_v(pair, par):
                    act.wait_ge(v_turn, pair + 1)
                    if not first(pair):
                        act.wait_ge(o_full, (pair - 1) * units)
                    act.activation(v[par][:, :, :].rearrange("p n c -> p (n c)"),
                                   psum[:, 4:6, :].rearrange("p b n -> p (b n)"), ACT.Copy).then_inc(v_new, 1)

                def exp(pair, u):
                    nk = (u % TT + 1) * P
                    act.wait_ge(biased, pair * units + (u + 1))
                    if u >= 2:
                        act.wait_ge(turned, pair * units + (u - 1))
                        act.wait_ge(o_ready, pair * units + (u - 2))
                    elif not first(pair):
                        act.wait_ge(turned, pair * units - 1)
                        act.wait_ge(o_ready, pair * units - 2)
                    act.activation(prob[u % 2][:, 0:nk], logit[u % 2][:, 0:nk], ACT.Exp, scale=-1.0,
                                   bias=shift[:, u:u + 1],
                                   **({"accum_out": den[:, u:u + 1]} if fox else {})).then_inc(probs, 1)

                def pair_step(pair, par, following):
                    for u in range(units):
                        if following is not None and u - 1 in ends:
                            take(following, 1 - par, ends[u - 1])
                        if u == 0:
                            nk = 2 * P
                            act.wait_ge(biased, pair * units + 2)
                            act.wait_ge(turned, pair * units)
                            act.wait_ge(o_ready, pair * units)
                            act.activation(prob[1][:, 0:nk], logit[1][:, 0:nk], ACT.Exp, scale=-1.0,
                                           bias=shift[:, 1:2],
                                           **({"accum_out": den[:, 1:2]} if fox else {})).then_inc(probs, 1)
                        elif u + 1 < units:
                            exp(pair, u + 1)
                        elif following is not None:
                            exp(following, 0)
                        act.wait_ge(turned, pair * units + (u + 1))
                        act.wait_ge(o_full, pair * units + max(u - 1, 0))
                        nk = (u % TT + 1) * P
                        act.activation(probt[u % 2][:, 0:nk],
                                       psum[:, 4:6, :].rearrange("p b n -> p (b n)")[:, 0:nk],
                                       ACT.Copy).then_inc(turned_read, 1)
                    if following is not None:
                        take(following, 1 - par, 5)
                        take_v(following, 1 - par)
                    act.wait_ge(o_turn, pair + 1)
                    act.activation(y_buf[:, pair, :], psum[:, PROJ:PROJ + 2, :].rearrange("p b n -> p (b n)"),
                                   ACT.Copy).then_inc(y_ready, 1)

                if fox:
                    act.wait_ge(mask_in, 16)
                    act.activation(mask_b[:, :], mask_f[:, :], ACT.Copy).then_inc(mask_ready, 1)
                    act.activation(ident_b[:, :], ident[:, :], ACT.Copy).then_inc(mask_ready, 1)
                else:
                    act.wait_ge(rot_zero, 1)
                for f in range(6):
                    take(0, 0, f)
                exp(0, 0)
                take_v(0, 0)
                for_pairs(act, pair_step)

            @block.vector
            def _(dve):
                def rotate_a(pair, par, t):
                    dve.wait_ge(proj_read, pair * 6 + (2 * t + 2))
                    if not first(pair):
                        dve.wait_ge(s_full, (pair - 1) * units)
                    dst = (q, k)[t][par]
                    dve.tensor_tensor(dst[:, :], stage[:, :], cos_t[:, :], ALU.mult).then_inc(rot1, 1)

                def rotate_b(pair, par, t):
                    dst = (q, k)[t][par]
                    dve.wait_ge(swapped, pair * 128 + 64 * (t + 1))
                    dve.tensor_tensor(swap[:, :], swap[:, :], sin_t[:, :], ALU.mult).then_inc(rot2, 1)
                    dve.wait_ge(rot2, pair * 2 + t + 1)
                    dve.wait_ge(rot1, pair * 2 + t + 1)
                    dve.tensor_tensor(dst[:, :], dst[:, :], swap[:, :], ALU.add).then_inc(rot3, 1)

                def bias(pair, u):
                    e, qt = u // TT, u % TT
                    nk = (qt + 1) * P
                    dve.wait_ge(s_full, pair * units + (u + 1))
                    if u >= 1:
                        dve.wait_ge(probs, pair * units + (u - 1))
                    elif not first(pair):
                        dve.wait_ge(probs, pair * units - 1)
                    if fox and qt == 0:
                        dve.wait_ge(gate_in[e], pair * 16 + 16)
                    if u == 0:
                        dve.wait_ge(mask_in, 16)
                    dve.memset(carrier[:, u:u + 1], 0.0)
                    more = extra[:, e, 0:nk] if fox else extra[:, 0, (TT - 1 - qt) * P:T]
                    s = psum[:, 2 * (u % 2):2 * (u % 2) + 2, :].rearrange("p b n -> p (b n)")[:, 0:nk]
                    dve.tensor_tensor_reduce(out=logit[u % 2][:, 0:nk], in0=s, in1=more,
                                             scale=(-1.0 if fox else -ATT_SCALE), scalar=3.0e38,
                                             op0=ALU.add, op1=ALU.min,
                                             accum_out=shift[:, u:u + 1]).then_inc(biased, 1)

                def count(pair, u):
                    qt = u % TT
                    nk = (qt + 1) * P
                    dve.wait_ge(probs, pair * units + (u + 1))
                    dve.tensor_tensor_reduce(out=prob[u % 2][:, 0:nk], in0=prob[u % 2][:, 0:nk],
                                             in1=extra[:, 1, (TT - 1 - qt) * P:T], scale=1.0, scalar=0.0,
                                             op0=ALU.mult, op1=ALU.add,
                                             accum_out=den[:, u:u + 1]).then_inc(counted, 1)

                def norm_out(pair, u):
                    e, qt = u // TT, u % TT
                    dve.wait_ge(probs if fox else counted, pair * units + (u + 1))
                    dve.reciprocal(rden[:, u:u + 1], den[:, u:u + 1]).then_inc(recips, 1)
                    dve.wait_ge(recips, pair * units + (u + 1))
                    if u == 0:
                        dve.wait_ge(o_turn, pair)
                    dve.wait_ge(o_full, pair * units + (u + 1))
                    dve.tensor_scalar(o_sb[:, qt, e * HD:(e + 1) * HD], psum[:, OUT, 0:HD],
                                      rden[:, u:u + 1], None, ALU.mult).then_inc(o_ready, 1)

                def pair_step(pair, par, following):
                    for u in range(units):
                        if not fox:
                            count(pair, u)
                        if u + 1 < units:
                            bias(pair, u + 1)
                        elif following is not None:
                            bias(following, 0)
                        if u:
                            norm_out(pair, u - 1)
                        if not fox and following is not None and u in rotations:
                            part, t = rotations[u]
                            (rotate_a if part == "a" else rotate_b)(following, 1 - par, t)
                    norm_out(pair, units - 1)

                if not fox:
                    dve.wait_ge(mask_in, 16)
                    dve.memset(swap[:, :], 0.0).then_inc(rot_zero, 1)
                    for t in range(2):
                        rotate_a(0, 0, t)
                        rotate_b(0, 0, t)
                bias(0, 0)
                for_pairs(dve, pair_step)
    z_buf = at("z_buf", [P, RWKV_IN // P, T], F32, B_OFF + 32768)
    Z_R, Z_K, Z_V, Z_LO, Z_G = 0, RW_T, 2 * RW_T, 3 * RW_T, 3 * RW_T + 1
    cum_buf = at("cum_buf", [P, RW_T, T], F32, A_OFF)
    nkk_buf = at("nkk_buf", [P, RW_T, T], F32, A_OFF + 16384)
    bb_buf = at("bb_buf", [P, RW_T, T], F32, A_OFF + 32768)

    def rwkv_project(tag):
        n_pairs = RWKV_IN // P // 2
        raw = [at(f"{tag}_raw{j}", [P, KT, P], F32, W_OFF + 4096 * j) for j in range(2)]
        whi = [at(f"{tag}_whi{j}", [P, KT, P], F32R, W_OFF + 8192 + 4096 * j) for j in range(2)]
        wlo = [at(f"{tag}_wlo{j}", [P, KT, P], F32R, W_OFF + 16384 + 4096 * j) for j in range(2)]
        zero = at(f"{tag}_zero", [P, 8], F32, W_OFF + 24576)
        z = [at(f"{tag}_z{j}", [P, T + 1], F32, T_OFF + 4128 * j) for j in range(2)]
        diff = [at(f"{tag}_diff{j}", [P, T], F32, T_OFF + 8256 + 4096 * j) for j in range(2)]
        w = w_in0.rearrange("(k p) n -> p k n", p=P)
        with ExitStack() as ctx:
            zeroed, pads, split_hi = sems(ctx, tag, "zeroed pads split_hi")
            raw_in = sems(ctx, tag, "raw0 raw1")
            w_full = sems(ctx, tag, "wfull0 wfull1")
            ps_full = sems(ctx, tag, "psfull0 psfull1")
            evac = sems(ctx, tag, "evac0 evac1")
            diffed = sems(ctx, tag, "diffed0 diffed1")
            mixed = sems(ctx, tag, "mixed0 mixed1")
            block = ctx.enter_context(nc.Block())

            @block.sync
            def _(sp):
                with sp.Fori(0, n_pairs) as c:
                    for j in range(2):
                        col = sp.snap(c * (2 * P) + (j * P + FOX_IN))
                        sp.compute_val(col * 4)
                        sp.wait_ge(w_full[j], c)
                        sp.dma_start(raw[j][:, :, :], w[:, :, ds(col, P)]).then_inc(raw_in[j], 16)

            @block.gpsimd
            def _(pool):
                pool.memset(zero[:, :], 0.0).then_inc(zeroed, 1)
                pool.wait_ge(zeroed, 1)
                with pool.Fori(0, n_pairs) as c:
                    for j in range(2):
                        pool.wait_ge(ps_full[j], c * 2)
                        pool.wait_ge(raw_in[j], c * 16 + 16)
                        split_weights(pool, raw[j][:, :, :], whi[j][:, :, :], wlo[j][:, :, :], zero,
                                      split_hi, c * 2 + j + 1, w_full[j])

            @block.tensor
            def _(pe):
                with pe.Fori(0, n_pairs) as c:
                    for j in range(2):
                        for h in range(2):
                            pe.wait_ge(evac[j], c * 2)
                            pe.wait_ge(w_full[j], c + 1)
                            project_half(pe, psum[:, 2 * j + h, :], whi[j], wlo[j], h_hi, h_lo, h
                                         ).then_inc(ps_full[j], 1)

            @block.scalar
            def _(act):
                with act.Fori(0, n_pairs) as c:
                    for j in range(2):
                        act.wait_ge(mixed[j], c)
                        for h in range(2):
                            act.wait_ge(ps_full[j], c * 2 + h + 1)
                            act.activation(z[j][:, 1 + h * HALF:1 + (h + 1) * HALF], psum[:, 2 * j + h, :],
                                           ACT.Copy).then_inc(evac[j], 1)

            @block.vector
            def _(dve):
                for j in range(2):
                    dve.memset(z[j][:, 0:1], 0.0).then_inc(pads, 1)
                dve.wait_ge(pads, 2)
                with dve.Fori(0, n_pairs) as c:
                    for j in range(2):
                        dve.wait_ge(evac[j], c * 2 + 2)
                        dve.tensor_tensor(diff[j][:, :], z[j][:, 0:T], z[j][:, 1:T + 1],
                                          ALU.subtract).then_inc(diffed[j], 1)
                        dve.wait_ge(diffed[j], c + 1)
                        dve.scalar_tensor_tensor(z_buf[:, c * 2 + j, :], diff[j][:, :],
                                                 vec[:, ds(c * 2 + (j + V_MU), 1)], z[j][:, 1:T + 1],
                                                 ALU.mult, ALU.add).then_inc(mixed[j], 1)

    def rwkv_prepare(tag):
        lora = at(f"{tag}_lora", [P, RWKV_W], F32, W_OFF)
        blk = at(f"{tag}_blk", [P, P], F32, W_OFF + 2048)
        reset = at(f"{tag}_reset", [P, HALF], F32, W_OFF + 2560)
        neg = at(f"{tag}_neg", [P, 2, RW_T], F32, W_OFF + 4608)
        sq, sig, iclr, norm_, rnorm, fac = ([at(f"{tag}_{n}{s}", [P, HALF], F32, T_OFF - 20480 + 4096 * i + 2048 * s)
                                             for s in range(2)] for i, n in enumerate(
            "sq sig iclr norm rnorm fac".split()))
        blocks = 2 * RW_T
        with ExitStack() as ctx:
            (loaded, loras, squared, lora_ps, sum_ps, sigs, iclrs, floors, roots, recips, scans,
             nkks, bbs, facs, ks, negs) = sems(
                ctx, tag, "loaded loras squared lora_ps sum_ps sigs iclrs floors roots recips scans "
                "nkks bbs facs ks negs")
            block = ctx.enter_context(nc.Block())

            @block.sync
            def _(sp):
                sp.dma_start(lora[0:64, :], w2).then_inc(loaded, 16)
                sp.dma_start(lora[64:128, :], a2).then_inc(loaded, 16)
                sp.dma_start(blk[:, :], consts[:, K_BLK:K_BLK + P]).then_inc(loaded, 16)
                sp.dma_start(reset[:, :], consts[:, K_RESET:K_RESET + HALF]).then_inc(loaded, 16)

            def place(n):
                ct, h = n // 2, n % 2
                return ct, slice(h * HALF, (h + 1) * HALF), n % 2

            @block.tensor
            def _(pe):
                pe.wait_ge(loaded, 64)
                pe.wait_ge(loras, 1)
                for n in range(blocks):
                    ct, cols, s = place(n)
                    if n >= 2:
                        pe.wait_ge(sigs, n - 1)
                        pe.wait_ge(iclrs, n - 1)
                        pe.wait_ge(floors, n - 1)
                    pe.matmul(psum[:, s, :], lora[0:64, ct * P:(ct + 1) * P], z_buf[0:64, Z_LO, cols],
                              start=True, stop=True)
                    pe.matmul(psum[:, 2 + s, :], lora[64:128, ct * P:(ct + 1) * P], z_buf[64:128, Z_LO, cols],
                              start=True, stop=True).then_inc(lora_ps, 1)
                    pe.wait_ge(squared, n + 1)
                    pe.matmul(psum[:, 4 + s, :], blk[:, :], sq[s][:, :], start=True, stop=True).then_inc(sum_ps, 1)

            @block.scalar
            def _(act):
                act.activation(z_buf[0:64, Z_LO, :], z_buf[0:64, Z_LO, :], ACT.Tanh).then_inc(loras, 1)
                act.activation(z_buf[:, Z_G, :], z_buf[:, Z_G, :], ACT.Sigmoid)
                for n in range(blocks):
                    ct, cols, s = place(n)
                    if n >= 2:
                        act.wait_ge(sum_ps, n - 1)
                        act.wait_ge(scans, n - 1)
                        act.wait_ge(facs, n - 1)
                        act.wait_ge(bbs, n - 1)
                    act.activation(sq[s][:, :], z_buf[:, Z_K + ct, cols], ACT.Square,
                                   scale=vec[:, V_KK + ct:V_KK + ct + 1]).then_inc(squared, 1)
                    act.wait_ge(lora_ps, n + 1)
                    act.activation(sig[s][:, :], psum[:, s, :], ACT.Sigmoid,
                                   bias=vec[:, V_W0 + ct:V_W0 + ct + 1]).then_inc(sigs, 1)
                    act.activation(iclr[s][:, :], psum[:, 2 + s, :], ACT.Sigmoid,
                                   bias=vec[:, V_A0 + ct:V_A0 + ct + 1]).then_inc(iclrs, 1)
                    act.wait_ge(floors, n + 1)
                    act.activation(norm_[s][:, :], norm_[s][:, :], ACT.Sqrt).then_inc(roots, 1)

            @block.vector
            def _(dve):
                dve.tensor_scalar(neg[:, 0, :], vec[:, V_KK:V_KK + RW_T], -1.0, None, ALU.mult).then_inc(negs, 1)
                dve.tensor_scalar(neg[:, 1, :], vec[:, V_KA:V_KA + RW_T], -1.0, 1.0, ALU.mult, ALU.add
                                  ).then_inc(negs, 1)
                dve.wait_ge(negs, 2)
                dve.wait_ge(loaded, 64)
                for n in range(blocks):
                    ct, cols, s = place(n)
                    dve.wait_ge(sum_ps, n + 1)
                    if n >= 2:
                        dve.wait_ge(recips, n - 1)
                    dve.tensor_scalar(norm_[s][:, :], psum[:, 4 + s, :], 1e-24, None, ALU.max).then_inc(floors, 1)
                    dve.wait_ge(sigs, n + 1)
                    dve.tensor_tensor_scan(cum_buf[:, ct, cols], reset[:, :], sig[s][:, :], 0.0,
                                           ALU.mult, ALU.add).then_inc(scans, 1)
                    dve.wait_ge(iclrs, n + 1)
                    dve.tensor_scalar(fac[s][:, :], iclr[s][:, :], vec[:, V_KA + ct:V_KA + ct + 1],
                                      neg[:, 1, ct:ct + 1], ALU.mult, ALU.add).then_inc(facs, 1)
                    dve.wait_ge(roots, n + 1)
                    dve.reciprocal(rnorm[s][:, :], norm_[s][:, :]).then_inc(recips, 1)
                    dve.wait_ge(recips, n + 1)
                    dve.scalar_tensor_tensor(nkk_buf[:, ct, cols], z_buf[:, Z_K + ct, cols], neg[:, 0, ct:ct + 1],
                                             rnorm[s][:, :], ALU.mult, ALU.mult).then_inc(nkks, 1)
                    dve.wait_ge(nkks, n + 1)
                    dve.scalar_tensor_tensor(bb_buf[:, ct, cols], nkk_buf[:, ct, cols], -1.0, iclr[s][:, :],
                                             ALU.mult, ALU.mult).then_inc(bbs, 1)
                    dve.wait_ge(facs, n + 1)
                    dve.wait_ge(squared, n + 1)
                    dve.tensor_tensor(z_buf[:, Z_K + ct, cols], z_buf[:, Z_K + ct, cols], fac[s][:, :],
                                      ALU.mult).then_inc(ks, 1)

    def rwkv_chunks(tag):
        off = [W_OFF]

        def buf(name, shape, nbytes):
            t = at(f"{tag}_{name}", shape, F32, off[0])
            off[0] += nbytes
            return t
        e_in = buf("ein", [P, RW_T, 2, CHUNK + 1], 2112)
        e_neg = buf("eneg", [P, RW_T, P], 2048)
        ar = buf("ar", [P, RW_T, 2, P], 4096)
        bt = buf("bt", [P, RW_T, P], 2048)
        kt = buf("kt", [P, RW_T, P], 2048)
        bh = buf("bh", [P, RW_T, P], 2048)
        kh = buf("kh", [P, RW_T, P], 2048)
        tok = buf("tok", [P, 4, RWKV_W], 8192)
        mx = buf("mx", [P, 2, 2, 4 * P], 8192)
        lsb = buf("l", [P, 2, 2, P], 2048)
        xs = buf("x", [P, 2, 2, 2 * P], 4096)
        zt = buf("zt", [P, 2, 2, P], 2048)
        akv = buf("akv", [P, 2, 2, HD], 1024)
        pq = buf("pq", [P, 2, 2, P], 2048)
        gt = buf("gt", [P, 2, P], 1024)
        mt = buf("mt", [P, 2, 2, P], 2048)
        nsb = buf("n", [P, 2, 2, HD], 1024)
        off[0] = A_OFF + 49152
        st = buf("st", [P, RW_T, 2, HD], 2048)
        sbd = buf("sbd", [P, RW_T, 2, P], 4096)
        mask_ab = buf("mab", [P, 4 * P], 2048)
        mask_l = buf("ml", [P, P], 512)
        mask_1 = buf("m1", [P, 2 * P], 1024)
        mask_lev = buf("mlev", [P, 5, P], 2560)
        id64 = buf("id64", [P, HD], 256)
        ysb = buf("y", [P, N_RWKV, HD], 2048)
        stat = buf("stat", [P, 3, N_RWKV], 96)
        vt = at(f"{tag}_vt", [P, RW_T, P], F32, C_OFF + 4096)
        carrier = at(f"{tag}_carrier", [P, 4], F32, C_OFF + 3424)
        with ExitStack() as ctx:
            (consts_in, zeroed, exp_in, exp_neg, v_copied, prepared, hats, t_turned, tok_act, tok_dve,
             ab, mxs, ls, x0a, x0, akv_ps, akv_sb, z_ps, zts, xx_ps, xadd, pq_ps, pqs, mn_ps, n_sb, mts,
             g_ps, gts, ms_ps, sts, sbds, y_ps, ys, sums, centred, squares, varis, roots, rrs, normed,
             y_turned, y_out) = sems(
                ctx, tag, "consts_in zeroed exp_in exp_neg v_copied prepared hats t_turned tok_act tok_dve "
                "ab mxs ls x0a x0 akv_ps akv_sb z_ps zts xx_ps xadd pq_ps pqs mn_ps n_sb mts "
                "g_ps gts ms_ps sts sbds y_ps ys sums centred squares varis roots rrs normed "
                "y_turned y_out")
            block = ctx.enter_context(nc.Block())
            per_e = [slice(0, HD), slice(HD, P)]

            def wc(ct=slice(None), rows=slice(None)):
                return e_in[rows, ct, :, CHUNK:CHUNK + 1]

            @block.sync
            def _(sp):
                for dst, col, n in ((mask_ab, K_AB, 4 * P), (mask_l, K_L, P), (mask_1, K_M1, 2 * P),
                                    (id64, K_ID64, HD)):
                    sp.dma_start(dst[:, :], consts[:, col:col + n]).then_inc(consts_in, 16)
                sp.dma_start(mask_lev[:, :, :], consts[:, K_LEV:K_LEV + 5 * P].rearrange("p (l n) -> p l n", l=5)
                             ).then_inc(consts_in, 16)

            @block.scalar
            def _(act):
                def pair(i, g, s):
                    pr = 2 * g + s
                    n = i * 4 + pr
                    return pr, n
                def wait_here(n):
                    act.activation(carrier[:, n:n + 1], cst[:, 1:2], ACT.Copy)

                with act.Fori(0, TT) as i:
                    cols = ds(i * P, P)
                    act.wait_ge(mts, i * 4)
                    act.wait_ge(hats, i * 2)
                    act.wait_ge(prepared, i * 4)
                    wait_here(0)
                    src = cum_buf[:, :, cols].rearrange("p c (j t) -> p c j t", j=2)
                    act.activation(e_in[:, :, :, 1:CHUNK + 1], src, ACT.Exp, scale=-DECAY).then_inc(exp_in, 1)
                    act.wait_ge(varis, i)
                    wait_here(1)
                    act.activation(e_neg[:, :, :], cum_buf[:, :, cols], ACT.Exp, scale=DECAY).then_inc(exp_neg, 1)
                    act.wait_ge(t_turned, i * 4)
                    wait_here(2)
                    act.activation(vt[:, :, :], z_buf[:, Z_V:Z_V + RW_T, cols], ACT.Copy).then_inc(v_copied, 1)
                    act.wait_ge(t_turned, i * 4 + 4)
                    act.wait_ge(y_ps, i * 4)
                    for bank in (0, 3):
                        act.activation(tok[:, bank, :], psum[:, bank, :], ACT.Copy).then_inc(tok_act, 1)
                    for g in range(2):
                        for s in range(2):
                            n = i * 4 + 2 * g + s
                            act.wait_ge(akv_ps, n + 1)
                            act.activation(akv[:, s, :, :], psum[:, 5 + 2 * s, 0:P].rearrange("p (e v) -> p e v", e=2),
                                           ACT.Copy).then_inc(akv_sb, 1)
                        for s in range(2):
                            n = i * 4 + 2 * g + s
                            act.wait_ge(pq_ps, n + 1)
                            act.activation(pq[:, s, :, :], psum[:, 4 + 2 * s, 0:2 * P].rearrange("p (e v) -> p e v", e=2),
                                           ACT.Copy).then_inc(pqs, 1)
                        for s in range(2):
                            n = i * 4 + 2 * g + s
                            act.wait_ge(mn_ps, n + 1)
                            act.activation(nsb[:, s, :, :], psum[:, 2:4, HD:P], ACT.Copy).then_inc(n_sb, 1)
                            for j in range(2):
                                act.wait_ge(sts, n * 2 + j + 1)
                                to = 1 - j
                                if j:
                                    act.wait_ge(y_ps, n + 1)
                                for e in range(2):
                                    act.activation(sbd[per_e[e], 2 * g + s, to, per_e[e]],
                                                   st[per_e[e], 2 * g + s, to, :], ACT.Copy).then_inc(sbds, 1)
                            act.wait_ge(y_ps, n + 1)
                            if g == 0 and s == 0:
                                act.wait_ge(centred, i)
                            act.activation(ysb[:, 4 * g + 2 * s:4 * g + 2 * s + 2, :],
                                           psum[:, 4 + 2 * s, 0:P].rearrange("p (e v) -> p e v", e=2),
                                           ACT.Copy).then_inc(ys, 1)
                    act.wait_ge(centred, i + 1)
                    act.activation(e_neg[:, :, :], ysb[:, :, :].rearrange("p h v -> p (h v)").rearrange(
                        "p (c t) -> p c t", c=RW_T), ACT.Square).then_inc(squares, 1)
                    act.wait_ge(varis, i + 1)
                    act.activation(stat[:, 2, :], stat[:, 1, :], ACT.Sqrt, scale=1.0 / HD, bias=cst[:, 1:2]
                                   ).then_inc(roots, 1)
                    act.wait_ge(y_turned, i + 1)
                    wait_here(3)
                    act.activation(y_buf[:, RW_T:2 * RW_T, cols], psum[:, 0, :].rearrange("p (c t) -> p c t", c=RW_T),
                                   ACT.Copy).then_inc(y_out, 1)

            @block.gpsimd
            def _(pool):
                def bcast(a):
                    return a.broadcast_to([P, RW_T, 2, CHUNK])

                def split(a):
                    return a.rearrange("p c (j t) -> p c j t", j=2)
                pool.wait_ge(consts_in, 80)
                with pool.Fori(0, TT) as i:
                    pool.wait_ge(t_turned, i * 4)
                    for n, (dst, src) in enumerate(((bh, bt), (kh, kt))):
                        pool.wait_ge(prepared, i * 4 + 3 + n)
                        pool.tensor_tensor(split(dst[:, :, :]), split(src[:, :, :]), bcast(wc()), ALU.mult
                                           ).then_inc(hats, 1)
                    for g in range(2):
                        for s in range(2):
                            n = i * 4 + 2 * g + s
                            pool.wait_ge(mxs, n + 1)
                            pool.wait_ge(ls, n + 1)
                            pool.wait_ge(pq_ps, i * 4 + 2 * g)
                            one = mask_1[:, 0:P].rearrange("p (e t) -> p e t", e=1).broadcast_to([P, 2, P])
                            one_t = mask_1[:, P:2 * P].rearrange("p (e t) -> p e t", e=1).broadcast_to([P, 2, P])
                            idb = ident[:, :].rearrange("p (e t) -> p e t", e=1).broadcast_to([P, 2, P])
                            pool.tensor_tensor(xs[:, s, :, 0:P], lsb[:, s, :, :], one, ALU.mult).then_inc(x0a, 1)
                            pool.tensor_tensor(xs[:, s, :, P:2 * P], mx[:, s, :, 0:P], one_t, ALU.mult).then_inc(x0a, 1)
                            for m in range(2):
                                pool.wait_ge(x0a, n * 2 + m + 1)
                                half = xs[:, s, :, m * P:(m + 1) * P]
                                pool.tensor_tensor(half, half, idb, ALU.add).then_inc(x0, 1)

            @block.vector
            def _(dve):
                def split(a):
                    return a.rearrange("p c (j t) -> p c j t", j=2)
                for m in (st, sbd, mt):
                    dve.memset(m[:, :, :, :], 0.0).then_inc(zeroed, 1)
                dve.memset(e_in[:, :, :, 0:1], 1.0).then_inc(zeroed, 1)
                dve.wait_ge(zeroed, 4)
                dve.wait_ge(consts_in, 80)
                with dve.Fori(0, TT) as i:
                    cols = ds(i * P, P)
                    dve.wait_ge(exp_in, i + 1)
                    dve.wait_ge(gts, i * 4)
                    dve.wait_ge(ab, i * 4)
                    dve.wait_ge(t_turned, i * 4)
                    dve.tensor_tensor(split(ar[:, :, 0, :]), split(nkk_buf[:, :, cols]), e_in[:, :, :, 0:CHUNK],
                                      ALU.mult).then_inc(prepared, 1)
                    dve.tensor_tensor(split(ar[:, :, 1, :]), split(z_buf[:, Z_R:Z_R + RW_T, cols]),
                                      e_in[:, :, :, 1:CHUNK + 1], ALU.mult).then_inc(prepared, 1)
                    dve.wait_ge(exp_neg, i + 1)
                    dve.wait_ge(hats, i * 2)
                    dve.tensor_tensor(bt[:, :, :], bb_buf[:, :, cols], e_neg[:, :, :], ALU.mult).then_inc(prepared, 1)
                    dve.tensor_tensor(kt[:, :, :], z_buf[:, Z_K:Z_K + RW_T, cols], e_neg[:, :, :], ALU.mult
                                      ).then_inc(prepared, 1)
                    dve.wait_ge(t_turned, i * 4 + 3)
                    dve.wait_ge(y_ps, i * 4)
                    for bank in (1, 2):
                        dve.tensor_copy(tok[:, bank, :], psum[:, bank, :]).then_inc(tok_dve, 1)
                    for g in range(2):
                        for s in range(2):
                            n = i * 4 + 2 * g + s
                            dve.wait_ge(ab, n + 1)
                            dve.wait_ge(y_ps, i * 4 + 2 * g)
                            dve.tensor_tensor(mx[:, s, :, :], psum[:, 0:2, :],
                                              mask_ab[:, :].rearrange("p (e t) -> p e t", e=1).broadcast_to([P, 2, 4 * P]),
                                              ALU.mult).then_inc(mxs, 1)
                            dve.tensor_tensor(lsb[:, s, :, :], psum[:, 2:4, 0:P],
                                              mask_l[:, :].rearrange("p (e t) -> p e t", e=1).broadcast_to([P, 2, P]),
                                              ALU.mult).then_inc(ls, 1)
                        for lev in range(5):
                            for s in range(2):
                                n = i * 4 + 2 * g + s
                                dve.wait_ge(z_ps, i * 20 + g * 10 + 2 * lev + s + 1)
                                dve.tensor_tensor(
                                    zt[:, s, :, :], psum[:, 4 + 2 * s, 0:2 * P].rearrange("p (e t) -> p e t", e=2),
                                    mask_lev[:, lev:lev + 1, :].broadcast_to([P, 2, P]), ALU.mult).then_inc(zts, 1)
                            for s in range(2):
                                dve.wait_ge(xx_ps, i * 20 + g * 10 + 2 * lev + s + 1)
                                part = slice(0, 2 * P) if lev < 4 else slice(P, 2 * P)
                                dve.tensor_tensor(xs[:, s, :, part], xs[:, s, :, part],
                                                  psum[:, 5 + 2 * s, :].rearrange("p (e t) -> p e t", e=2)[:, :, part],
                                                  ALU.add).then_inc(xadd, 1)
                        for s in range(2):
                            pr, n = 2 * g + s, i * 4 + 2 * g + s
                            dve.wait_ge(g_ps, n + 1)
                            dve.tensor_tensor(gt[:, s, :], psum[:, 5 + 2 * s, 0:P], ar[:, pr, 1, :], ALU.add
                                              ).then_inc(gts, 1)
                            dve.wait_ge(n_sb, n + 1)
                            for j in range(2):
                                for e in range(2):
                                    ins = dve.scalar_tensor_tensor(
                                        mt[per_e[e], s, j, per_e[e]], id64[per_e[e], :],
                                        e_in[per_e[e], pr, j, CHUNK:CHUNK + 1], psum[per_e[e], 2 + j, 0:HD],
                                        ALU.mult, ALU.add)
                            ins.then_inc(mts, 1)
                            for j in range(2):
                                dve.wait_ge(ms_ps, n * 2 + j + 1)
                                if j:
                                    dve.wait_ge(sbds, n * 4)
                                dve.tensor_tensor(st[:, pr, 1 - j, :], psum[:, 2 + j, 0:HD], nsb[:, s, j, :],
                                                  ALU.add).then_inc(sts, 1)
                    dve.wait_ge(ys, i * 4 + 4)
                    dve.tensor_reduce(stat[:, 0, :], ysb[:, :, :], AX_X, ALU.add).then_inc(sums, 1)
                    dve.wait_ge(sums, i * 2 + 1)
                    dve.tensor_scalar(stat[:, 0, :], stat[:, 0, :], 1.0 / HD, None, ALU.mult).then_inc(sums, 1)
                    dve.wait_ge(sums, i * 2 + 2)
                    mean = stat[:, 0, :].rearrange("p (h o) -> p h o", o=1).broadcast_to([P, N_RWKV, HD])
                    dve.tensor_tensor(ysb[:, :, :], ysb[:, :, :], mean, ALU.subtract).then_inc(centred, 1)
                    dve.wait_ge(squares, i + 1)
                    dve.tensor_reduce(stat[:, 1, :], e_neg[:, :, :].rearrange("p c t -> p (c t)").rearrange(
                        "p (h v) -> p h v", v=HD), AX_X, ALU.add).then_inc(varis, 1)
                    dve.wait_ge(roots, i + 1)
                    dve.reciprocal(stat[:, 2, :], stat[:, 2, :]).then_inc(rrs, 1)
                    dve.wait_ge(rrs, i + 1)
                    rstd = stat[:, 2, :].rearrange("p (h o) -> p h o", o=1).broadcast_to([P, N_RWKV, HD])
                    dve.wait_ge(centred, i + 1)
                    dve.tensor_tensor(ysb[:, :, :], ysb[:, :, :], rstd, ALU.mult).then_inc(normed, 1)

            @block.tensor
            def _(pe):
                def mm(out, lhs, rhs, start=True, stop=True, **k):
                    return pe.matmul(out, lhs, rhs, start=start, stop=stop, **k)
                pe.wait_ge(zeroed, 4)
                with pe.Fori(0, TT) as i:
                    pe.wait_ge(y_out, i)
                    pe.wait_ge(sts, i * 8)
                    for n, (src, ready, count) in enumerate((
                            (lambda ct: ar[:, ct, 0, :], prepared, i * 4 + 1), (lambda ct: bh[:, ct, :], hats, i * 2 + 1),
                            (lambda ct: kh[:, ct, :], hats, i * 2 + 2), (lambda ct: vt[:, ct, :], v_copied, i + 1))):
                        pe.wait_ge(ready, count)
                        for ct in range(RW_T):
                            tr = pe.transpose(psum[:, n, ct * P:(ct + 1) * P], src(ct), ident[:, :])
                        tr.then_inc(t_turned, 1)
                    pe.wait_ge(prepared, i * 4 + 4)
                    pe.wait_ge(tok_act, i * 2 + 2)
                    pe.wait_ge(tok_dve, i * 2 + 2)
                    for g in range(2):
                        for s in range(2):
                            pr, n = 2 * g + s, i * 4 + 2 * g + s
                            pe.wait_ge(mxs, n)
                            pe.wait_ge(ls, n)
                            if s == 0 and g:
                                pe.wait_ge(sts, n * 2)
                            for e in range(2):
                                rows = per_e[e]
                                both = ar[rows, pr, :, :].rearrange("p m t -> p (m t)")
                                mm(psum[:, e, 0:2 * P], bt[rows, pr, :], both)
                                mm(psum[:, e, 2 * P:4 * P], kt[rows, pr, :], both)
                                last = mm(psum[:, 2 + e, 0:P], ar[rows, pr, 0, :], bt[rows, pr, :])
                            last.then_inc(ab, 1)
                        for s in range(2):
                            pr, n = 2 * g + s, i * 4 + 2 * g + s
                            pe.wait_ge(mxs, n + 1)
                            for e in range(2):
                                last = mm(psum[:, 5 + 2 * s, e * HD:(e + 1) * HD], mx[:, s, e, 2 * P:3 * P],
                                          tok[:, 3, pr * P + e * HD:pr * P + (e + 1) * HD])
                            last.then_inc(akv_ps, 1)
                        for lev in range(5):
                            for s in range(2):
                                n = i * 4 + 2 * g + s
                                if lev == 0:
                                    pe.wait_ge(x0, n * 2 + 2)
                                    pe.wait_ge(akv_sb, n + 1)
                                else:
                                    pe.wait_ge(xadd, i * 20 + g * 10 + 2 * (lev - 1) + s + 1)
                                for e in range(2):
                                    last = mm(psum[:, 4 + 2 * s, e * P:(e + 1) * P], lsb[:, s, e, :],
                                              xs[:, s, e, P:2 * P])
                                last.then_inc(z_ps, 1)
                            for s in range(2):
                                pe.wait_ge(zts, i * 20 + g * 10 + 2 * lev + s + 1)
                                for e in range(2):
                                    if lev < 4:
                                        mm(psum[:, 5 + 2 * s, e * 2 * P:e * 2 * P + P], zt[:, s, e, :], xs[:, s, e, 0:P])
                                    last = mm(psum[:, 5 + 2 * s, e * 2 * P + P:(e + 1) * 2 * P], xs[:, s, e, 0:P],
                                              zt[:, s, e, :])
                                last.then_inc(xx_ps, 1)
                        for s in range(2):
                            pr, n = 2 * g + s, i * 4 + 2 * g + s
                            pe.wait_ge(xadd, i * 20 + g * 10 + 8 + s + 1)
                            for e in range(2):
                                x_t = xs[:, s, e, P:2 * P]
                                mm(psum[:, 4 + 2 * s, e * P:e * P + HD], x_t, tok[:, 0, pr * P + e * HD:pr * P + (e + 1) * HD])
                                last = mm(psum[:, 4 + 2 * s, e * P + HD:(e + 1) * P], x_t, akv[:, s, e, :])
                            last.then_inc(pq_ps, 1)
                        for s in range(2):
                            pr, n = 2 * g + s, i * 4 + 2 * g + s
                            pe.wait_ge(pqs, n + 1)
                            if s:
                                pe.wait_ge(sts, n * 2)
                            for e in range(2):
                                last = mm(psum[per_e[e], 5 + 2 * s, 0:P], pq[:, s, e, 0:HD], mx[:, s, e, P:2 * P])
                            last.then_inc(g_ps, 1)
                            for j in range(2):
                                rows = per_e[j]
                                for e in range(2):
                                    c = slice(pr * P + e * HD, pr * P + (e + 1) * HD)
                                    mm(psum[per_e[e], 2 + j, 0:HD], pq[rows, s, e, 0:HD], tok[rows, 1, c])
                                    mm(psum[per_e[e], 2 + j, HD:P], tok[rows, 1, c], pq[rows, s, e, HD:P],
                                       stop=False, skip_group_check=True)
                                    last = mm(psum[per_e[e], 2 + j, HD:P], tok[rows, 2, c], tok[rows, 3, c],
                                              start=False, skip_group_check=True)
                            last.then_inc(mn_ps, 1)
                            bank = psum[:, 4 + 2 * s, :]
                            for e in range(2):
                                c = slice(e * HD, (e + 1) * HD)
                                mm(bank[:, c], mx[:, s, e, P:2 * P], pq[:, s, e, HD:P], start=(e == 0), stop=False,
                                   skip_group_check=True)
                                mm(bank[:, c], mx[:, s, e, 3 * P:4 * P], tok[:, 3, pr * P + e * HD:pr * P + (e + 1) * HD],
                                   start=False, stop=False, skip_group_check=True)
                            pe.wait_ge(mts, n + 1)
                            mm(psum[:, 2, 0:HD], mt[:, s, 0, :], st[:, pr, 0, :]).then_inc(ms_ps, 1)
                            pe.wait_ge(gts, n + 1)
                            pe.wait_ge(sbds, n * 4)
                            mm(bank[0:HD, 0:P], gt[:, s, 0:HD], sbd[:, pr, 0, :], start=False, stop=True,
                               skip_group_check=True)
                            pe.wait_ge(sts, n * 2 + 1)
                            mm(psum[:, 3, 0:HD], mt[:, s, 1, :], st[:, pr, 1, :]).then_inc(ms_ps, 1)
                            pe.wait_ge(sbds, n * 4 + 2)
                            mm(bank[HD:P, 0:P], gt[:, s, HD:P], sbd[:, pr, 1, :], start=False, stop=True,
                               skip_group_check=True).then_inc(y_ps, 1)
                    pe.wait_ge(normed, i + 1)
                    pe.wait_ge(ls, i * 4 + 4)
                    flat = ysb[:, :, :].rearrange("p h v -> p (h v)")
                    for ct in range(RW_T):
                        tr = pe.transpose(psum[:, 0, ct * P:(ct + 1) * P], flat[:, ct * P:(ct + 1) * P], ident[:, :])
                    tr.then_inc(y_turned, 1)

    def rwkv_finish(tag):
        g2_sb = at(f"{tag}_g2", [P, RWKV_W], F32, W_OFF)
        blk = at(f"{tag}_blk", [P, P], F32, W_OFF + 2048)
        rk = [at(f"{tag}_rk{s}", [P, HALF], F32, T_OFF + 2048 * s) for s in range(2)]
        bonus = [at(f"{tag}_bonus{s}", [P, HALF], F32, T_OFF + 4096 + 2048 * s) for s in range(2)]
        with ExitStack() as ctx:
            loaded, rks, ps, scaled, bonuses, added, gated = sems(
                ctx, tag, "loaded rks ps scaled bonuses added gated")
            block = ctx.enter_context(nc.Block())

            @block.sync
            def _(sp):
                sp.dma_start(g2_sb[:, :], g2).then_inc(loaded, 16)
                sp.dma_start(blk[:, :], consts[:, K_BLK:K_BLK + P]).then_inc(loaded, 16)

            def place(n):
                ct, h = n // 2, n % 2
                return ct, slice(h * HALF, (h + 1) * HALF), n % 2

            @block.tensor
            def _(pe):
                pe.wait_ge(loaded, 32)
                for n in range(2 * RW_T):
                    ct, cols, s = place(n)
                    if n >= 2:
                        pe.wait_ge(gated, n - 1)
                    pe.matmul(psum[:, 2 + s, :], g2_sb[:, ct * P:(ct + 1) * P], z_buf[:, Z_G, cols],
                              start=True, stop=True)
                    pe.wait_ge(rks, n + 1)
                    pe.matmul(psum[:, s, :], blk[:, :], rk[s][:, :], start=True, stop=True).then_inc(ps, 1)

            @block.scalar
            def _(act):
                for n in range(2 * RW_T):
                    ct, cols, s = place(n)
                    y = y_buf[:, RW_T + ct, cols]
                    act.activation(y, y, ACT.Identity, scale=vec[:, V_LW + ct:V_LW + ct + 1],
                                   bias=vec[:, V_LB + ct:V_LB + ct + 1]).then_inc(scaled, 1)

            @block.vector
            def _(dve):
                def product(n):
                    ct, cols, s = place(n)
                    dve.wait_ge(ps, max(n - 1, 0))
                    dve.scalar_tensor_tensor(rk[s][:, :], z_buf[:, Z_R + ct, cols], vec[:, V_RK + ct:V_RK + ct + 1],
                                             z_buf[:, Z_K + ct, cols], ALU.mult, ALU.mult).then_inc(rks, 1)
                product(0)
                for n in range(2 * RW_T):
                    ct, cols, s = place(n)
                    y = y_buf[:, RW_T + ct, cols]
                    if n + 1 < 2 * RW_T:
                        product(n + 1)
                    dve.wait_ge(ps, n + 1)
                    dve.tensor_tensor(bonus[s][:, :], psum[:, s, :], z_buf[:, Z_V + ct, cols], ALU.mult
                                      ).then_inc(bonuses, 1)
                    dve.wait_ge(bonuses, n + 1)
                    dve.wait_ge(scaled, n + 1)
                    dve.tensor_tensor(y, y, bonus[s][:, :], ALU.add).then_inc(added, 1)
                    dve.wait_ge(added, n + 1)
                    dve.tensor_tensor(y, y, psum[:, 2 + s, :], ALU.mult).then_inc(gated, 1)
    setup()
    norm("n0", x, None, None, 0)
    fox_gates("fg")
    attention("fox", w_in0, FOX_W, N_FOX // 2, True)
    rwkv_project("rp")
    rwkv_prepare("rr")
    rwkv_chunks("rc")
    rwkv_finish("rf")
    clear_semaphores()
    down("o0", w_out0, y_buf, KT)
    norm("n1", x, 0, x_mid[0], 16)
    ffn_up("u0", 0)
    down("d0", w_down[0], g_buf, FT)
    norm("n2", x_mid[0], 2, x_mid[1], 8)
    clear_semaphores()
    rotary_tables("rt")
    attention("dil", w_in1, D, KT, False)
    clear_semaphores()
    down("o1", w_out1, y_buf, KT)
    norm("n3", x_mid[1], 1, x_mid[2], 24)
    ffn_up("u1", 1)
    down("d1", w_down[1], g_buf, FT)
    norm("n4", x_mid[2], 3, out, None)
    top.close()


def kernel(**inputs):
    import concourse.bacc as _bacc
    from concourse.bass_utils import run_bass_kernel_spmd as _run

    def a(name):
        return np.ascontiguousarray(inputs[name])

    consts, dil = constants()
    vecs = np.concatenate([a(n).reshape(-1, P) for n in (
        "norm_mix_pre", "norm_ffn_pre", "rwkv_mu", "rwkv_w0", "rwkv_a0", "rwkv_k_k", "rwkv_k_a",
        "rwkv_r_k", "rwkv_ln_w", "rwkv_ln_b")])
    conv = np.concatenate([a("ffn_conv_w"), a("ffn_conv_b")[:, None]], 1)
    g_post = np.concatenate([a("norm_mix_post"), a("norm_ffn_post")])
    arrays = dict(
        x=a("x")[0], positions=a("positions"), g_post=g_post, vecs=vecs, conv=conv,
        w_in0=a("even_w_in")[0], w_out0=a("even_w_out")[0], w_in1=a("odd_w_in")[0], w_out1=a("odd_w_out")[0],
        w_up=a("ffn_w_up"), w_down=a("ffn_w_down"), forget_bias=a("fox_forget_bias").reshape(N_FOX, 1),
        w2=a("rwkv_w2")[0], a2=a("rwkv_a2")[0], g2=a("rwkv_g2")[0], consts=consts, dil=dil)
    nc = _bacc.Bacc("TRN2", target_bir_lowering=False, num_devices=1)
    args = {n: nc.dram_tensor(f"in_{n}", v.shape, mybir.dt.from_np(v.dtype), kind="ExternalInput").ap()
            for n, v in arrays.items()}
    args["out"] = nc.dram_tensor("out_x", [T, D], F32, kind="ExternalOutput").ap()
    build(nc, **args)
    r = _run(nc, [{f"in_{n}": v for n, v in arrays.items()}], core_ids=[0])
    return np.asarray(r.results[0]["out_x"]).reshape(1, T, D)
```

```python
from contextlib import ExitStack

import numpy as np

import concourse.bass as bass
from concourse import mybir

F32 = mybir.dt.float32
F32R = mybir.dt.float32r
BF16 = mybir.dt.bfloat16
I32 = mybir.dt.int32
ACT = mybir.ActivationFunctionType
ALU = mybir.AluOpType
AX_X = mybir.AxisListType.X
ds = bass.ds

P = 128
D = 1024
T = 1024
KT = D // P
TT = T // P
HALF = 512
HD = 64
N_FOX = 8
N_RWKV = 8
FOX_W = N_FOX * HD
RWKV_W = N_RWKV * HD
RW_T = RWKV_W // P
FOX_IN = 3 * FOX_W + N_FOX
RWKV_IN = 3 * RWKV_W + 256
DIL_W = D
D_FF = ((8 * D // 3 + 127) // 128) * 128
FT = D_FF // P
CONV = 3
RMS_EPS = 1e-6
GN_EPS = 64e-5
CHUNK = 64
DECAY = float(np.exp(-0.5))
ATT_SCALE = HD ** -0.5
NEG = -1e30

BASE = 16512
A_OFF = BASE
B_OFF = A_OFF + 65536
W_OFF = B_OFF + 90112
T_OFF = W_OFF + 28672
C_OFF = T_OFF + 20608

V_PRE = 0
V_MU = 32
V_W0, V_A0, V_KK, V_KA, V_RK, V_LW, V_LB = (46 + 4 * n for n in range(7))
V_ROWS = 74

K_ID = 0
K_BLK = 128
K_AB = 256
K_L = 768
K_M1 = 896
K_LEV = 1152
K_ID64 = 1792
K_RESET = 1856
K_FREQ = 2368
K_CAUS = 2370
K_COLS = 2498


def constants():
    i, j = np.arange(P)[:, None], np.arange(P)[None, :]
    same = (i // CHUNK) == (j // CHUNK)
    c = np.zeros((P, K_COLS), np.float32)
    c[:, K_ID:K_ID + P] = i == j
    c[:, K_BLK:K_BLK + P] = same
    strict_t, incl_t = same & (i < j), same & (i <= j)
    for n, m in enumerate((strict_t, incl_t, strict_t, incl_t)):
        c[:, K_AB + n * P:K_AB + (n + 1) * P] = m
    c[:, K_L:K_L + P] = same & (i > j)

    def lower_left(b):
        return ((i // (2 * b)) == (j // (2 * b))) & (i % (2 * b) >= b) & (j % (2 * b) < b)
    c[:, K_M1:K_M1 + P] = lower_left(1)
    c[:, K_M1 + P:K_M1 + 2 * P] = lower_left(1).T
    for n in range(5):
        c[:, K_LEV + n * P:K_LEV + (n + 1) * P] = lower_left(2 << n).T | (i == j)
    c[:, K_ID64:K_ID64 + 64] = (i % 64) == j[:, :64]
    c[:, K_RESET:K_RESET + HALF] = (np.arange(HALF) % CHUNK != 0)[None]
    rot = HD // 4
    freq = np.float32(500000.0) ** (-np.arange(0, rot, 2, dtype=np.float32) / np.float32(rot))
    for r in range(P):
        d = r % HD
        if d < rot:
            c[r, K_FREQ] = freq[d % (rot // 2)]
            c[r, K_FREQ + 1] = -1.0 if d < rot // 2 else 1.0
    c[:, K_CAUS:K_CAUS + P] = np.where(j > i, NEG, 0.0)
    dist = i - np.arange(T)[None, :] + (TT - 1) * P
    count = sum((dist >= 0) & (dist % d == 0) & (dist <= w) for w, d in ((128, 1), (512, 4), (2048, 16)))
    dil = np.stack([np.where(count > 0, 0.0, NEG), count], 1).astype(np.float32)
    return c, dil


def build(nc, x, positions, g_post, vecs, conv, w_in0, w_out0, w_in1, w_out1, w_up, w_down,
          forget_bias, w2, a2, g2, consts, dil, out):
    top = ExitStack()

    def at(name, shape, dt, off):
        return nc.alloc_sbuf_tensor_at(name, shape, dt, offset=off)

    ident = at("ident", [P, P], F32, C_OFF)
    vec = at("vec", [P, V_ROWS], F32, C_OFF + 512)
    h_hi = at("h_hi", [P, KT, T], F32R, A_OFF)
    h_lo = at("h_lo", [P, KT, T], F32R, A_OFF + 32768)
    m_buf = at("m_buf", [P, TT, D], F32, A_OFF)
    g_buf = at("g_buf", [P, FT, T], F32, B_OFF)
    y_buf = at("y_buf", [P, KT, T], F32, B_OFF)
    cst = at("cst", [P, 8], F32, C_OFF + 832)
    convc = at("convc", [P, 2, 4, 2 * FT], F32, C_OFF + 1024)
    x_mid = [nc.dram_tensor(f"x_mid{n}", [T, D], F32, kind="Internal").ap() for n in range(3)]
    negc_dram = nc.dram_tensor("negc_dram", [N_FOX, T], F32, kind="Internal").ap()
    psum = top.enter_context(nc.psum_tensor("psum", [P, 8, HALF], F32))

    used_ids = []

    def sems(ctx, stage, names):
        got = [ctx.enter_context(nc.semaphore(f"{stage}_{n}")) for n in names.split()]
        used_ids.extend(s.num for s in got)
        return got

    def clear_semaphores():
        ids = sorted(used_ids)
        used_ids.clear()
        with nc.Block() as block:
            @block.gpsimd
            def _(pool):
                first = ids[0]
                for n, num in enumerate(ids):
                    if n + 1 == len(ids) or ids[n + 1] != num + 1:
                        pool.sem_clear(range(first, num + 1))
                        first = ids[n + 1] if n + 1 < len(ids) else 0

    def setup():
        rows = at("vec_rows", [V_ROWS, P], F32, B_OFF)
        crow = at("conv_rows", [2 * FT, 8, P], F32, B_OFF + 1024)
        with ExitStack() as ctx:
            loaded, turned, copied = sems(ctx, "set", "loaded turned copied")
            block = ctx.enter_context(nc.Block())

            @block.sync
            def _(sp):
                sp.dma_start(ident[:, :], consts[:, K_ID:K_ID + P]).then_inc(loaded, 16)
                sp.dma_start(rows[:, :], vecs).then_inc(loaded, 16)
                sp.dma_start(crow[:, :, :], conv.rearrange("l j (t p) -> t (l j) p", p=P)).then_inc(loaded, 16)

            @block.tensor
            def _(pe):
                pe.wait_ge(loaded, 48)
                for n in range(8):
                    pe.transpose(psum[:, 0, n * 2 * FT:(n + 1) * 2 * FT], crow[:, n, :],
                                 ident[0:2 * FT, 0:2 * FT])
                pe.transpose(psum[:, 1, 0:V_ROWS], rows[:, :],
                             ident[0:V_ROWS, 0:V_ROWS]).then_inc(turned, 1)

            @block.vector
            def _(dve):
                for n, value in enumerate((RMS_EPS, GN_EPS, 1.0)):
                    dve.memset(cst[:, n:n + 1], value).then_inc(copied, 1)
                dve.wait_ge(turned, 1)
                dve.tensor_copy(convc[:, :, :, :].rearrange("p l j t -> p (l j t)"),
                                psum[:, 0, 0:16 * FT]).then_inc(copied, 1)
                dve.tensor_copy(vec[:, :], psum[:, 1, 0:V_ROWS]).then_inc(copied, 1)

    def norm(tag, x_in, post_row, x_out, pre_col):
        last = pre_col is None
        m = m_buf
        xt = at(f"{tag}_x", [P, TT, D], F32, B_OFF)
        hn = at(f"{tag}_hn", [P, TT, D], F32, B_OFF + 32768)
        gp = at(f"{tag}_gp", [P, D], F32, T_OFF)
        junk = at(f"{tag}_junk", [P, 2, D], F32, T_OFF + 4096)
        st = at(f"{tag}_st", [P, 4, TT], F32, T_OFF + 12288)
        hi, lo = h_hi, h_lo
        with ExitStack() as ctx:
            (gain, m_sq, m_rms, m_rs, x_new, x_sq, x_rms, x_rs, scaled, turned, hi_done, lo_done, stored, tiny) = sems(
                ctx, tag, "gain m_sq m_rms m_rs x_new x_sq x_rms x_rs scaled turned hi_done lo_done stored tiny")
            x_in_sem = sems(ctx, tag, " ".join(f"xin{i}" for i in range(TT)))
            block = ctx.enter_context(nc.Block())

            @block.sync
            def _(sp):
                if post_row is not None:
                    sp.dma_start(gp[:, :], g_post[post_row:post_row + 1, :].broadcast_to([P, D])
                                 ).then_inc(gain, 16)
                for i in range(TT):
                    sp.dma_start(xt[:, i, :], x_in[i * P:(i + 1) * P, :]).then_inc(x_in_sem[i], 16)
                if post_row is not None:
                    for i in range(TT):
                        sp.wait_ge(x_new, i + 1)
                        sp.dma_start(x_out[i * P:(i + 1) * P, :], xt[:, i, :]).then_inc(stored, 16)
                    sp.wait_ge(stored, 16 * TT)

            @block.scalar
            def _(act):
                if post_row is not None:
                    for i in range(TT):
                        act.activation(junk[:, 0, :], m[:, i, :], ACT.Square,
                                       accum_out=st[:, 0, i:i + 1]).then_inc(m_sq, 1)
                        act.wait_ge(m_sq, i + 1)
                        act.activation(st[:, 1, i:i + 1], st[:, 0, i:i + 1], ACT.Sqrt, scale=1.0 / D,
                                       bias=cst[:, 0:1]).then_inc(m_rms, 1)
                for i in range(TT if not last else 0):
                    if post_row is not None:
                        act.wait_ge(x_new, i + 1)
                    else:
                        act.wait_ge(x_in_sem[i], 16)
                    act.activation(junk[:, 0, :], xt[:, i, :], ACT.Square,
                                   accum_out=st[:, 2, i:i + 1]).then_inc(x_sq, 1)
                    act.wait_ge(x_sq, i + 1)
                    act.activation(st[:, 3, i:i + 1], st[:, 2, i:i + 1], ACT.Sqrt, scale=1.0 / D,
                                   bias=cst[:, 0:1]).then_inc(x_rms, 1)
                    act.wait_ge(x_rs, i + 1)
                    act.activation(hn[:, i, :], xt[:, i, :], ACT.Copy, scale=st[:, 3, i:i + 1]).then_inc(scaled, 1)
                if last:
                    return
                for n in range(2 * KT):
                    k, h = n % KT, n // KT
                    act.wait_ge(turned, n + 1)
                    act.activation(hi[:, k, h * HALF:(h + 1) * HALF], psum[:, n % 8, :], ACT.Copy,
                                   scale=vec[:, pre_col + k:pre_col + k + 1]).then_inc(hi_done, 1)

            @block.vector
            def _(dve):
                n_tiny = 0
                if post_row is not None:
                    dve.wait_ge(gain, 16)
                for i in range(TT):
                    if post_row is not None:
                        dve.wait_ge(m_rms, i + 1)
                        dve.reciprocal(st[:, 1, i:i + 1], st[:, 1, i:i + 1]).then_inc(m_rs, 1)
                        dve.wait_ge(m_rs, i + 1)
                        dve.scalar_tensor_tensor(junk[:, 1, :], m[:, i, :], st[:, 1, i:i + 1], gp[:, :],
                                                 ALU.mult, ALU.mult).then_inc(tiny, 1)
                        n_tiny += 1
                        dve.wait_ge(tiny, n_tiny)
                        dve.wait_ge(x_in_sem[i], 16)
                        dve.tensor_tensor(xt[:, i, :], xt[:, i, :], junk[:, 1, :], ALU.add).then_inc(x_new, 1)
                        if not last and i == 0:
                            continue
                    if last:
                        continue
                    for b in ([i] if post_row is None else [i - 1] + ([i] if i == TT - 1 else [])):
                        dve.wait_ge(x_rms, b + 1)
                        dve.reciprocal(st[:, 3, b:b + 1], st[:, 3, b:b + 1]).then_inc(x_rs, 1)
                if last:
                    return
                for n in range(2 * KT):
                    k, h = n % KT, n // KT
                    dve.wait_ge(hi_done, n + 1)
                    dve.scalar_tensor_tensor(lo[:, k, h * HALF:(h + 1) * HALF], psum[:, n % 8, :],
                                             vec[:, pre_col + k:pre_col + k + 1],
                                             hi[:, k, h * HALF:(h + 1) * HALF],
                                             ALU.mult, ALU.subtract).then_inc(lo_done, 1)

            if not last:
                @block.tensor
                def _(pe):
                    pe.wait_ge(scaled, TT)
                    for n in range(2 * KT):
                        k, h = n % KT, n // KT
                        if n >= 8:
                            pe.wait_ge(lo_done, n - 7)
                        for i in range(4):
                            t = pe.transpose(psum[:, n % 8, i * P:(i + 1) * P],
                                             hn[:, 4 * h + i, k * P:(k + 1) * P], ident[:, :])
                        t.then_inc(turned, 1)

    def split_weights(pool, raw, whi, wlo, zero, hi_sem, hi_count, done):
        n = raw.shape[-1]
        pool.tensor_tensor(whi, raw, zero[:, 0:1].broadcast_to([P, raw.shape[1], n]) if len(raw.shape) == 3
                           else zero[:, 0:1].broadcast_to([P, n]), ALU.add).then_inc(hi_sem, 1)
        pool.wait_ge(hi_sem, hi_count)
        pool.tensor_tensor(wlo, raw, whi, ALU.subtract).then_inc(done, 1)

    def project_half(pe, bank, whi, wlo, hhi, hlo, half, ks=range(KT)):
        cols = slice(half * HALF, (half + 1) * HALF)
        for k in ks:
            pe.matmul(bank, whi[:, k, :], hhi[:, k, cols], start=(k == 0), stop=False)
            pe.matmul(bank, whi[:, k, :], hlo[:, k, cols], start=False, stop=False)
            mm = pe.matmul(bank, wlo[:, k, :], hhi[:, k, cols], start=False, stop=(k == KT - 1))
        return mm

    def ffn_up(tag, layer):
        hi, lo = h_hi, h_lo
        g = g_buf
        raw = [at(f"{tag}_raw{j}", [P, KT, P], F32, W_OFF + 4096 * j) for j in range(2)]
        whi = [at(f"{tag}_whi{j}", [P, KT, P], F32R, W_OFF + 8192 + 4096 * j) for j in range(2)]
        wlo = [at(f"{tag}_wlo{j}", [P, KT, P], F32R, W_OFF + 16384 + 4096 * j) for j in range(2)]
        zero = at(f"{tag}_zero", [P, 8], F32, W_OFF + 24576)
        u = [at(f"{tag}_u{j}", [P, T + 2], F32, T_OFF + 4128 * j) for j in range(2)]
        acc = [at(f"{tag}_acc{j}", [P, T], F32, T_OFF + 8256 + 4096 * j) for j in range(2)]
        act_g = at(f"{tag}_actg", [P, T], F32, T_OFF + 16448)
        w = w_up[layer].rearrange("(k p) n -> p k n", p=P)
        with ExitStack() as ctx:
            zeroed, pads, split_hi, gelu_done, gated = sems(ctx, tag, "zeroed pads split_hi gelu gated")
            raw_in = sems(ctx, tag, "raw0 raw1")
            w_full = sems(ctx, tag, "wfull0 wfull1")
            ps_full = sems(ctx, tag, "psfull0 psfull1")
            evac = sems(ctx, tag, "evac0 evac1")
            conv1 = sems(ctx, tag, "conv1_0 conv1_1")
            conv2 = sems(ctx, tag, "conv2_0 conv2_1")
            block = ctx.enter_context(nc.Block())

            @block.sync
            def _(sp):
                with sp.Fori(0, FT) as c:
                    for j in range(2):
                        sp.wait_ge(w_full[j], c)
                        sp.dma_start(raw[j][:, :, :], w[:, :, ds(c * P + j * D_FF, P)]).then_inc(raw_in[j], 16)

            @block.gpsimd
            def _(pool):
                pool.memset(zero[:, :], 0.0).then_inc(zeroed, 1)
                pool.wait_ge(zeroed, 1)
                with pool.Fori(0, FT) as c:
                    for j in range(2):
                        pool.wait_ge(ps_full[j], c * 2)
                        pool.wait_ge(raw_in[j], c * 16 + 16)
                        split_weights(pool, raw[j][:, :, :], whi[j][:, :, :], wlo[j][:, :, :], zero,
                                      split_hi, c * 2 + j + 1, w_full[j])

            @block.tensor
            def _(pe):
                with pe.Fori(0, FT) as c:
                    for j in range(2):
                        for h in range(2):
                            pe.wait_ge(evac[j], c * 2)
                            pe.wait_ge(w_full[j], c + 1)
                            project_half(pe, psum[:, 2 * j + h, :], whi[j], wlo[j], hi, lo, h
                                         ).then_inc(ps_full[j], 1)

            @block.scalar
            def _(act):
                cc = convc[:, layer, :, :]
                with act.Fori(0, FT) as c:
                    def take(j):
                        act.wait_ge(conv2[j], c)
                        act.wait_ge(gated if j else gelu_done, c)
                        for h in range(2):
                            bank = psum[:, 2 * j + h, :]
                            act.wait_ge(ps_full[j], c * 2 + h + 1)
                            act.activation(u[j][:, 2 + h * HALF:2 + (h + 1) * HALF], bank, ACT.Copy)
                            act.activation(acc[j][:, h * HALF:(h + 1) * HALF], bank, ACT.Identity,
                                           scale=cc[:, 2, ds(c + j * FT, 1)],
                                           bias=cc[:, 3, ds(c + j * FT, 1)]).then_inc(evac[j], 1)
                    take(0)
                    act.wait_ge(conv2[0], c + 1)
                    act.wait_ge(gated, c)
                    act.activation(act_g[:, :], acc[0][:, :], ACT.Gelu_apprx_tanh).then_inc(gelu_done, 1)
                    take(1)

            @block.vector
            def _(dve):
                cc = convc[:, layer, :, :]
                for j in range(2):
                    dve.memset(u[j][:, 0:2], 0.0).then_inc(pads, 1)
                dve.wait_ge(pads, 2)
                with dve.Fori(0, FT) as c:
                    for j in range(2):
                        dve.wait_ge(evac[j], c * 2 + 2)
                        if j == 0:
                            dve.wait_ge(gelu_done, c)
                        dve.scalar_tensor_tensor(acc[j][:, :], u[j][:, 1:T + 1], cc[:, 1, ds(c + j * FT, 1)],
                                                 acc[j][:, :], ALU.mult, ALU.add).then_inc(conv1[j], 1)
                        dve.wait_ge(conv1[j], c + 1)
                        dve.scalar_tensor_tensor(acc[j][:, :], u[j][:, 0:T], cc[:, 0, ds(c + j * FT, 1)],
                                                 acc[j][:, :], ALU.mult, ALU.add).then_inc(conv2[j], 1)
                    dve.wait_ge(gelu_done, c + 1)
                    dve.wait_ge(conv2[1], c + 1)
                    dve.tensor_tensor(g[:, c, :], act_g[:, :], acc[1][:, :], ALU.mult).then_inc(gated, 1)

    def down(tag, w, src, n_tiles):
        m = m_buf
        raw = [at(f"{tag}_raw{j}", [P, HALF], F32, W_OFF + 2048 * j) for j in range(2)]
        whi = [at(f"{tag}_whi{j}", [P, HALF], F32R, W_OFF + 4096 + 2048 * j) for j in range(2)]
        wlo = [at(f"{tag}_wlo{j}", [P, HALF], F32R, W_OFF + 8192 + 2048 * j) for j in range(2)]
        zero = at(f"{tag}_zero", [P, 8], F32, W_OFF + 24576)
        shi = [at(f"{tag}_shi{j}", [P, T], F32R, T_OFF + 4096 * j) for j in range(2)]
        slo = [at(f"{tag}_slo{j}", [P, T], F32R, T_OFF + 8192 + 4096 * j) for j in range(2)]
        pairs = n_tiles // 2
        with ExitStack() as ctx:
            zeroed, split_hi = sems(ctx, tag, "zeroed split_hi")
            raw_in = sems(ctx, tag, "raw0 raw1")
            w_full = sems(ctx, tag, "wfull0 wfull1")
            s_hi = sems(ctx, tag, "shi0 shi1")
            s_lo = sems(ctx, tag, "slo0 slo1")
            used = sems(ctx, tag, "used0 used1")
            bank_full = sems(ctx, tag, " ".join(f"bank{b}" for b in range(8)))
            bank_read = sems(ctx, tag, " ".join(f"read{b}" for b in range(8)))
            block = ctx.enter_context(nc.Block())

            @block.sync
            def _(sp):
                for nh in range(2):
                    with sp.Fori(nh * pairs, (nh + 1) * pairs) as c:
                        for j in range(2):
                            sp.wait_ge(w_full[j], c)
                            sp.dma_start(raw[j][:, :], w[ds(c * (2 * P) + (j - nh * n_tiles) * P, P),
                                                         nh * HALF:(nh + 1) * HALF]).then_inc(raw_in[j], 16)

            @block.gpsimd
            def _(pool):
                pool.memset(zero[:, :], 0.0).then_inc(zeroed, 1)
                pool.wait_ge(zeroed, 1)
                with pool.Fori(0, 2 * pairs) as c:
                    for j in range(2):
                        pool.wait_ge(used[j], c)
                        pool.wait_ge(raw_in[j], c * 16 + 16)
                        split_weights(pool, raw[j][:, :], whi[j][:, :], wlo[j][:, :], zero,
                                      split_hi, c * 2 + j + 1, w_full[j])

            @block.scalar
            def _(act):
                for nh in range(2):
                    with act.Fori(0, pairs) as c:
                        for j in range(2):
                            act.wait_ge(used[j], c + nh * pairs)
                            act.activation(shi[j][:, :], src[:, c * 2 + j, :], ACT.Copy).then_inc(s_hi[j], 1)
                    for b in range(0, 8, 2):
                        act.wait_ge(bank_full[b], nh + 1)
                        act.activation(m[:, b, nh * HALF:(nh + 1) * HALF], psum[:, b, :],
                                       ACT.Copy).then_inc(bank_read[b], 1)

            @block.vector
            def _(dve):
                for nh in range(2):
                    with dve.Fori(0, pairs) as c:
                        for j in range(2):
                            dve.wait_ge(s_hi[j], c + nh * pairs + 1)
                            dve.tensor_tensor(slo[j][:, :], src[:, c * 2 + j, :], shi[j][:, :],
                                              ALU.subtract).then_inc(s_lo[j], 1)
                    for b in range(1, 8, 2):
                        if b < 7:
                            dve.wait_ge(bank_full[b], nh + 1)
                        else:
                            dve.wait_ge(used[1], (nh + 1) * pairs)
                        dve.tensor_copy(m[:, b, nh * HALF:(nh + 1) * HALF], psum[:, b, :]).then_inc(bank_read[b], 1)

            @block.tensor
            def _(pe):
                def pair(nh, c, first=False, last=False):
                    for j in range(2):
                        pe.wait_ge(w_full[j], c + nh * pairs + 1)
                        pe.wait_ge(s_lo[j], c + nh * pairs + 1)
                        for b in range(8):
                            lhi, llo = shi[j][:, b * P:(b + 1) * P], slo[j][:, b * P:(b + 1) * P]
                            if first and j == 0 and nh:
                                pe.wait_ge(bank_read[b], nh)
                            pe.matmul(psum[:, b, :], lhi, whi[j][:, :], start=(first and j == 0), stop=False,
                                      skip_group_check=True)
                            pe.matmul(psum[:, b, :], lhi, wlo[j][:, :], start=False, stop=False,
                                      skip_group_check=True)
                            mm = pe.matmul(psum[:, b, :], llo, whi[j][:, :], start=False,
                                           stop=(last and j == 1), skip_group_check=True)
                            if last and j == 1 and b < 7:
                                mm.then_inc(bank_full[b], 1)
                        mm.then_inc(used[j], 1)
                for nh in range(2):
                    pair(nh, 0, first=True)
                    with pe.Fori(1, pairs - 1) as c:
                        pair(nh, c)
                    pair(nh, pairs - 1, last=True)

    def fox_gates(tag):
        col = 3 * FOX_W
        raw = at(f"{tag}_raw", [P, KT, P], F32, W_OFF)
        whi = at(f"{tag}_whi", [P, KT, P], F32R, W_OFF + 4096)
        wlo = at(f"{tag}_wlo", [P, KT, P], F32R, W_OFF + 8192)
        zero = at(f"{tag}_zero", [P, 8], F32, W_OFF + 12288)
        bias = at(f"{tag}_bias", [N_FOX, 8], F32, W_OFF + 12320)
        size, low, nl, cum, ones = (at(f"{tag}_{n}", [N_FOX, T], F32, B_OFF + 4096 * i)
                                    for i, n in enumerate("size low nl cum ones".split()))
        with ExitStack() as ctx:
            loaded, zeroed, split_hi, w_full, proj, act_done, dve_done, bias_in, stored = sems(
                ctx, tag, "loaded zeroed split_hi w_full proj act_done dve_done bias_in stored")
            block = ctx.enter_context(nc.Block())

            @block.sync
            def _(sp):
                sp.dma_start(raw[:, :, :], w_in0.rearrange("(k p) n -> p k n", p=P)[:, :, col:col + P]
                             ).then_inc(loaded, 16)
                sp.dma_start(bias[:, 0:1], forget_bias).then_inc(bias_in, 16)
                sp.wait_ge(dve_done, 4)
                sp.dma_start(negc_dram, cum[:, :]).then_inc(stored, 16)
                sp.wait_ge(stored, 16)

            @block.gpsimd
            def _(pool):
                pool.memset(zero[:, :], 0.0).then_inc(zeroed, 1)
                pool.wait_ge(zeroed, 1)
                pool.wait_ge(loaded, 16)
                split_weights(pool, raw[:, :, :], whi[:, :, :], wlo[:, :, :], zero, split_hi, 1, w_full)

            @block.tensor
            def _(pe):
                pe.wait_ge(w_full, 1)
                for h in range(2):
                    project_half(pe, psum[:, h, :], whi, wlo, h_hi, h_lo, h).then_inc(proj, 1)

            @block.scalar
            def _(act):
                act.wait_ge(proj, 2)
                act.wait_ge(bias_in, 16)
                z = psum[0:N_FOX, 0:2, :].rearrange("p b n -> p (b n)")
                act.activation(size[:, :], z, ACT.Abs, bias=bias[:, 0:1]).then_inc(act_done, 1)
                act.wait_ge(act_done, 1)
                act.activation(size[:, :], size[:, :], ACT.Exp, scale=-1.0).then_inc(act_done, 1)
                act.wait_ge(act_done, 2)
                act.activation(size[:, :], size[:, :], ACT.Ln, bias=cst[0:N_FOX, 2:3]).then_inc(act_done, 1)

            @block.vector
            def _(dve):
                dve.memset(ones[:, :], 1.0).then_inc(dve_done, 1)
                dve.wait_ge(act_done, 1)
                dve.wait_ge(bias_in, 16)
                z = psum[0:N_FOX, 0:2, :].rearrange("p b n -> p (b n)")
                dve.tensor_scalar(low[:, :], z, bias[:, 0:1], 0.0, ALU.add, ALU.min).then_inc(dve_done, 1)
                dve.wait_ge(act_done, 3)
                dve.wait_ge(dve_done, 2)
                dve.tensor_tensor(nl[:, :], size[:, :], low[:, :], ALU.subtract).then_inc(dve_done, 1)
                dve.wait_ge(dve_done, 3)
                dve.tensor_tensor_scan(cum[:, :], ones[:, :], nl[:, :], 0.0, ALU.mult, ALU.add
                                       ).then_inc(dve_done, 1)

    cos_t = at("cos_t", [P, T], F32, T_OFF + 8192)
    sin_t = at("sin_t", [P, T], F32, T_OFF + 12288)

    def rotary_tables(tag):
        two_pi = (6.28125, 0.00193500518798828125, 3.0199159819567e-7)
        rounder = 1.5 * 2.0 ** 23
        pos_i = at(f"{tag}_posi", [P, T], I32, B_OFF)
        ang, turns, red, half = (at(f"{tag}_{n}", [P, T], F32, B_OFF + 4096 * (i + 1))
                                 for i, n in enumerate("ang turns red half".split()))
        freq = at(f"{tag}_freq", [P, 2], F32, B_OFF + 20480)
        with ExitStack() as ctx:
            loaded, step, sines = sems(ctx, tag, "loaded step sines")
            block = ctx.enter_context(nc.Block())

            @block.sync
            def _(sp):
                sp.dma_start(pos_i[:, :], positions.broadcast_to([P, T])).then_inc(loaded, 16)
                sp.dma_start(freq[:, :], consts[:, K_FREQ:K_FREQ + 2]).then_inc(loaded, 16)

            @block.vector
            def _(dve):
                n = [0]

                def then(ins):
                    n[0] += 1
                    ins.then_inc(step, 1)
                    dve.wait_ge(step, n[0])
                dve.wait_ge(loaded, 32)
                then(dve.tensor_copy(ang[:, :], pos_i[:, :]))
                then(dve.tensor_scalar(ang[:, :], ang[:, :], freq[:, 0:1], None, ALU.mult))
                then(dve.tensor_scalar(turns[:, :], ang[:, :], 1.0 / (2 * np.pi), rounder, ALU.mult, ALU.add))
                then(dve.tensor_scalar(turns[:, :], turns[:, :], -rounder, None, ALU.add))
                then(dve.scalar_tensor_tensor(red[:, :], turns[:, :], -two_pi[0], ang[:, :], ALU.mult, ALU.add))
                then(dve.scalar_tensor_tensor(red[:, :], turns[:, :], -two_pi[1], red[:, :], ALU.mult, ALU.add))
                then(dve.scalar_tensor_tensor(red[:, :], turns[:, :], -two_pi[2], red[:, :], ALU.mult, ALU.add))
                then(dve.tensor_scalar(red[:, :], red[:, :], 3.141592, -3.141592, ALU.min, ALU.max))
                dve.wait_ge(sines, 2)
                then(dve.tensor_scalar(sin_t[:, :], sin_t[:, :], freq[:, 1:2], None, ALU.mult))
                then(dve.tensor_tensor(half[:, :], half[:, :], half[:, :], ALU.mult))
                then(dve.tensor_scalar(cos_t[:, :], half[:, :], -2.0, 1.0, ALU.mult, ALU.add))

            @block.scalar
            def _(act):
                act.wait_ge(step, 8)
                act.activation(sin_t[:, :], red[:, :], ACT.Sin).then_inc(sines, 1)
                act.activation(half[:, :], red[:, :], ACT.Sin, scale=0.5).then_inc(sines, 1)

    def attention(tag, w_in, width, n_pairs, fox):
        def b(n, name, shape=(P, T)):
            return at(f"{tag}_{name}", list(shape), F32, B_OFF + 32768 + 4096 * n)
        q = [b(0, "q0"), b(1, "q1")]
        k = [b(2, "k0"), b(3, "k1")]
        v = [b(4, "v0", (P, TT, P)), b(5, "v1", (P, TT, P))]
        stage = b(6, "stage")
        logit = [b(7, "logit0"), b(8, "logit1")]
        prob = [b(9, "prob0"), b(10, "prob1")]
        extra = b(11, "extra", (P, 2, T))
        o_sb = b(13, "o", (P, TT, P))
        probt = [at(f"{tag}_probt{n}", [P, T], F32, T_OFF + 4096 * n) for n in range(2)]
        swap = at(f"{tag}_swap", [P, T], F32, T_OFF + 16384)
        raw = at(f"{tag}_raw", [P, KT, P], F32, W_OFF)
        whi = [at(f"{tag}_whi{j}", [P, KT, P], F32R, W_OFF + 4096 + 4096 * j) for j in range(3)]
        wlo = [at(f"{tag}_wlo{j}", [P, KT, P], F32R, W_OFF + 16384 + 4096 * j) for j in range(3)]
        zero = at(f"{tag}_zero", [P, 8], F32, C_OFF + 2560)
        mask_b = at(f"{tag}_maskb", [P, P], BF16, C_OFF + 2688)
        ident_b = at(f"{tag}_identb", [P, P], BF16, C_OFF + 2944)
        mask_f = at(f"{tag}_maskf", [P, P], F32, C_OFF + 3520)
        small = at(f"{tag}_small", [P, 3, 16], F32, C_OFF + 3200)
        carrier = at(f"{tag}_carrier", [P, 16], F32, C_OFF + 3424)
        shift, den, rden = small[:, 0, :], small[:, 1, :], small[:, 2, :]
        wv = w_in.rearrange("(k p) n -> p k n", p=P)
        units = 2 * TT
        PROJ, OUT = 6, 7
        share = (3, 3, 2, 4, 4, 3, 3, 2, 4, 4, 3, 3, 2, 3, 3, 2)
        done_by = [sum(share[:u]) for u in range(units + 1)]
        ends = {u: done_by[u + 1] // KT - 1 for u in range(units) if done_by[u + 1] % KT == 0}
        rotations = {6: ("a", 0), 8: ("b", 0), 11: ("a", 1), 12: ("b", 1)}
        assert done_by[units] == 6 * KT
        q_scale = ATT_SCALE if fox else 1.0
        with ExitStack() as ctx:
            (zeroed, raw_in, split_hi, w_full, proj, proj_read, v_turn, v_new,
             s_full, biased, probs, counted, turned, turned_read, o_full, o_ready, o_turn, y_ready,
             recips, mask_in, mask_ready, swapped, rot1, rot2, rot3, rot_zero) = sems(
                ctx, tag, "zeroed raw_in split_hi w_full proj proj_read v_turn v_new "
                "s_full biased probs counted turned turned_read o_full o_ready o_turn "
                "y_ready recips mask_in mask_ready swapped rot1 rot2 rot3 rot_zero")
            gate_in = sems(ctx, tag, "gate0 gate1")
            block = ctx.enter_context(nc.Block())

            def for_pairs(engine, pair_step):
                with engine.Fori(0, n_pairs // 2 - 1) as c:
                    pair_step(c * 2, 0, c * 2 + 1)
                    pair_step(c * 2 + 1, 1, c * 2 + 2)
                pair_step(n_pairs - 2, 0, n_pairs - 1)
                pair_step(n_pairs - 1, 1, None)

            def first(pair, u=0):
                return isinstance(pair, int) and pair == 0 and u == 0

            @block.sync
            def _(sp):
                def weights(pair):
                    for t in range(3):
                        col = sp.snap(pair * P + t * width)
                        sp.compute_val(col * 4)
                        sp.wait_ge(w_full, pair * 3 + t)
                        sp.dma_start(raw[:, :, :], wv[:, :, ds(col, P)]).then_inc(raw_in, 16)

                def gates(pair, e):
                    row = sp.snap(pair * 2 + e)
                    if not first(pair):
                        sp.wait_ge(biased, pair * units + (8 * e - 8))
                    sp.dma_start(extra[:, e, :], negc_dram[ds(row, 1), :].broadcast_to([P, T])
                                 ).then_inc(gate_in[e], 16)

                weights(0)
                if fox:
                    gates(0, 0)
                    gates(0, 1)
                    sp.dma_start(mask_f[:, :], consts[:, K_CAUS:K_CAUS + P]).then_inc(mask_in, 16)
                else:
                    sp.dma_start(extra[:, :, :], dil).then_inc(mask_in, 16)
                weights(1)
                with sp.Fori(1, n_pairs - 1) as pair:
                    if fox:
                        gates(pair, 0)
                    weights(pair + 1)
                    if fox:
                        gates(pair, 1)
                if fox:
                    for e in range(2):
                        gates(n_pairs - 1, e)

            @block.gpsimd
            def _(pool):
                def split(pair, t):
                    pool.wait_ge(raw_in, (pair * 3 + t + 1) * 16)
                    split_weights(pool, raw[:, :, :], whi[t][:, :, :], wlo[t][:, :, :], zero,
                                  split_hi, pair * 3 + t + 1, w_full)
                pool.memset(zero[:, :], 0.0).then_inc(zeroed, 1)
                pool.wait_ge(zeroed, 1)
                for t in range(3):
                    split(0, t)
                with pool.Fori(1, n_pairs) as pair:
                    for t in range(3):
                        pool.wait_ge(proj, pair * 6 + (2 * t - 4))
                        split(pair, t)

            @block.tensor
            def _(pe):
                def fill(pair, lo, hi):
                    for step in range(lo, hi):
                        f, ch = step // KT, step % KT
                        t, h = f // 2, f % 2
                        if ch == 0:
                            if not h:
                                pe.wait_ge(w_full, pair * 3 + t + 1)
                            if not first(pair, f):
                                pe.wait_ge(proj_read, pair * 6 + f)
                            if f == 0 and not first(pair):
                                pe.wait_ge(y_ready, pair - 1)
                        mm = project_half(pe, psum[:, PROJ, :], whi[t], wlo[t], h_hi, h_lo, h, [ch])
                        if ch == KT - 1:
                            mm.then_inc(proj, 1)

                def turn_v(pair, before):
                    pe.wait_ge(proj_read, pair * 6 + 6)
                    if before is not None:
                        pe.wait_ge(turned_read, before * units + units)
                    for n in range(TT):
                        tr = pe.transpose(psum[:, 4 + n // 4, (n % 4) * P:(n % 4 + 1) * P],
                                          stage[:, n * P:(n + 1) * P], ident[:, :])
                    tr.then_inc(v_turn, 1)

                def scores(pair, par, u):
                    e, qt = u // TT, u % TT
                    if u == 0:
                        if fox:
                            pe.wait_ge(proj_read, pair * 6 + 4)
                        else:
                            pe.wait_ge(rot3, pair * 2 + 2)
                    if u >= 2 or not first(pair):
                        pe.wait_ge(biased, pair * units + (u - 1))
                    nk = (qt + 1) * P
                    rows = slice(e * HD, (e + 1) * HD)
                    for c in range(0, nk, HALF):
                        n = min(HALF, nk - c)
                        diag = fox and c + n == nk
                        mm = pe.matmul(psum[:, 2 * (u % 2) + c // HALF, 0:n], q[par][rows, qt * P:(qt + 1) * P],
                                       k[par][rows, c:c + n], start=True, stop=not diag)
                    if fox:
                        mm = pe.matmul(psum[:, 2 * (u % 2) + c // HALF, n - P:n], ident_b[:, :], mask_b[:, :],
                                       start=False, stop=True)
                    mm.then_inc(s_full, 1)

                def turn(pair, u):
                    pe.wait_ge(probs if fox else counted, pair * units + (u + 1))
                    pe.wait_ge(turned_read, pair * units + u)
                    if u == 0:
                        pe.wait_ge(v_new, pair + 1)
                    for n in range(u % TT + 1):
                        tr = pe.transpose(psum[:, 4 + n // 4, (n % 4) * P:(n % 4 + 1) * P],
                                          prob[u % 2][:, n * P:(n + 1) * P], ident[:, :])
                    tr.then_inc(turned, 1)

                def weigh(pair, par, u):
                    e, qt = u // TT, u % TT
                    pe.wait_ge(turned_read, pair * units + (u + 1))
                    pe.wait_ge(o_ready, pair * units + u)
                    if u == 0:
                        pe.wait_ge(y_ready, pair)
                    for n in range(qt + 1):
                        mm = pe.matmul(psum[:, OUT, 0:HD], probt[u % 2][:, n * P:(n + 1) * P],
                                       v[par][:, n, e * HD:(e + 1) * HD], start=(n == 0), stop=(n == qt))
                    mm.then_inc(o_full, 1)

                def pair_step(pair, par, following):
                    for u in range(units):
                        if u + 2 < units:
                            scores(pair, par, u + 2)
                        elif following is not None:
                            scores(following, 1 - par, u + 2 - units)
                        middle = done_by[u] + (share[u] + 1) // 2
                        if following is not None and u < units - 1:
                            fill(following, done_by[u], middle)
                        turn(pair, u)
                        if following is not None:
                            fill(following, middle if u < units - 1 else done_by[u], done_by[u + 1])
                        if u:
                            weigh(pair, par, u - 1)
                    weigh(pair, par, units - 1)
                    if following is not None:
                        turn_v(following, pair)
                    pe.wait_ge(o_ready, pair * units + units)
                    if following is not None:
                        pe.wait_ge(proj_read, following * 6 + 6)
                    for n in range(TT):
                        tr = pe.transpose(psum[:, PROJ + n // 4, (n % 4) * P:(n % 4 + 1) * P],
                                          o_sb[:, n, :], ident[:, :])
                    tr.then_inc(o_turn, 1)

                fill(0, 0, 4 * KT)
                if fox:
                    pe.wait_ge(mask_ready, 2)
                scores(0, 0, 0)
                scores(0, 0, 1)
                fill(0, 4 * KT, 6 * KT)
                turn_v(0, None)
                for_pairs(pe, pair_step)

            @block.scalar
            def _(act):
                def take(pair, par, f):
                    t, h = f // 2, f % 2
                    cols = slice(h * HALF, (h + 1) * HALF)
                    act.wait_ge(proj, pair * 6 + (f + 1))
                    dst = stage
                    if fox and t < 2:
                        dst = (q, k)[t][par]
                        if f == 0 and not first(pair):
                            act.wait_ge(s_full, (pair - 1) * units)
                    elif h == 0 and (fox or t == 0):
                        act.wait_ge(v_turn, pair)
                    elif h == 0:
                        act.wait_ge(rot1, pair * 2 + t)
                        act.wait_ge(swapped, pair * 128 + 64 * t)
                    act.activation(dst[:, cols], psum[:, PROJ, :], ACT.Copy,
                                   scale=(q_scale if t == 0 else 1.0)).then_inc(proj_read, 1)
                    if not fox and t < 2 and h:
                        act.wait_ge(proj_read, pair * 6 + (f + 1))
                        act.wait_ge(rot3, pair * 2 + t)
                        for to, of in ((0, 8), (8, 0), (64, 72), (72, 64)):
                            act.dma_start(swap[to:to + 8, :], stage[of:of + 8, :]).then_inc(swapped, 16)

                def take_v(pair, par):
                    act.wait_ge(v_turn, pair + 1)
                    if not first(pair):
                        act.wait_ge(o_full, (pair - 1) * units)
                    act.activation(v[par][:, :, :].rearrange("p n c -> p (n c)"),
                                   psum[:, 4:6, :].rearrange("p b n -> p (b n)"), ACT.Copy).then_inc(v_new, 1)

                def exp(pair, u):
                    nk = (u % TT + 1) * P
                    act.wait_ge(biased, pair * units + (u + 1))
                    if u >= 2:
                        act.wait_ge(turned, pair * units + (u - 1))
                        act.wait_ge(o_ready, pair * units + (u - 2))
                    elif not first(pair):
                        act.wait_ge(turned, pair * units - 1)
                        act.wait_ge(o_ready, pair * units - 2)
                    act.activation(prob[u % 2][:, 0:nk], logit[u % 2][:, 0:nk], ACT.Exp, scale=-1.0,
                                   bias=shift[:, u:u + 1],
                                   **({"accum_out": den[:, u:u + 1]} if fox else {})).then_inc(probs, 1)

                def pair_step(pair, par, following):
                    for u in range(units):
                        if following is not None and u - 1 in ends:
                            take(following, 1 - par, ends[u - 1])
                        if u == 0:
                            nk = 2 * P
                            act.wait_ge(biased, pair * units + 2)
                            act.wait_ge(turned, pair * units)
                            act.wait_ge(o_ready, pair * units)
                            act.activation(prob[1][:, 0:nk], logit[1][:, 0:nk], ACT.Exp, scale=-1.0,
                                           bias=shift[:, 1:2],
                                           **({"accum_out": den[:, 1:2]} if fox else {})).then_inc(probs, 1)
                        elif u + 1 < units:
                            exp(pair, u + 1)
                        elif following is not None:
                            exp(following, 0)
                        act.wait_ge(turned, pair * units + (u + 1))
                        act.wait_ge(o_full, pair * units + max(u - 1, 0))
                        nk = (u % TT + 1) * P
                        act.activation(probt[u % 2][:, 0:nk],
                                       psum[:, 4:6, :].rearrange("p b n -> p (b n)")[:, 0:nk],
                                       ACT.Copy).then_inc(turned_read, 1)
                    if following is not None:
                        take(following, 1 - par, 5)
                        take_v(following, 1 - par)
                    act.wait_ge(o_turn, pair + 1)
                    act.activation(y_buf[:, pair, :], psum[:, PROJ:PROJ + 2, :].rearrange("p b n -> p (b n)"),
                                   ACT.Copy).then_inc(y_ready, 1)

                if fox:
                    act.wait_ge(mask_in, 16)
                    act.activation(mask_b[:, :], mask_f[:, :], ACT.Copy).then_inc(mask_ready, 1)
                    act.activation(ident_b[:, :], ident[:, :], ACT.Copy).then_inc(mask_ready, 1)
                else:
                    act.wait_ge(rot_zero, 1)
                for f in range(6):
                    take(0, 0, f)
                exp(0, 0)
                take_v(0, 0)
                for_pairs(act, pair_step)

            @block.vector
            def _(dve):
                def rotate_a(pair, par, t):
                    dve.wait_ge(proj_read, pair * 6 + (2 * t + 2))
                    if not first(pair):
                        dve.wait_ge(s_full, (pair - 1) * units)
                    dst = (q, k)[t][par]
                    dve.tensor_tensor(dst[:, :], stage[:, :], cos_t[:, :], ALU.mult).then_inc(rot1, 1)

                def rotate_b(pair, par, t):
                    dst = (q, k)[t][par]
                    dve.wait_ge(swapped, pair * 128 + 64 * (t + 1))
                    dve.tensor_tensor(swap[:, :], swap[:, :], sin_t[:, :], ALU.mult).then_inc(rot2, 1)
                    dve.wait_ge(rot2, pair * 2 + t + 1)
                    dve.wait_ge(rot1, pair * 2 + t + 1)
                    dve.tensor_tensor(dst[:, :], dst[:, :], swap[:, :], ALU.add).then_inc(rot3, 1)

                def bias(pair, u):
                    e, qt = u // TT, u % TT
                    nk = (qt + 1) * P
                    dve.wait_ge(s_full, pair * units + (u + 1))
                    if u >= 1:
                        dve.wait_ge(probs, pair * units + (u - 1))
                    elif not first(pair):
                        dve.wait_ge(probs, pair * units - 1)
                    if fox and qt == 0:
                        dve.wait_ge(gate_in[e], pair * 16 + 16)
                    if u == 0:
                        dve.wait_ge(mask_in, 16)
                    dve.memset(carrier[:, u:u + 1], 0.0)
                    more = extra[:, e, 0:nk] if fox else extra[:, 0, (TT - 1 - qt) * P:T]
                    s = psum[:, 2 * (u % 2):2 * (u % 2) + 2, :].rearrange("p b n -> p (b n)")[:, 0:nk]
                    dve.tensor_tensor_reduce(out=logit[u % 2][:, 0:nk], in0=s, in1=more,
                                             scale=(-1.0 if fox else -ATT_SCALE), scalar=3.0e38,
                                             op0=ALU.add, op1=ALU.min,
                                             accum_out=shift[:, u:u + 1]).then_inc(biased, 1)

                def count(pair, u):
                    qt = u % TT
                    nk = (qt + 1) * P
                    dve.wait_ge(probs, pair * units + (u + 1))
                    dve.tensor_tensor_reduce(out=prob[u % 2][:, 0:nk], in0=prob[u % 2][:, 0:nk],
                                             in1=extra[:, 1, (TT - 1 - qt) * P:T], scale=1.0, scalar=0.0,
                                             op0=ALU.mult, op1=ALU.add,
                                             accum_out=den[:, u:u + 1]).then_inc(counted, 1)

                def norm_out(pair, u):
                    e, qt = u // TT, u % TT
                    dve.wait_ge(probs if fox else counted, pair * units + (u + 1))
                    dve.reciprocal(rden[:, u:u + 1], den[:, u:u + 1]).then_inc(recips, 1)
                    dve.wait_ge(recips, pair * units + (u + 1))
                    if u == 0:
                        dve.wait_ge(o_turn, pair)
                    dve.wait_ge(o_full, pair * units + (u + 1))
                    dve.tensor_scalar(o_sb[:, qt, e * HD:(e + 1) * HD], psum[:, OUT, 0:HD],
                                      rden[:, u:u + 1], None, ALU.mult).then_inc(o_ready, 1)

                def pair_step(pair, par, following):
                    for u in range(units):
                        if not fox:
                            count(pair, u)
                        if u + 1 < units:
                            bias(pair, u + 1)
                        elif following is not None:
                            bias(following, 0)
                        if u:
                            norm_out(pair, u - 1)
                        if not fox and following is not None and u in rotations:
                            part, t = rotations[u]
                            (rotate_a if part == "a" else rotate_b)(following, 1 - par, t)
                    norm_out(pair, units - 1)

                if not fox:
                    dve.wait_ge(mask_in, 16)
                    dve.memset(swap[:, :], 0.0).then_inc(rot_zero, 1)
                    for t in range(2):
                        rotate_a(0, 0, t)
                        rotate_b(0, 0, t)
                bias(0, 0)
                for_pairs(dve, pair_step)
    z_buf = at("z_buf", [P, RWKV_IN // P, T], F32, B_OFF + 32768)
    Z_R, Z_K, Z_V, Z_LO, Z_G = 0, RW_T, 2 * RW_T, 3 * RW_T, 3 * RW_T + 1
    cum_buf = at("cum_buf", [P, RW_T, T], F32, A_OFF)
    nkk_buf = at("nkk_buf", [P, RW_T, T], F32, A_OFF + 16384)
    bb_buf = at("bb_buf", [P, RW_T, T], F32, A_OFF + 32768)

    def rwkv_project(tag):
        n_pairs = RWKV_IN // P // 2
        raw = [at(f"{tag}_raw{j}", [P, KT, P], F32, W_OFF + 4096 * j) for j in range(2)]
        whi = [at(f"{tag}_whi{j}", [P, KT, P], F32R, W_OFF + 8192 + 4096 * j) for j in range(2)]
        wlo = [at(f"{tag}_wlo{j}", [P, KT, P], F32R, W_OFF + 16384 + 4096 * j) for j in range(2)]
        zero = at(f"{tag}_zero", [P, 8], F32, W_OFF + 24576)
        z = [at(f"{tag}_z{j}", [P, T + 1], F32, T_OFF + 4128 * j) for j in range(2)]
        diff = [at(f"{tag}_diff{j}", [P, T], F32, T_OFF + 8256 + 4096 * j) for j in range(2)]
        w = w_in0.rearrange("(k p) n -> p k n", p=P)
        with ExitStack() as ctx:
            zeroed, pads, split_hi = sems(ctx, tag, "zeroed pads split_hi")
            raw_in = sems(ctx, tag, "raw0 raw1")
            w_full = sems(ctx, tag, "wfull0 wfull1")
            ps_full = sems(ctx, tag, "psfull0 psfull1")
            evac = sems(ctx, tag, "evac0 evac1")
            diffed = sems(ctx, tag, "diffed0 diffed1")
            mixed = sems(ctx, tag, "mixed0 mixed1")
            block = ctx.enter_context(nc.Block())

            @block.sync
            def _(sp):
                with sp.Fori(0, n_pairs) as c:
                    for j in range(2):
                        col = sp.snap(c * (2 * P) + (j * P + FOX_IN))
                        sp.compute_val(col * 4)
                        sp.wait_ge(w_full[j], c)
                        sp.dma_start(raw[j][:, :, :], w[:, :, ds(col, P)]).then_inc(raw_in[j], 16)

            @block.gpsimd
            def _(pool):
                pool.memset(zero[:, :], 0.0).then_inc(zeroed, 1)
                pool.wait_ge(zeroed, 1)
                with pool.Fori(0, n_pairs) as c:
                    for j in range(2):
                        pool.wait_ge(ps_full[j], c * 2)
                        pool.wait_ge(raw_in[j], c * 16 + 16)
                        split_weights(pool, raw[j][:, :, :], whi[j][:, :, :], wlo[j][:, :, :], zero,
                                      split_hi, c * 2 + j + 1, w_full[j])

            @block.tensor
            def _(pe):
                with pe.Fori(0, n_pairs) as c:
                    for j in range(2):
                        for h in range(2):
                            pe.wait_ge(evac[j], c * 2)
                            pe.wait_ge(w_full[j], c + 1)
                            project_half(pe, psum[:, 2 * j + h, :], whi[j], wlo[j], h_hi, h_lo, h
                                         ).then_inc(ps_full[j], 1)

            @block.scalar
            def _(act):
                with act.Fori(0, n_pairs) as c:
                    for j in range(2):
                        act.wait_ge(mixed[j], c)
                        for h in range(2):
                            act.wait_ge(ps_full[j], c * 2 + h + 1)
                            act.activation(z[j][:, 1 + h * HALF:1 + (h + 1) * HALF], psum[:, 2 * j + h, :],
                                           ACT.Copy).then_inc(evac[j], 1)

            @block.vector
            def _(dve):
                for j in range(2):
                    dve.memset(z[j][:, 0:1], 0.0).then_inc(pads, 1)
                dve.wait_ge(pads, 2)
                with dve.Fori(0, n_pairs) as c:
                    for j in range(2):
                        dve.wait_ge(evac[j], c * 2 + 2)
                        dve.tensor_tensor(diff[j][:, :], z[j][:, 0:T], z[j][:, 1:T + 1],
                                          ALU.subtract).then_inc(diffed[j], 1)
                        dve.wait_ge(diffed[j], c + 1)
                        dve.scalar_tensor_tensor(z_buf[:, c * 2 + j, :], diff[j][:, :],
                                                 vec[:, ds(c * 2 + (j + V_MU), 1)], z[j][:, 1:T + 1],
                                                 ALU.mult, ALU.add).then_inc(mixed[j], 1)

    def rwkv_prepare(tag):
        lora = at(f"{tag}_lora", [P, RWKV_W], F32, W_OFF)
        blk = at(f"{tag}_blk", [P, P], F32, W_OFF + 2048)
        reset = at(f"{tag}_reset", [P, HALF], F32, W_OFF + 2560)
        neg = at(f"{tag}_neg", [P, 2, RW_T], F32, W_OFF + 4608)
        sq, sig, iclr, norm_, rnorm, fac = ([at(f"{tag}_{n}{s}", [P, HALF], F32, T_OFF - 20480 + 4096 * i + 2048 * s)
                                             for s in range(2)] for i, n in enumerate(
            "sq sig iclr norm rnorm fac".split()))
        blocks = 2 * RW_T
        with ExitStack() as ctx:
            (loaded, loras, squared, lora_ps, sum_ps, sigs, iclrs, floors, roots, recips, scans,
             nkks, bbs, facs, ks, negs) = sems(
                ctx, tag, "loaded loras squared lora_ps sum_ps sigs iclrs floors roots recips scans "
                "nkks bbs facs ks negs")
            block = ctx.enter_context(nc.Block())

            @block.sync
            def _(sp):
                sp.dma_start(lora[0:64, :], w2).then_inc(loaded, 16)
                sp.dma_start(lora[64:128, :], a2).then_inc(loaded, 16)
                sp.dma_start(blk[:, :], consts[:, K_BLK:K_BLK + P]).then_inc(loaded, 16)
                sp.dma_start(reset[:, :], consts[:, K_RESET:K_RESET + HALF]).then_inc(loaded, 16)

            def place(n):
                ct, h = n // 2, n % 2
                return ct, slice(h * HALF, (h + 1) * HALF), n % 2

            @block.tensor
            def _(pe):
                pe.wait_ge(loaded, 64)
                pe.wait_ge(loras, 1)
                for n in range(blocks):
                    ct, cols, s = place(n)
                    if n >= 2:
                        pe.wait_ge(sigs, n - 1)
                        pe.wait_ge(iclrs, n - 1)
                        pe.wait_ge(floors, n - 1)
                    pe.matmul(psum[:, s, :], lora[0:64, ct * P:(ct + 1) * P], z_buf[0:64, Z_LO, cols],
                              start=True, stop=True)
                    pe.matmul(psum[:, 2 + s, :], lora[64:128, ct * P:(ct + 1) * P], z_buf[64:128, Z_LO, cols],
                              start=True, stop=True).then_inc(lora_ps, 1)
                    pe.wait_ge(squared, n + 1)
                    pe.matmul(psum[:, 4 + s, :], blk[:, :], sq[s][:, :], start=True, stop=True).then_inc(sum_ps, 1)

            @block.scalar
            def _(act):
                act.activation(z_buf[0:64, Z_LO, :], z_buf[0:64, Z_LO, :], ACT.Tanh).then_inc(loras, 1)
                act.activation(z_buf[:, Z_G, :], z_buf[:, Z_G, :], ACT.Sigmoid)
                for n in range(blocks):
                    ct, cols, s = place(n)
                    if n >= 2:
                        act.wait_ge(sum_ps, n - 1)
                        act.wait_ge(scans, n - 1)
                        act.wait_ge(facs, n - 1)
                        act.wait_ge(bbs, n - 1)
                    act.activation(sq[s][:, :], z_buf[:, Z_K + ct, cols], ACT.Square,
                                   scale=vec[:, V_KK + ct:V_KK + ct + 1]).then_inc(squared, 1)
                    act.wait_ge(lora_ps, n + 1)
                    act.activation(sig[s][:, :], psum[:, s, :], ACT.Sigmoid,
                                   bias=vec[:, V_W0 + ct:V_W0 + ct + 1]).then_inc(sigs, 1)
                    act.activation(iclr[s][:, :], psum[:, 2 + s, :], ACT.Sigmoid,
                                   bias=vec[:, V_A0 + ct:V_A0 + ct + 1]).then_inc(iclrs, 1)
                    act.wait_ge(floors, n + 1)
                    act.activation(norm_[s][:, :], norm_[s][:, :], ACT.Sqrt).then_inc(roots, 1)

            @block.vector
            def _(dve):
                dve.tensor_scalar(neg[:, 0, :], vec[:, V_KK:V_KK + RW_T], -1.0, None, ALU.mult).then_inc(negs, 1)
                dve.tensor_scalar(neg[:, 1, :], vec[:, V_KA:V_KA + RW_T], -1.0, 1.0, ALU.mult, ALU.add
                                  ).then_inc(negs, 1)
                dve.wait_ge(negs, 2)
                dve.wait_ge(loaded, 64)
                for n in range(blocks):
                    ct, cols, s = place(n)
                    dve.wait_ge(sum_ps, n + 1)
                    if n >= 2:
                        dve.wait_ge(recips, n - 1)
                    dve.tensor_scalar(norm_[s][:, :], psum[:, 4 + s, :], 1e-24, None, ALU.max).then_inc(floors, 1)
                    dve.wait_ge(sigs, n + 1)
                    dve.tensor_tensor_scan(cum_buf[:, ct, cols], reset[:, :], sig[s][:, :], 0.0,
                                           ALU.mult, ALU.add).then_inc(scans, 1)
                    dve.wait_ge(iclrs, n + 1)
                    dve.tensor_scalar(fac[s][:, :], iclr[s][:, :], vec[:, V_KA + ct:V_KA + ct + 1],
                                      neg[:, 1, ct:ct + 1], ALU.mult, ALU.add).then_inc(facs, 1)
                    dve.wait_ge(roots, n + 1)
                    dve.reciprocal(rnorm[s][:, :], norm_[s][:, :]).then_inc(recips, 1)
                    dve.wait_ge(recips, n + 1)
                    dve.scalar_tensor_tensor(nkk_buf[:, ct, cols], z_buf[:, Z_K + ct, cols], neg[:, 0, ct:ct + 1],
                                             rnorm[s][:, :], ALU.mult, ALU.mult).then_inc(nkks, 1)
                    dve.wait_ge(nkks, n + 1)
                    dve.scalar_tensor_tensor(bb_buf[:, ct, cols], nkk_buf[:, ct, cols], -1.0, iclr[s][:, :],
                                             ALU.mult, ALU.mult).then_inc(bbs, 1)
                    dve.wait_ge(facs, n + 1)
                    dve.wait_ge(squared, n + 1)
                    dve.tensor_tensor(z_buf[:, Z_K + ct, cols], z_buf[:, Z_K + ct, cols], fac[s][:, :],
                                      ALU.mult).then_inc(ks, 1)

    def rwkv_chunks(tag):
        regions = [[W_OFF, C_OFF], [A_OFF + 49152, B_OFF], [B_OFF + 16384, B_OFF + 32768],
                   [C_OFF + 2432, C_OFF + 7928]]

        def buf(name, shape, nbytes, copies=0, dt=F32):
            if copies:
                return [buf(f"{name}{n}", shape, nbytes) for n in range(copies)]
            for region in regions:
                if region[0] + nbytes <= region[1]:
                    t = at(f"{tag}_{name}", shape, dt, region[0])
                    region[0] += nbytes
                    return t
            raise ValueError(f"no room for {name}: {regions}")
        mx = buf("mx", [P, 2, 2, 4 * P], 8192, 2)
        tok = buf("tok", [P, 4, RWKV_W], 8192, 2)
        ar = buf("ar", [P, RW_T, 2, P], 4096, 2)
        xs = buf("x", [P, 2, 2, 2 * P], 4096)
        mask_lev = buf("mlev", [P, 5, P], 2560)
        e_in = buf("ein", [P, RW_T, 2, CHUNK + 1], 2112, 2)
        e_neg = buf("eneg", [P, RW_T, P], 2048)
        bt = buf("bt", [P, RW_T, P], 2048, 2)
        kt = buf("kt", [P, RW_T, P], 2048, 2)
        kh = buf("kh", [P, RW_T, P], 2048)
        vt = buf("vt", [P, RW_T, P], 2048)
        lsb = buf("l", [P, 2, 2, P], 2048)
        zt = buf("zt", [P, 2, 2, P], 2048)
        pq = buf("pq", [P, 2, 2, P], 2048)
        mt = buf("mt", [P, 2, 2, P], 2048)
        st = buf("st", [P, RW_T, 2, HD], 2048)
        ysb = buf("y", [P, N_RWKV, HD], 2048)
        sqn = buf("sqn", [P, N_RWKV, HD], 2048)
        akv = buf("akv", [P, 2, 2, HD], 1024)
        gt = buf("gt", [P, 2, P], 1024)
        mask_ab = buf("mab", [P, 2 * P], 1024)
        mask_1 = buf("m1", [P, 2 * P], 1024)
        mask_l = buf("ml", [P, P], 512)
        id64 = buf("id64", [P, HD], 256)
        ident_b = buf("identb", [P, 2 * P], 512, dt=BF16)
        stat = buf("stat", [P, 3, N_RWKV], 96)
        carrier = buf("carrier", [P, 4], 16)
        bh = e_neg
        with ExitStack() as ctx:
            (consts_in, zeroed, exp_in, exp_neg, v_copied, prepared, hats, t_turned, toks,
             ab, mxs, ls, ones_in, x0a, x0, akv_ps, akv_sb, z_ps, zts, xx_ps, x_new, pq_ps, pqs, mn0_ps, mn_ps, gts, mts,
             y0_ps, ms0_ps, ms1_ps, st1s, st0s, ys, sums, centred, squares, varis, roots, rrs, normed,
             y_turned, y_out) = sems(
                ctx, tag, "consts_in zeroed exp_in exp_neg v_copied prepared hats t_turned toks "
                "ab mxs ls ones_in x0a x0 akv_ps akv_sb z_ps zts xx_ps x_new pq_ps pqs mn0_ps mn_ps gts mts "
                "y0_ps ms0_ps ms1_ps st1s st0s ys sums centred squares varis roots rrs normed "
                "y_turned y_out")
            block = ctx.enter_context(nc.Block())
            per_e = [slice(0, HD), slice(HD, P)]
            halves = "p (e t) -> p e t"

            def for_groups(engine, step):
                for g in range(2):
                    step(g, g, 0, 0, first=True)
                with engine.Fori(0, TT // 2 - 1) as c:
                    for m in range(4):
                        step(c * 4 + (2 + m), m % 2, c * 2 + (1 + m // 2), (1 + m // 2) % 2)
                for g in range(2):
                    step(2 * TT - 2 + g, g, TT - 1, (TT - 1) % 2, last=True)

            @block.sync
            def _(sp):
                for dst, col, n in ((mask_ab, K_AB, 2 * P), (mask_l, K_L, P), (mask_1, K_M1, 2 * P),
                                    (id64, K_ID64, HD)):
                    sp.dma_start(dst[:, :], consts[:, col:col + n]).then_inc(consts_in, 16)
                sp.dma_start(mask_lev[:, :, :], consts[:, K_LEV:K_LEV + 5 * P].rearrange("p (l n) -> p l n", l=5)
                             ).then_inc(consts_in, 16)

            @block.scalar
            def _(act):
                def wait_here(n):
                    act.activation(carrier[:, n:n + 1], cst[:, 1:2], ACT.Copy)

                def prepare(i, slot):
                    cols = ds(i * P, P)
                    if not isinstance(i, int) or i:
                        act.wait_ge(mts, i * 4 - 4)
                        act.wait_ge(prepared, i * 4)
                        act.wait_ge(t_turned, i * 4)
                    wait_here(0)
                    src = cum_buf[:, :, cols].rearrange("p c (j t) -> p c j t", j=2)
                    act.activation(e_in[slot][:, :, :, 1:CHUNK + 1], src, ACT.Exp, scale=-DECAY).then_inc(exp_in, 1)
                    act.activation(e_neg[:, :, :], cum_buf[:, :, cols], ACT.Exp, scale=DECAY).then_inc(exp_neg, 1)
                    act.activation(vt[:, :, :], z_buf[:, Z_V:Z_V + RW_T, cols], ACT.Copy).then_inc(v_copied, 1)

                def take_tok(i, slot, m):
                    act.wait_ge(t_turned, i * 4 + (m + 1))
                    act.activation(tok[slot][:, m, :], psum[:, m % 2, :], ACT.Copy).then_inc(toks, 1)

                def take_pq(G):
                    for s in range(2):
                        act.wait_ge(pq_ps, G * 2 + (s + 1))
                        act.activation(pq[:, s, :, :], psum[:, 2 + s, 0:2 * P].rearrange(halves, e=2),
                                       ACT.Copy).then_inc(pqs, 1)

                def take_y(G, g):
                    for s in range(2):
                        act.wait_ge(st0s, G * 2 + (s + 1))
                        act.activation(ysb[:, 4 * g + 2 * s:4 * g + 2 * s + 2, :],
                                       psum[:, 2 + s, 3 * P:4 * P].rearrange(halves, e=2), ACT.Copy
                                       ).then_inc(ys, 1)

                def norm_squares(i):
                    act.wait_ge(centred, i + 1)
                    act.wait_ge(y_turned, i)
                    act.activation(sqn[:, :, :], ysb[:, :, :], ACT.Square).then_inc(squares, 1)

                def norm_root(i):
                    act.wait_ge(varis, i + 1)
                    act.activation(stat[:, 2, :], stat[:, 1, :], ACT.Sqrt, scale=1.0 / HD, bias=cst[:, 1:2]
                                   ).then_inc(roots, 1)

                def take_out(i):
                    act.wait_ge(y_turned, i + 1)
                    wait_here(1)
                    act.activation(cum_buf[:, :, ds(i * P, P)], psum[:, 2, :].rearrange("p (c t) -> p c t", c=RW_T),
                                   ACT.Copy).then_inc(y_out, 1)

                def step(G, g, i, slot, first=False, last=False):
                    tail = not (first and g == 0)
                    norms = g == 1 and not first
                    prepares = g == 1 and not last
                    if tail:
                        take_pq(G - 1)
                    for lev in range(5):
                        for s in range(2):
                            act.wait_ge(xx_ps, G * 10 + (2 * lev + s + 1))
                            part = slice(0, 2 * P) if lev < 4 else slice(P, 2 * P)
                            act.activation(xs[:, s, :, part],
                                           psum[:, 5 + 2 * s, :].rearrange(halves, e=2)[:, :, part],
                                           ACT.Copy).then_inc(x_new, 1)
                        if lev == 1:
                            for s in range(2):
                                act.wait_ge(akv_ps, G * 2 + (s + 1))
                                act.activation(akv[:, s, :, :], psum[:, s, 0:P].rearrange(halves, e=2),
                                               ACT.Copy).then_inc(akv_sb, 1)
                        if prepares and lev == 0:
                            prepare(i + 1, 1 - slot)
                        if norms and lev == 0:
                            norm_squares(i - 1)
                        if norms and lev == 2:
                            norm_root(i - 1)
                        if prepares and lev == 3:
                            take_tok(i + 1, 1 - slot, 0)
                            take_tok(i + 1, 1 - slot, 1)
                    if prepares:
                        take_tok(i + 1, 1 - slot, 2)
                    if tail:
                        if norms:
                            act.wait_ge(normed, i)
                        take_y(G - 1, 1 - g)
                    if prepares:
                        take_tok(i + 1, 1 - slot, 3)
                    if norms:
                        take_out(i - 1)

                for n in range(2):
                    act.activation(ident_b[:, n * P:(n + 1) * P], ident[:, :], ACT.Copy).then_inc(ones_in, 1)
                prepare(0, 0)
                for m in range(4):
                    take_tok(0, 0, m)
                for_groups(act, step)
                take_pq(2 * TT - 1)
                take_y(2 * TT - 1, 1)
                norm_squares(TT - 1)
                norm_root(TT - 1)
                take_out(TT - 1)

            @block.gpsimd
            def _(pool):
                def split(a):
                    return a.rearrange("p c (j t) -> p c j t", j=2)

                def prepare(i, slot):
                    cols = ds(i * P, P)
                    pool.wait_ge(exp_neg, i + 1)
                    if not isinstance(i, int) or i:
                        pool.wait_ge(t_turned, i * 4)
                    pool.tensor_tensor(split(ar[slot][:, :, 0, :]), split(nkk_buf[:, :, cols]),
                                       e_in[slot][:, :, :, 0:CHUNK], ALU.mult).then_inc(prepared, 1)
                    pool.tensor_tensor(bt[slot][:, :, :], bb_buf[:, :, cols], e_neg[:, :, :], ALU.mult
                                       ).then_inc(prepared, 1)
                    pool.tensor_tensor(kt[slot][:, :, :], z_buf[:, Z_K:Z_K + RW_T, cols], e_neg[:, :, :], ALU.mult
                                       ).then_inc(prepared, 1)
                    w_end = e_in[slot][:, :, :, CHUNK:CHUNK + 1].broadcast_to([P, RW_T, 2, CHUNK])
                    for n, (dst, src) in enumerate(((bh, bt), (kh, kt))):
                        pool.wait_ge(prepared, i * 4 + 3)
                        pool.tensor_tensor(split(dst[:, :, :]), split(src[slot][:, :, :]), w_end, ALU.mult
                                           ).then_inc(hats, 1)
                    pool.tensor_tensor(split(ar[slot][:, :, 1, :]), split(z_buf[:, Z_R:Z_R + RW_T, cols]),
                                       e_in[slot][:, :, :, 1:CHUNK + 1], ALU.mult).then_inc(prepared, 1)

                def step(G, g, i, slot, first=False, last=False):
                    if g == 1 and not last:
                        prepare(i + 1, 1 - slot)

                pool.wait_ge(consts_in, 80)
                pool.wait_ge(zeroed, 4)
                prepare(0, 0)
                for_groups(pool, step)

            @block.vector
            def _(dve):
                def to_pair(mask):
                    return mask.rearrange(halves, e=1).broadcast_to([P, 2, P])

                def first_x(G, s):
                    n = G * 2 + s
                    own = psum[:, 4 + 2 * s:6 + 2 * s, 0:P]
                    dve.tensor_tensor(xs[:, s, :, 0:P], own, to_pair(mask_1[:, 0:P]), ALU.mult).then_inc(x0a, 1)
                    dve.tensor_tensor(lsb[:, s, :, :], own, to_pair(mask_l[:, :]), ALU.mult).then_inc(ls, 1)
                    dve.wait_ge(x0a, n * 2 + 2)
                    for m in (1, 0):
                        part = xs[:, s, :, m * P:(m + 1) * P]
                        dve.tensor_tensor(part, part, to_pair(ident[:, :]), ALU.add).then_inc(x0, 1)

                def first_x_t(G, s):
                    dve.wait_ge(ab, G * 2 + (s + 1))
                    if not isinstance(G, int) or G >= 1:
                        dve.wait_ge(pq_ps, G * 2 - 1 + s)
                    dve.tensor_tensor(xs[:, s, :, P:2 * P], psum[:, 0:2, 0:P], to_pair(mask_1[:, P:2 * P]),
                                      ALU.mult).then_inc(x0a, 1)

                def take_scores(G, g, s):
                    if not isinstance(G, int) or G >= 2:
                        dve.wait_ge(ms1_ps, G * 2 - 2)
                    dve.tensor_tensor(mx[g][:, s, :, :].rearrange("p e (m t) -> p (e m) t", m=2),
                                      psum[:, 0:2, :].rearrange("p e (m t) -> p (e m) t", m=2),
                                      mask_ab[:, :].rearrange(halves, e=1).broadcast_to([P, 4, 2 * P]),
                                      ALU.mult).then_inc(mxs, 1)

                def transfer(G, g, slot, s):
                    n, pr = G * 2 + s, 2 * g + s
                    dve.wait_ge(mn_ps, n + 1)
                    dve.tensor_tensor(gt[:, s, :], psum[:, 2 + s, 2 * P:3 * P], ar[slot][:, pr, 1, :], ALU.add
                                      ).then_inc(gts, 1)
                    for j in range(2):
                        for e in range(2):
                            ins = dve.scalar_tensor_tensor(
                                mt[per_e[e], s, j, per_e[e]], id64[per_e[e], :],
                                e_in[slot][per_e[e], pr, j, CHUNK:CHUNK + 1],
                                psum[per_e[e], 2 + s, j * P:j * P + HD], ALU.mult, ALU.add)
                    ins.then_inc(mts, 1)

                def state(G, g, s, j):
                    n, pr = G * 2 + s, 2 * g + s
                    dve.wait_ge((ms0_ps, ms1_ps)[j], n + 1)
                    dve.tensor_copy(st[:, pr, 1 - j, :], psum[:, 2 + s, j * P + HD:(j + 1) * P]
                                    ).then_inc((st1s, st0s)[j], 1)

                def norm_a(i):
                    dve.wait_ge(ys, i * 4 + 4)
                    dve.tensor_reduce(stat[:, 0, :], ysb[:, :, :], AX_X, ALU.add).then_inc(sums, 1)
                    dve.wait_ge(sums, i * 2 + 1)
                    dve.tensor_scalar(stat[:, 0, :], stat[:, 0, :], 1.0 / HD, None, ALU.mult).then_inc(sums, 1)
                    dve.wait_ge(sums, i * 2 + 2)
                    mean = stat[:, 0, :].rearrange("p (h o) -> p h o", o=1).broadcast_to([P, N_RWKV, HD])
                    dve.tensor_tensor(ysb[:, :, :], ysb[:, :, :], mean, ALU.subtract).then_inc(centred, 1)

                def norm_b(i):
                    dve.wait_ge(squares, i + 1)
                    dve.tensor_reduce(stat[:, 1, :], sqn[:, :, :], AX_X, ALU.add).then_inc(varis, 1)

                def norm_c(i):
                    dve.wait_ge(roots, i + 1)
                    dve.reciprocal(stat[:, 2, :], stat[:, 2, :]).then_inc(rrs, 1)
                    dve.wait_ge(rrs, i + 1)
                    rstd = stat[:, 2, :].rearrange("p (h o) -> p h o", o=1).broadcast_to([P, N_RWKV, HD])
                    dve.wait_ge(centred, i + 1)
                    dve.wait_ge(varis, i + 1)
                    dve.tensor_tensor(sqn[:, :, :], ysb[:, :, :], rstd, ALU.mult).then_inc(normed, 1)

                def step(G, g, i, slot, first=False, last=False):
                    tail = not (first and g == 0)
                    before = (G - 1, 1 - g, slot if g else 1 - slot)
                    norms = g == 1 and not first
                    first_x_t(G, 0)
                    take_scores(G, g, 0)
                    first_x(G, 0)
                    first_x_t(G, 1)
                    first_x(G, 1)
                    for lev in range(5):
                        for s in range(2):
                            dve.wait_ge(z_ps, G * 10 + (2 * lev + s + 1))
                            dve.tensor_tensor(
                                zt[:, s, :, :], psum[:, 4 + 2 * s, 0:2 * P].rearrange(halves, e=2),
                                to_pair(mask_lev[:, lev, :]), ALU.mult).then_inc(zts, 1)
                            if lev == 0 and s == 0:
                                take_scores(G, g, 1)
                                if tail:
                                    transfer(*before, 0)
                        if tail and lev == 1:
                            transfer(*before, 1)
                        if tail and lev == 2:
                            for s in range(2):
                                state(*before[:2], s, 0)
                        if tail and lev >= 3:
                            state(*before[:2], lev - 3, 1)
                        if norms:
                            if lev == 0:
                                norm_a(i - 1)
                            if lev == 1:
                                norm_b(i - 1)
                            if lev == 3:
                                norm_c(i - 1)

                for m in (st, mt):
                    dve.memset(m[:, :, :, :], 0.0).then_inc(zeroed, 1)
                for w in e_in:
                    dve.memset(w[:, :, :, 0:1], 1.0).then_inc(zeroed, 1)
                dve.wait_ge(zeroed, 4)
                dve.wait_ge(consts_in, 80)
                for_groups(dve, step)
                final = (2 * TT - 1, 1, (TT - 1) % 2)
                for s in range(2):
                    transfer(*final, s)
                for s in range(2):
                    state(*final[:2], s, 0)
                for s in range(2):
                    state(*final[:2], s, 1)
                norm_a(TT - 1)
                norm_b(TT - 1)
                norm_c(TT - 1)

            @block.tensor
            def _(pe):
                def mm(out, lhs, rhs, start=True, stop=True, **k):
                    return pe.matmul(out, lhs, rhs, start=start, stop=stop, **k)

                def turn_tok(i, slot, m):
                    src = (lambda ct: ar[slot][:, ct, 0, :], lambda ct: bh[:, ct, :],
                           lambda ct: kh[:, ct, :], lambda ct: vt[:, ct, :])[m]
                    ready, count = ((prepared, i * 4 + 1), (hats, i * 2 + 1), (hats, i * 2 + 2),
                                    (v_copied, i + 1))[m]
                    pe.wait_ge(ready, count)
                    if m >= 2:
                        pe.wait_ge(toks, i * 4 + (m - 1))
                    for ct in range(RW_T):
                        tr = pe.transpose(psum[:, m % 2, ct * P:(ct + 1) * P], src(ct), ident[:, :])
                    tr.then_inc(t_turned, 1)

                def scores(G, g, slot, s):
                    pr = 2 * g + s
                    for e in range(2):
                        rows = per_e[e]
                        both = ar[slot][rows, pr, :, :].rearrange("p m t -> p (m t)")
                        mm(psum[:, e, 0:2 * P], bt[slot][rows, pr, :], both)
                        mm(psum[:, e, 2 * P:4 * P], kt[slot][rows, pr, :], both)
                        last = mm(psum[:, 4 + 2 * s + e, 0:P], ar[slot][rows, pr, 0, :], bt[slot][rows, pr, :])
                    last.then_inc(ab, 1)

                def a_k_v(G, g, slot, s):
                    pr = 2 * g + s
                    pe.wait_ge(mxs, G * 2 + 2)
                    for e in range(2):
                        last = mm(psum[:, s, e * HD:(e + 1) * HD], mx[g][:, s, e, 2 * P:3 * P],
                                  tok[slot][:, 3, pr * P + e * HD:pr * P + (e + 1) * HD])
                    last.then_inc(akv_ps, 1)

                def solve(G, g, slot, s):
                    pr = 2 * g + s
                    pe.wait_ge(x_new, G * 10 + (8 + s + 1))
                    pe.wait_ge(akv_sb, G * 2 + (s + 1))
                    pe.wait_ge(ys, G * 2)
                    for e in range(2):
                        x_t = xs[:, s, e, P:2 * P]
                        mm(psum[:, 2 + s, e * P:e * P + HD], x_t,
                           tok[slot][:, 0, pr * P + e * HD:pr * P + (e + 1) * HD])
                        last = mm(psum[:, 2 + s, e * P + HD:(e + 1) * P], x_t, akv[:, s, e, :])
                    last.then_inc(pq_ps, 1)

                def moves(G, g, slot, s):
                    pr = 2 * g + s
                    pe.wait_ge(pqs, G * 2 + (s + 1))
                    for j in range(2):
                        if j:
                            pe.wait_ge(mn0_ps, G * 2 + (s + 1))
                        mm(psum[per_e[j], 2 + s, 2 * P:3 * P], pq[:, s, j, 0:HD], mx[g][:, s, j, P:2 * P],
                           start=(j == 0), stop=False, skip_group_check=True)
                        rows, to = per_e[j], j * P
                        for e in range(2):
                            c = slice(pr * P + e * HD, pr * P + (e + 1) * HD)
                            mm(psum[per_e[e], 2 + s, to:to + HD], pq[rows, s, e, 0:HD], tok[slot][rows, 1, c],
                               start=(j == 0 and e == 1), stop=False, skip_group_check=True)
                            mm(psum[per_e[e], 2 + s, to + HD:to + P], tok[slot][rows, 1, c], pq[rows, s, e, HD:P],
                               start=False, stop=False, skip_group_check=True)
                            last = mm(psum[per_e[e], 2 + s, to + HD:to + P], tok[slot][rows, 2, c],
                                      tok[slot][rows, 3, c], start=False, stop=False, skip_group_check=True)
                        last.then_inc((mn0_ps, mn_ps)[j], 1)

                def advance(G, g, s, j):
                    pr = 2 * g + s
                    mm(psum[:, 2 + s, j * P + HD:(j + 1) * P], mt[:, s, j, :], st[:, pr, j, :], start=False,
                       skip_group_check=True).then_inc((ms0_ps, ms1_ps)[j], 1)

                def outputs(G, g, slot, s):
                    pr = 2 * g + s
                    pe.wait_ge(gts, G * 2 + (s + 1))
                    pe.wait_ge(st1s, G * 2 + (s + 1))
                    for e in range(2):
                        if e:
                            pe.wait_ge(y0_ps, G * 2 + (s + 1))
                        out = psum[:, 2 + s, 3 * P + e * HD:3 * P + (e + 1) * HD]
                        mm(out, mx[g][:, s, e, P:2 * P], pq[:, s, e, HD:P], start=False, stop=False,
                           skip_group_check=True)
                        mm(out, mx[g][:, s, e, 3 * P:4 * P],
                           tok[slot][:, 3, pr * P + e * HD:pr * P + (e + 1) * HD],
                           start=False, stop=False, skip_group_check=True)
                        for j in range(2):
                            ins = mm(psum[per_e[j], 2 + s, 3 * P + e * HD:3 * P + (e + 1) * HD],
                                     gt[per_e[e], s, per_e[j]], st[per_e[e], pr, j, :], start=False,
                                     skip_group_check=True)
                        if e == 0:
                            ins.then_inc(y0_ps, 1)
                    advance(G, g, s, 1)

                def turn_out(i):
                    pe.wait_ge(normed, i + 1)
                    flat = sqn[:, :, :].rearrange("p h v -> p (h v)")
                    for ct in range(RW_T):
                        tr = pe.transpose(psum[:, 2, ct * P:(ct + 1) * P], flat[:, ct * P:(ct + 1) * P], ident[:, :])
                    tr.then_inc(y_turned, 1)

                def step(G, g, i, slot, first=False, last=False):
                    tail = not (first and g == 0)
                    before = (G - 1, 1 - g, slot if g else 1 - slot)
                    if g == 0:
                        pe.wait_ge(prepared, i * 4 + 4)
                        pe.wait_ge(toks, i * 4 + 4)
                    if tail:
                        pe.wait_ge(akv_sb, G * 2)
                        pe.wait_ge(x_new, G * 10 - 1)
                    scores(G, g, slot, 0)
                    if tail:
                        if g == 0 and not (isinstance(i, int) and i < 2):
                            pe.wait_ge(y_out, i - 1)
                        for s in range(2):
                            solve(*before, s)

                    def expand(lev, s):
                        if lev == 0:
                            pe.wait_ge(x0, (G * 2 + s) * 2 + 2)
                        mm(psum[:, 4 + 2 * s, 0:2 * P], ident_b[:, 0:P], ident_b[:, :], stop=False,
                           skip_group_check=True)
                        if lev:
                            pe.wait_ge(x_new, G * 10 + (2 * (lev - 1) + s + 1))
                        for e in range(2):
                            ins = mm(psum[:, 4 + 2 * s, e * P:(e + 1) * P], lsb[:, s, e, :],
                                     xs[:, s, e, P:2 * P], start=False, skip_group_check=True)
                        ins.then_inc(z_ps, 1)

                    def double(lev, s):
                        pe.wait_ge(zts, G * 10 + (2 * lev + s + 1))
                        for e in range(2):
                            if lev < 4:
                                mm(psum[:, 5 + 2 * s, e * 2 * P:e * 2 * P + P], zt[:, s, e, :], xs[:, s, e, 0:P])
                            ins = mm(psum[:, 5 + 2 * s, e * 2 * P + P:(e + 1) * 2 * P], xs[:, s, e, 0:P],
                                     zt[:, s, e, :])
                        ins.then_inc(xx_ps, 1)

                    pe.wait_ge(mxs, G * 2 + 1)
                    scores(G, g, slot, 1)
                    for s in range(2):
                        expand(0, s)
                        if tail:
                            moves(*before, s)
                        double(0, s)
                    for lev in range(1, 5):
                        for s in range(2):
                            expand(lev, s)
                        if lev == 1:
                            for s in range(2):
                                a_k_v(G, g, slot, s)
                        if lev == 2 and tail:
                            for s in range(2):
                                pe.wait_ge(mts, (G - 1) * 2 + (s + 1))
                                advance(*before[:2], s, 0)
                        if g == 1 and not last:
                            if lev == 3:
                                pe.wait_ge(akv_sb, G * 2 + 2)
                                turn_tok(i + 1, 1 - slot, 0)
                                turn_tok(i + 1, 1 - slot, 1)
                            if lev == 4:
                                turn_tok(i + 1, 1 - slot, 2)
                        if lev >= 3 and tail:
                            outputs(*before, lev - 3)
                        for s in range(2):
                            double(lev, s)
                    if g == 1 and not last:
                        turn_tok(i + 1, 1 - slot, 3)
                    if g == 1 and not first:
                        pe.wait_ge(ys, G * 2)
                        turn_out(i - 1)

                pe.wait_ge(zeroed, 4)
                pe.wait_ge(ones_in, 2)
                for m in range(4):
                    turn_tok(0, 0, m)
                for_groups(pe, step)
                final = (2 * TT - 1, 1, (TT - 1) % 2)
                pe.wait_ge(y_out, TT - 1)
                for s in range(2):
                    solve(*final, s)
                for s in range(2):
                    moves(*final, s)
                for s in range(2):
                    pe.wait_ge(mts, 2 * (2 * TT - 1) + s + 1)
                    advance(*final[:2], s, 0)
                for s in range(2):
                    outputs(*final, s)
                pe.wait_ge(ys, 4 * TT)
                turn_out(TT - 1)

    def rwkv_finish(tag):
        g2_sb = at(f"{tag}_g2", [P, RWKV_W], F32, W_OFF)
        blk = at(f"{tag}_blk", [P, P], F32, W_OFF + 2048)
        rk = [at(f"{tag}_rk{s}", [P, HALF], F32, T_OFF + 2048 * s) for s in range(2)]
        bonus = [at(f"{tag}_bonus{s}", [P, HALF], F32, T_OFF + 4096 + 2048 * s) for s in range(2)]
        with ExitStack() as ctx:
            loaded, rks, ps, scaled, bonuses, added, gated = sems(
                ctx, tag, "loaded rks ps scaled bonuses added gated")
            block = ctx.enter_context(nc.Block())

            @block.sync
            def _(sp):
                sp.dma_start(g2_sb[:, :], g2).then_inc(loaded, 16)
                sp.dma_start(blk[:, :], consts[:, K_BLK:K_BLK + P]).then_inc(loaded, 16)

            def place(n):
                ct, h = n // 2, n % 2
                return ct, slice(h * HALF, (h + 1) * HALF), n % 2

            @block.tensor
            def _(pe):
                pe.wait_ge(loaded, 32)
                for n in range(2 * RW_T):
                    ct, cols, s = place(n)
                    if n >= 2:
                        pe.wait_ge(gated, n - 1)
                    pe.matmul(psum[:, 2 + s, :], g2_sb[:, ct * P:(ct + 1) * P], z_buf[:, Z_G, cols],
                              start=True, stop=True)
                    pe.wait_ge(rks, n + 1)
                    pe.matmul(psum[:, s, :], blk[:, :], rk[s][:, :], start=True, stop=True).then_inc(ps, 1)

            @block.scalar
            def _(act):
                for n in range(2 * RW_T):
                    ct, cols, s = place(n)
                    y = y_buf[:, RW_T + ct, cols]
                    act.activation(y, cum_buf[:, ct, cols], ACT.Identity, scale=vec[:, V_LW + ct:V_LW + ct + 1],
                                   bias=vec[:, V_LB + ct:V_LB + ct + 1]).then_inc(scaled, 1)

            @block.vector
            def _(dve):
                def product(n):
                    ct, cols, s = place(n)
                    dve.wait_ge(ps, max(n - 1, 0))
                    dve.scalar_tensor_tensor(rk[s][:, :], z_buf[:, Z_R + ct, cols], vec[:, V_RK + ct:V_RK + ct + 1],
                                             z_buf[:, Z_K + ct, cols], ALU.mult, ALU.mult).then_inc(rks, 1)
                product(0)
                for n in range(2 * RW_T):
                    ct, cols, s = place(n)
                    y = y_buf[:, RW_T + ct, cols]
                    if n + 1 < 2 * RW_T:
                        product(n + 1)
                    dve.wait_ge(ps, n + 1)
                    dve.tensor_tensor(bonus[s][:, :], psum[:, s, :], z_buf[:, Z_V + ct, cols], ALU.mult
                                      ).then_inc(bonuses, 1)
                    dve.wait_ge(bonuses, n + 1)
                    dve.wait_ge(scaled, n + 1)
                    dve.tensor_tensor(y, y, bonus[s][:, :], ALU.add).then_inc(added, 1)
                    dve.wait_ge(added, n + 1)
                    dve.tensor_tensor(y, y, psum[:, 2 + s, :], ALU.mult).then_inc(gated, 1)
    setup()
    norm("n0", x, None, None, 0)
    fox_gates("fg")
    attention("fox", w_in0, FOX_W, N_FOX // 2, True)
    rwkv_project("rp")
    rwkv_prepare("rr")
    rwkv_chunks("rc")
    rwkv_finish("rf")
    clear_semaphores()
    down("o0", w_out0, y_buf, KT)
    norm("n1", x, 0, x_mid[0], 16)
    ffn_up("u0", 0)
    down("d0", w_down[0], g_buf, FT)
    norm("n2", x_mid[0], 2, x_mid[1], 8)
    clear_semaphores()
    rotary_tables("rt")
    attention("dil", w_in1, D, KT, False)
    clear_semaphores()
    down("o1", w_out1, y_buf, KT)
    norm("n3", x_mid[1], 1, x_mid[2], 24)
    ffn_up("u1", 1)
    down("d1", w_down[1], g_buf, FT)
    norm("n4", x_mid[2], 3, out, None)
    top.close()


def kernel(**inputs):
    import concourse.bacc as _bacc
    from concourse.bass_utils import run_bass_kernel_spmd as _run

    def a(name):
        return np.ascontiguousarray(inputs[name])

    consts, dil = constants()
    vecs = np.concatenate([a(n).reshape(-1, P) for n in (
        "norm_mix_pre", "norm_ffn_pre", "rwkv_mu", "rwkv_w0", "rwkv_a0", "rwkv_k_k", "rwkv_k_a",
        "rwkv_r_k", "rwkv_ln_w", "rwkv_ln_b")])
    conv = np.concatenate([a("ffn_conv_w"), a("ffn_conv_b")[:, None]], 1)
    g_post = np.concatenate([a("norm_mix_post"), a("norm_ffn_post")])
    arrays = dict(
        x=a("x")[0], positions=a("positions"), g_post=g_post, vecs=vecs, conv=conv,
        w_in0=a("even_w_in")[0], w_out0=a("even_w_out")[0], w_in1=a("odd_w_in")[0], w_out1=a("odd_w_out")[0],
        w_up=a("ffn_w_up"), w_down=a("ffn_w_down"), forget_bias=a("fox_forget_bias").reshape(N_FOX, 1),
        w2=a("rwkv_w2")[0], a2=a("rwkv_a2")[0], g2=a("rwkv_g2")[0], consts=consts, dil=dil)
    nc = _bacc.Bacc("TRN2", target_bir_lowering=False, num_devices=1)
    args = {n: nc.dram_tensor(f"in_{n}", v.shape, mybir.dt.from_np(v.dtype), kind="ExternalInput").ap()
            for n, v in arrays.items()}
    args["out"] = nc.dram_tensor("out_x", [T, D], F32, kind="ExternalOutput").ap()
    build(nc, **args)
    r = _run(nc, [{f"in_{n}": v for n, v in arrays.items()}], core_ids=[0])
    return np.asarray(r.results[0]["out_x"]).reshape(1, T, D)
```

```python
from contextlib import ExitStack

import numpy as np

import concourse.bass as bass
from concourse import mybir

F32 = mybir.dt.float32
F32R = mybir.dt.float32r
BF16 = mybir.dt.bfloat16
I32 = mybir.dt.int32
ACT = mybir.ActivationFunctionType
ALU = mybir.AluOpType
AX_X = mybir.AxisListType.X
ds = bass.ds

P = 128
D = 1024
T = 1024
KT = D // P
TT = T // P
HALF = 512
HD = 64
N_FOX = 8
N_RWKV = 8
FOX_W = N_FOX * HD
RWKV_W = N_RWKV * HD
RW_T = RWKV_W // P
FOX_IN = 3 * FOX_W + N_FOX
RWKV_IN = 3 * RWKV_W + 256
D_FF = ((8 * D // 3 + 127) // 128) * 128
FT = D_FF // P
RMS_EPS = 1e-6
GN_EPS = 64e-5
CHUNK = 64
DECAY = float(np.exp(-0.5))
ATT_SCALE = HD ** -0.5
NEG = -1e30

BASE = 16512
A_OFF = BASE
B_OFF = A_OFF + 65536
W_OFF = B_OFF + 90112
T_OFF = W_OFF + 28672
C_OFF = T_OFF + 20608

V_MU = 32
V_W0, V_A0, V_KK, V_KA, V_RK, V_LW, V_LB = (46 + 4 * n for n in range(7))
V_ROWS = 74

K_ID = 0
K_BLK = 128
K_AB = 256
K_L = 768
K_M1 = 896
K_LEV = 1152
K_ID64 = 1792
K_RESET = 1856
K_FREQ = 2368
K_CAUS = 2370
K_COLS = 2498


def constants():
    i, j = np.arange(P)[:, None], np.arange(P)[None, :]
    same = (i // CHUNK) == (j // CHUNK)
    c = np.zeros((P, K_COLS), np.float32)
    c[:, K_ID:K_ID + P] = i == j
    c[:, K_BLK:K_BLK + P] = same
    strict_t, incl_t = same & (i < j), same & (i <= j)
    for n, m in enumerate((strict_t, incl_t, strict_t, incl_t)):
        c[:, K_AB + n * P:K_AB + (n + 1) * P] = m
    c[:, K_L:K_L + P] = same & (i > j)

    def lower_left(b):
        return ((i // (2 * b)) == (j // (2 * b))) & (i % (2 * b) >= b) & (j % (2 * b) < b)
    c[:, K_M1:K_M1 + P] = lower_left(1)
    c[:, K_M1 + P:K_M1 + 2 * P] = lower_left(1).T
    for n in range(5):
        c[:, K_LEV + n * P:K_LEV + (n + 1) * P] = lower_left(2 << n).T | (i == j)
    c[:, K_ID64:K_ID64 + 64] = (i % 64) == j[:, :64]
    c[:, K_RESET:K_RESET + HALF] = (np.arange(HALF) % CHUNK != 0)[None]
    rot = HD // 4
    freq = np.float32(500000.0) ** (-np.arange(0, rot, 2, dtype=np.float32) / np.float32(rot))
    for r in range(P):
        d = r % HD
        if d < rot:
            c[r, K_FREQ] = freq[d % (rot // 2)]
            c[r, K_FREQ + 1] = -1.0 if d < rot // 2 else 1.0
    c[:, K_CAUS:K_CAUS + P] = np.where(j > i, NEG, 0.0)
    dist = i - np.arange(T)[None, :] + (TT - 1) * P
    count = sum((dist >= 0) & (dist % d == 0) & (dist <= w) for w, d in ((128, 1), (512, 4), (2048, 16)))
    dil = np.stack([np.where(count > 0, 0.0, NEG), count], 1).astype(np.float32)
    return c, dil


def build(nc, x, positions, g_post, vecs, conv, w_in0, w_out0, w_in1, w_out1, w_up, w_down,
          forget_bias, w2, a2, g2, consts, dil, out):
    top = ExitStack()

    def at(name, shape, dt, off):
        return nc.alloc_sbuf_tensor_at(name, shape, dt, offset=off)

    ident = at("ident", [P, P], F32, C_OFF)
    vec = at("vec", [P, V_ROWS], F32, C_OFF + 512)
    h_hi = at("h_hi", [P, KT, T], F32R, A_OFF)
    h_lo = at("h_lo", [P, KT, T], F32R, A_OFF + 32768)
    m_buf = at("m_buf", [P, TT, D], F32, A_OFF)
    g_buf = at("g_buf", [P, FT, T], F32, B_OFF)
    y_buf = at("y_buf", [P, KT, T], F32, B_OFF)
    gain_buf = at("gain", [P, D], F32, T_OFF + 16384)
    m_sums = at("m_sums", [P, 2, TT], F32, T_OFF + 20480)
    cst = at("cst", [P, 8], F32, C_OFF + 832)
    convc = at("convc", [P, 2, 4, 2 * FT], F32, C_OFF + 1024)
    x_mid = [nc.dram_tensor(f"x_mid{n}", [T, D], F32, kind="Internal").ap() for n in range(3)]
    negc_dram = nc.dram_tensor("negc_dram", [N_FOX, T], F32, kind="Internal").ap()
    psum = top.enter_context(nc.psum_tensor("psum", [P, 8, HALF], F32))

    used_ids = []

    def sems(ctx, stage, names):
        got = [ctx.enter_context(nc.semaphore(f"{stage}_{n}")) for n in names.split()]
        used_ids.extend(s.num for s in got)
        return got

    def clear_semaphores():
        ids = sorted(used_ids)
        used_ids.clear()
        with nc.Block() as block:
            @block.gpsimd
            def _(pool):
                first = ids[0]
                for n, num in enumerate(ids):
                    if n + 1 == len(ids) or ids[n + 1] != num + 1:
                        pool.sem_clear(range(first, num + 1))
                        first = ids[n + 1] if n + 1 < len(ids) else 0

    def setup():
        rows = at("vec_rows", [V_ROWS, P], F32, B_OFF)
        crow = at("conv_rows", [2 * FT, 8, P], F32, B_OFF + 1024)
        with ExitStack() as ctx:
            loaded, turned, copied = sems(ctx, "set", "loaded turned copied")
            block = ctx.enter_context(nc.Block())

            @block.sync
            def _(sp):
                sp.dma_start(ident[:, :], consts[:, K_ID:K_ID + P]).then_inc(loaded, 16)
                sp.dma_start(rows[:, :], vecs).then_inc(loaded, 16)
                sp.dma_start(crow[:, :, :], conv.rearrange("l j (t p) -> t (l j) p", p=P)).then_inc(loaded, 16)

            @block.tensor
            def _(pe):
                pe.wait_ge(loaded, 48)
                for n in range(8):
                    pe.transpose(psum[:, 0, n * 2 * FT:(n + 1) * 2 * FT], crow[:, n, :],
                                 ident[0:2 * FT, 0:2 * FT])
                pe.transpose(psum[:, 1, 0:V_ROWS], rows[:, :],
                             ident[0:V_ROWS, 0:V_ROWS]).then_inc(turned, 1)

            @block.vector
            def _(dve):
                for n, value in enumerate((RMS_EPS, GN_EPS, 1.0)):
                    dve.memset(cst[:, n:n + 1], value).then_inc(copied, 1)
                dve.wait_ge(turned, 1)
                dve.tensor_copy(convc[:, :, :, :].rearrange("p l j t -> p (l j t)"),
                                psum[:, 0, 0:16 * FT]).then_inc(copied, 1)
                dve.tensor_copy(vec[:, :], psum[:, 1, 0:V_ROWS]).then_inc(copied, 1)

    class FirstWeights:
        def __init__(self, ctx, tag, w, cols, off, shared):
            self.w, self.cols, self.shared, self.tiles = w.rearrange("(k p) n -> p k n", p=P), cols, shared, len(cols)
            n_raw = 1 if shared else self.tiles
            tiles = [(n_raw, "raw", F32), (self.tiles, "whi", F32R), (self.tiles, "wlo", F32R)]
            self.raw, self.whi, self.wlo = [
                [at(f"{tag}_{name}{j}", [P, KT, P], dt, off + 4096 * (sum(m for m, *_ in tiles[:k]) + j))
                 for j in range(n)] for k, (n, name, dt) in enumerate(tiles)]
            self.zero = at(f"{tag}_zero", [P, 8], F32, C_OFF + 2560)
            self.raw_in = sems(ctx, tag, " ".join(f"raw{j}" for j in range(n_raw)))
            self.w_full = sems(ctx, tag, " ".join(f"wfull{j}" for j in range(n_raw)))
            self.zeroed, self.split_hi = sems(ctx, tag, "zeroed split_hi")

        def load(self, sp, t):
            j = 0 if self.shared else t
            if self.shared and t:
                sp.wait_ge(self.w_full[0], t)
            sp.dma_start(self.raw[j][:, :, :], self.w[:, :, self.cols[t]:self.cols[t] + P]
                         ).then_inc(self.raw_in[j], 16)

        def split(self, pool, t):
            if t == 0:
                pool.memset(self.zero[:, :], 0.0).then_inc(self.zeroed, 1)
                pool.wait_ge(self.zeroed, 1)
            j = 0 if self.shared else t
            pool.wait_ge(self.raw_in[j], 16 * (t + 1) if self.shared else 16)
            split_weights(pool, self.raw[j][:, :, :], self.whi[t][:, :, :], self.wlo[t][:, :, :],
                          self.zero, self.split_hi, t + 1, self.w_full[j])

    def norm(tag, x_in, after_branch, x_out, pre_col, ahead=None):
        last = pre_col is None
        m = m_buf
        xt = at(f"{tag}_x", [P, TT, D], F32, B_OFF)
        hn = at(f"{tag}_hn", [P, TT, D], F32, B_OFF + 32768)
        junk = at(f"{tag}_junk", [P, D], F32, T_OFF + 4096)
        st = at(f"{tag}_st", [P, 4, TT], F32, T_OFF + 12288)
        hi, lo = h_hi, h_lo
        half_tiles = TT // 2
        on_act, on_pool = (4, 5, 6), (7,)
        with ExitStack() as ctx:
            (m_sum, m_rms, m_rs, x_new, x_sq, x_rms, x_rs, scaled_dve, scaled_act, scaled_pool, turned,
             hi_done, lo_done, stored) = sems(
                ctx, tag, "m_sum m_rms m_rs x_new x_sq x_rms x_rs scaled_dve scaled_act scaled_pool turned "
                "hi_done lo_done stored")
            x_in_sem = sems(ctx, tag, " ".join(f"xin{i}" for i in range(TT)))
            block = ctx.enter_context(nc.Block())

            def load(engine, i):
                engine.dma_start(xt[:, i, :], x_in[i * P:(i + 1) * P, :]).then_inc(x_in_sem[i], 16)

            @block.sync
            def _(sp):
                for i in range(0, TT, 2):
                    load(sp, i)
                if ahead:
                    ahead.load(sp, 0)
                for i in range(TT):
                    if after_branch:
                        sp.wait_ge(x_new, i + 1)
                        sp.dma_start(x_out[i * P:(i + 1) * P, :], xt[:, i, :]).then_inc(stored, 16)
                    if ahead and i % 4 == 3 and 1 + i // 4 < ahead.tiles:
                        ahead.load(sp, 1 + i // 4)
                if after_branch:
                    sp.wait_ge(stored, 16 * TT)

            @block.scalar
            def _(act):
                for i in range(1, TT, 2):
                    load(act, i)
                if after_branch:
                    act.wait_ge(m_sum, 1)
                    act.activation(st[:, 1, :], st[:, 0, :], ACT.Sqrt, scale=1.0 / D, bias=cst[:, 0:1]
                                   ).then_inc(m_rms, 1)
                if last:
                    return
                for h in range(2):
                    for i in range(h * half_tiles, (h + 1) * half_tiles):
                        if after_branch:
                            act.wait_ge(x_new, i + 1)
                        else:
                            act.wait_ge(x_in_sem[i], 16)
                        if i:
                            act.wait_ge(x_sq, i)
                        act.activation(junk[:, :], xt[:, i, :], ACT.Square,
                                       accum_out=st[:, 2, i:i + 1]).then_inc(x_sq, 1)
                    of = slice(h * half_tiles, (h + 1) * half_tiles)
                    act.wait_ge(x_sq, (h + 1) * half_tiles)
                    act.activation(st[:, 3, of], st[:, 2, of], ACT.Sqrt, scale=1.0 / D,
                                   bias=cst[:, 0:1]).then_inc(x_rms, 1)
                act.wait_ge(x_rs, 2)
                for i in on_act:
                    act.activation(hn[:, i, :], xt[:, i, :], ACT.Copy, scale=st[:, 3, i:i + 1]
                                   ).then_inc(scaled_act, 1)
                if after_branch:
                    act.wait_ge(x_new, TT)
                for n in range(2 * KT):
                    k, h = n % KT, n // KT
                    act.wait_ge(turned, n + 1)
                    act.activation(hi[:, k, h * HALF:(h + 1) * HALF], psum[:, n % 8, :], ACT.Copy,
                                   scale=vec[:, pre_col + k:pre_col + k + 1]).then_inc(hi_done, 1)

            @block.gpsimd
            def _(pool):
                if last:
                    return
                if ahead:
                    ahead.split(pool, 0)
                pool.wait_ge(x_rs, 2)
                for i in on_pool:
                    pool.tensor_tensor(hn[:, i, :], xt[:, i, :], st[:, 3, i:i + 1].broadcast_to([P, D]),
                                       ALU.mult).then_inc(scaled_pool, 1)
                if ahead:
                    for t in range(1, ahead.tiles):
                        ahead.split(pool, t)

            @block.vector
            def _(dve):
                if after_branch:
                    dve.tensor_tensor(st[:, 0, :], m_sums[:, 0, :], m_sums[:, 1, :], ALU.add).then_inc(m_sum, 1)
                    dve.wait_ge(m_rms, 1)
                    dve.reciprocal(st[:, 1, :], st[:, 1, :]).then_inc(m_rs, 1)
                    dve.wait_ge(m_rs, 1)
                    for i in range(TT):
                        dve.wait_ge(x_in_sem[i], 16)
                        dve.scalar_tensor_tensor(xt[:, i, :], m[:, i, :], st[:, 1, i:i + 1], xt[:, i, :],
                                                 ALU.mult, ALU.add).then_inc(x_new, 1)
                if last:
                    return
                for h in range(2):
                    of = slice(h * half_tiles, (h + 1) * half_tiles)
                    dve.wait_ge(x_rms, h + 1)
                    dve.reciprocal(st[:, 3, of], st[:, 3, of]).then_inc(x_rs, 1)
                    dve.wait_ge(x_rs, h + 1)
                    for i in range(h * half_tiles, (h + 1) * half_tiles):
                        if i not in on_act + on_pool:
                            dve.tensor_scalar(hn[:, i, :], xt[:, i, :], st[:, 3, i:i + 1], None, ALU.mult
                                              ).then_inc(scaled_dve, 1)
                for n in range(2 * KT):
                    k, h = n % KT, n // KT
                    dve.wait_ge(hi_done, n + 1)
                    dve.scalar_tensor_tensor(lo[:, k, h * HALF:(h + 1) * HALF], psum[:, n % 8, :],
                                             vec[:, pre_col + k:pre_col + k + 1],
                                             hi[:, k, h * HALF:(h + 1) * HALF],
                                             ALU.mult, ALU.subtract).then_inc(lo_done, 1)

            if not last:
                @block.tensor
                def _(pe):
                    pe.wait_ge(scaled_dve, TT - len(on_act) - len(on_pool))
                    for n in range(2 * KT):
                        k, h = n % KT, n // KT
                        if n == KT:
                            pe.wait_ge(scaled_act, len(on_act))
                            pe.wait_ge(scaled_pool, len(on_pool))
                        if n >= 8:
                            pe.wait_ge(lo_done, n - 7)
                        for i in range(4):
                            t = pe.transpose(psum[:, n % 8, i * P:(i + 1) * P],
                                             hn[:, 4 * h + i, k * P:(k + 1) * P], ident[:, :])
                        t.then_inc(turned, 1)

    def split_weights(pool, raw, whi, wlo, zero, hi_sem, hi_count, done):
        n = raw.shape[-1]
        pool.tensor_tensor(whi, raw, zero[:, 0:1].broadcast_to([P, raw.shape[1], n]) if len(raw.shape) == 3
                           else zero[:, 0:1].broadcast_to([P, n]), ALU.add).then_inc(hi_sem, 1)
        pool.wait_ge(hi_sem, hi_count)
        pool.tensor_tensor(wlo, raw, whi, ALU.subtract).then_inc(done, 1)

    def project_half(pe, bank, whi, wlo, hhi, hlo, half, ks=range(KT)):
        cols = slice(half * HALF, (half + 1) * HALF)
        for k in ks:
            pe.matmul(bank, whi[:, k, :], hhi[:, k, cols], start=(k == 0), stop=False)
            pe.matmul(bank, whi[:, k, :], hlo[:, k, cols], start=False, stop=False)
            mm = pe.matmul(bank, wlo[:, k, :], hhi[:, k, cols], start=False, stop=(k == KT - 1))
        return mm

    def ffn_up(tag, layer, first):
        hi, lo = h_hi, h_lo
        g = g_buf
        raw, whi, wlo, zero = first.raw, first.whi, first.wlo, first.zero
        raw_in, w_full, split_hi = first.raw_in, first.w_full, first.split_hi
        u = [at(f"{tag}_u{j}", [P, T + 2], F32, T_OFF + 4128 * j) for j in range(2)]
        acc = [at(f"{tag}_acc{j}", [P, T], F32, T_OFF + 8256 + 4096 * j) for j in range(2)]
        act_g = at(f"{tag}_actg", [P, T], F32, T_OFF + 16448)
        w = w_up[layer].rearrange("(k p) n -> p k n", p=P)
        with ExitStack() as ctx:
            pads, gelu_done, gated = sems(ctx, tag, "pads gelu gated")
            ps_full = sems(ctx, tag, "psfull0 psfull1")
            evac = sems(ctx, tag, "evac0 evac1")
            conv1 = sems(ctx, tag, "conv1_0 conv1_1")
            conv2 = sems(ctx, tag, "conv2_0 conv2_1")
            block = ctx.enter_context(nc.Block())

            @block.sync
            def _(sp):
                with sp.Fori(1, FT) as c:
                    for j in range(2):
                        sp.wait_ge(w_full[j], c)
                        sp.dma_start(raw[j][:, :, :], w[:, :, ds(c * P + j * D_FF, P)]).then_inc(raw_in[j], 16)

            @block.gpsimd
            def _(pool):
                with pool.Fori(1, FT) as c:
                    for j in range(2):
                        pool.wait_ge(ps_full[j], c * 2)
                        pool.wait_ge(raw_in[j], c * 16 + 16)
                        split_weights(pool, raw[j][:, :, :], whi[j][:, :, :], wlo[j][:, :, :], zero,
                                      split_hi, c * 2 + j + 1, w_full[j])

            @block.tensor
            def _(pe):
                with pe.Fori(0, FT) as c:
                    for j in range(2):
                        for h in range(2):
                            pe.wait_ge(evac[j], c * 2)
                            pe.wait_ge(w_full[j], c + 1)
                            project_half(pe, psum[:, 2 * j + h, :], whi[j], wlo[j], hi, lo, h
                                         ).then_inc(ps_full[j], 1)

            @block.scalar
            def _(act):
                cc = convc[:, layer, :, :]
                with act.Fori(0, FT) as c:
                    def take(j):
                        act.wait_ge(conv2[j], c)
                        act.wait_ge(gated if j else gelu_done, c)
                        for h in range(2):
                            bank = psum[:, 2 * j + h, :]
                            act.wait_ge(ps_full[j], c * 2 + h + 1)
                            act.activation(u[j][:, 2 + h * HALF:2 + (h + 1) * HALF], bank, ACT.Copy)
                            act.activation(acc[j][:, h * HALF:(h + 1) * HALF], bank, ACT.Identity,
                                           scale=cc[:, 2, ds(c + j * FT, 1)],
                                           bias=cc[:, 3, ds(c + j * FT, 1)]).then_inc(evac[j], 1)
                    take(0)
                    act.wait_ge(conv2[0], c + 1)
                    act.wait_ge(gated, c)
                    act.activation(act_g[:, :], acc[0][:, :], ACT.Gelu_apprx_tanh).then_inc(gelu_done, 1)
                    take(1)

            @block.vector
            def _(dve):
                cc = convc[:, layer, :, :]
                for j in range(2):
                    dve.memset(u[j][:, 0:2], 0.0).then_inc(pads, 1)
                dve.wait_ge(pads, 2)
                with dve.Fori(0, FT) as c:
                    for j in range(2):
                        dve.wait_ge(evac[j], c * 2 + 2)
                        if j == 0:
                            dve.wait_ge(gelu_done, c)
                        dve.scalar_tensor_tensor(acc[j][:, :], u[j][:, 1:T + 1], cc[:, 1, ds(c + j * FT, 1)],
                                                 acc[j][:, :], ALU.mult, ALU.add).then_inc(conv1[j], 1)
                        dve.wait_ge(conv1[j], c + 1)
                        dve.scalar_tensor_tensor(acc[j][:, :], u[j][:, 0:T], cc[:, 0, ds(c + j * FT, 1)],
                                                 acc[j][:, :], ALU.mult, ALU.add).then_inc(conv2[j], 1)
                    dve.wait_ge(gelu_done, c + 1)
                    dve.wait_ge(conv2[1], c + 1)
                    dve.tensor_tensor(g[:, c, :], act_g[:, :], acc[1][:, :], ALU.mult).then_inc(gated, 1)

    def down(tag, w, src, n_tiles, post_row):
        m = m_buf
        raw = [at(f"{tag}_raw{j}", [P, HALF], F32, W_OFF + 2048 * j) for j in range(2)]
        whi = [at(f"{tag}_whi{j}", [P, HALF], F32R, W_OFF + 4096 + 2048 * j) for j in range(2)]
        wlo = [at(f"{tag}_wlo{j}", [P, HALF], F32R, W_OFF + 8192 + 2048 * j) for j in range(2)]
        zero = at(f"{tag}_zero", [P, 8], F32, W_OFF + 24576)
        shi = [at(f"{tag}_shi{j}", [P, T], F32R, T_OFF + 4096 * j) for j in range(2)]
        slo = [at(f"{tag}_slo{j}", [P, T], F32R, T_OFF + 8192 + 4096 * j) for j in range(2)]
        junk = at(f"{tag}_junk", [P, HALF], F32, W_OFF + 12288)
        pairs = n_tiles // 2
        with ExitStack() as ctx:
            zeroed, split_hi, gain_in, squared = sems(ctx, tag, "zeroed split_hi gain_in squared")
            raw_in = sems(ctx, tag, "raw0 raw1")
            w_full = sems(ctx, tag, "wfull0 wfull1")
            s_hi = sems(ctx, tag, "shi0 shi1")
            s_lo = sems(ctx, tag, "slo0 slo1")
            used = sems(ctx, tag, "used0 used1")
            bank_full = sems(ctx, tag, " ".join(f"bank{b}" for b in range(8)))
            bank_read = sems(ctx, tag, " ".join(f"read{b}" for b in range(8)))
            block = ctx.enter_context(nc.Block())

            @block.sync
            def _(sp):
                sp.dma_start(gain_buf[:, :], g_post[post_row:post_row + 1, :].broadcast_to([P, D])
                             ).then_inc(gain_in, 16)
                for nh in range(2):
                    with sp.Fori(nh * pairs, (nh + 1) * pairs) as c:
                        for j in range(2):
                            sp.wait_ge(w_full[j], c)
                            sp.dma_start(raw[j][:, :], w[ds(c * (2 * P) + (j - nh * n_tiles) * P, P),
                                                         nh * HALF:(nh + 1) * HALF]).then_inc(raw_in[j], 16)

            @block.gpsimd
            def _(pool):
                pool.memset(zero[:, :], 0.0).then_inc(zeroed, 1)
                pool.wait_ge(zeroed, 1)
                with pool.Fori(0, 2 * pairs) as c:
                    for j in range(2):
                        pool.wait_ge(used[j], c)
                        pool.wait_ge(raw_in[j], c * 16 + 16)
                        split_weights(pool, raw[j][:, :], whi[j][:, :], wlo[j][:, :], zero,
                                      split_hi, c * 2 + j + 1, w_full[j])

            @block.scalar
            def _(act):
                for nh in range(2):
                    with act.Fori(0, pairs) as c:
                        for j in range(2):
                            act.wait_ge(used[j], c + nh * pairs)
                            act.activation(shi[j][:, :], src[:, c * 2 + j, :], ACT.Copy).then_inc(s_hi[j], 1)
                    for b in range(8):
                        if b < 7:
                            act.wait_ge(bank_full[b], nh + 1)
                        else:
                            act.wait_ge(used[1], (nh + 1) * pairs)
                        if b or nh:
                            act.wait_ge(squared, nh * 8 + b)
                        act.activation(junk[:, :], psum[:, b, :], ACT.Square,
                                       accum_out=m_sums[:, nh, b:b + 1]).then_inc(squared, 1)

            @block.vector
            def _(dve):
                for nh in range(2):
                    with dve.Fori(0, pairs) as c:
                        for j in range(2):
                            dve.wait_ge(s_hi[j], c + nh * pairs + 1)
                            dve.tensor_tensor(slo[j][:, :], src[:, c * 2 + j, :], shi[j][:, :],
                                              ALU.subtract).then_inc(s_lo[j], 1)
                    if nh == 0:
                        dve.wait_ge(gain_in, 16)
                    for b in range(8):
                        dve.wait_ge(squared, nh * 8 + b + 1)
                        dve.tensor_tensor(m[:, b, nh * HALF:(nh + 1) * HALF], psum[:, b, :],
                                          gain_buf[:, nh * HALF:(nh + 1) * HALF], ALU.mult
                                          ).then_inc(bank_read[b], 1)

            @block.tensor
            def _(pe):
                def pair(nh, c, first=False, last=False):
                    for j in range(2):
                        pe.wait_ge(w_full[j], c + nh * pairs + 1)
                        pe.wait_ge(s_lo[j], c + nh * pairs + 1)
                        for b in range(8):
                            lhi, llo = shi[j][:, b * P:(b + 1) * P], slo[j][:, b * P:(b + 1) * P]
                            if first and j == 0 and nh:
                                pe.wait_ge(bank_read[b], nh)
                            pe.matmul(psum[:, b, :], lhi, whi[j][:, :], start=(first and j == 0), stop=False,
                                      skip_group_check=True)
                            pe.matmul(psum[:, b, :], lhi, wlo[j][:, :], start=False, stop=False,
                                      skip_group_check=True)
                            mm = pe.matmul(psum[:, b, :], llo, whi[j][:, :], start=False,
                                           stop=(last and j == 1), skip_group_check=True)
                            if last and j == 1 and b < 7:
                                mm.then_inc(bank_full[b], 1)
                        mm.then_inc(used[j], 1)
                for nh in range(2):
                    pair(nh, 0, first=True)
                    with pe.Fori(1, pairs - 1) as c:
                        pair(nh, c)
                    pair(nh, pairs - 1, last=True)

    def fox_gates(tag, first, ahead):
        whi, wlo, w_full = first.whi[0], first.wlo[0], first.w_full[0]
        bias = at(f"{tag}_bias", [N_FOX, 8], F32, B_OFF + 20480)
        size, low, nl, cum, ones = (at(f"{tag}_{n}", [N_FOX, T], F32, B_OFF + 4096 * i)
                                    for i, n in enumerate("size low nl cum ones".split()))
        with ExitStack() as ctx:
            proj, act_done, dve_done, bias_in, stored = sems(ctx, tag, "proj act_done dve_done bias_in stored")
            block = ctx.enter_context(nc.Block())

            @block.sync
            def _(sp):
                sp.dma_start(bias[:, 0:1], forget_bias).then_inc(bias_in, 16)
                for t in range(ahead.tiles):
                    ahead.load(sp, t)
                sp.wait_ge(dve_done, 4)
                sp.dma_start(negc_dram, cum[:, :]).then_inc(stored, 16)
                sp.wait_ge(stored, 16)

            @block.gpsimd
            def _(pool):
                for t in range(ahead.tiles):
                    ahead.split(pool, t)

            @block.tensor
            def _(pe):
                pe.wait_ge(w_full, 1)
                for h in range(2):
                    project_half(pe, psum[:, h, :], whi, wlo, h_hi, h_lo, h).then_inc(proj, 1)

            @block.scalar
            def _(act):
                act.wait_ge(proj, 2)
                act.wait_ge(bias_in, 16)
                z = psum[0:N_FOX, 0:2, :].rearrange("p b n -> p (b n)")
                act.activation(size[:, :], z, ACT.Abs, bias=bias[:, 0:1]).then_inc(act_done, 1)
                act.wait_ge(act_done, 1)
                act.activation(size[:, :], size[:, :], ACT.Exp, scale=-1.0).then_inc(act_done, 1)
                act.wait_ge(act_done, 2)
                act.activation(size[:, :], size[:, :], ACT.Ln, bias=cst[0:N_FOX, 2:3]).then_inc(act_done, 1)

            @block.vector
            def _(dve):
                dve.memset(ones[:, :], 1.0).then_inc(dve_done, 1)
                dve.wait_ge(act_done, 1)
                dve.wait_ge(bias_in, 16)
                z = psum[0:N_FOX, 0:2, :].rearrange("p b n -> p (b n)")
                dve.tensor_scalar(low[:, :], z, bias[:, 0:1], 0.0, ALU.add, ALU.min).then_inc(dve_done, 1)
                dve.wait_ge(act_done, 3)
                dve.wait_ge(dve_done, 2)
                dve.tensor_tensor(nl[:, :], size[:, :], low[:, :], ALU.subtract).then_inc(dve_done, 1)
                dve.wait_ge(dve_done, 3)
                dve.tensor_tensor_scan(cum[:, :], ones[:, :], nl[:, :], 0.0, ALU.mult, ALU.add
                                       ).then_inc(dve_done, 1)

    cos_t = at("cos_t", [P, T], F32, T_OFF + 8192)
    sin_t = at("sin_t", [P, T], F32, T_OFF + 12288)

    class Rotary:
        def __init__(self, ctx, tag):
            self.pos_i = at(f"{tag}_posi", [P, T], I32, B_OFF)
            self.ang, self.turns, self.red, self.half = (
                at(f"{tag}_{n}", [P, T], F32, B_OFF + 4096 * (i + 1)) for i, n in enumerate("ang turns red half".split()))
            self.freq = at(f"{tag}_freq", [P, 2], F32, B_OFF + 20480)
            self.loaded, self.stepped, self.sines_done = sems(ctx, tag, "rot_in rot_step sines")

        def load(self, sp):
            sp.dma_start(self.pos_i[:, :], positions.broadcast_to([P, T])).then_inc(self.loaded, 16)
            sp.dma_start(self.freq[:, :], consts[:, K_FREQ:K_FREQ + 2]).then_inc(self.loaded, 16)

        def tables(self, dve):
            two_pi = (6.28125, 0.00193500518798828125, 3.0199159819567e-7)
            rounder = 1.5 * 2.0 ** 23
            ang, turns, red, half, freq = self.ang, self.turns, self.red, self.half, self.freq
            n = [0]

            def then(ins):
                n[0] += 1
                ins.then_inc(self.stepped, 1)
                dve.wait_ge(self.stepped, n[0])
            dve.wait_ge(self.loaded, 32)
            then(dve.tensor_copy(ang[:, :], self.pos_i[:, :]))
            then(dve.tensor_scalar(ang[:, :], ang[:, :], freq[:, 0:1], None, ALU.mult))
            then(dve.tensor_scalar(turns[:, :], ang[:, :], 1.0 / (2 * np.pi), rounder, ALU.mult, ALU.add))
            then(dve.tensor_scalar(turns[:, :], turns[:, :], -rounder, None, ALU.add))
            then(dve.scalar_tensor_tensor(red[:, :], turns[:, :], -two_pi[0], ang[:, :], ALU.mult, ALU.add))
            then(dve.scalar_tensor_tensor(red[:, :], turns[:, :], -two_pi[1], red[:, :], ALU.mult, ALU.add))
            then(dve.scalar_tensor_tensor(red[:, :], turns[:, :], -two_pi[2], red[:, :], ALU.mult, ALU.add))
            then(dve.tensor_scalar(red[:, :], red[:, :], 3.141592, -3.141592, ALU.min, ALU.max))
            dve.wait_ge(self.sines_done, 2)
            then(dve.tensor_scalar(sin_t[:, :], sin_t[:, :], freq[:, 1:2], None, ALU.mult))
            then(dve.tensor_tensor(half[:, :], half[:, :], half[:, :], ALU.mult))
            then(dve.tensor_scalar(cos_t[:, :], half[:, :], -2.0, 1.0, ALU.mult, ALU.add))

        def sines(self, act):
            act.wait_ge(self.stepped, 8)
            act.activation(sin_t[:, :], self.red[:, :], ACT.Sin).then_inc(self.sines_done, 1)
            act.activation(self.half[:, :], self.red[:, :], ACT.Sin, scale=0.5).then_inc(self.sines_done, 1)

    def attention(tag, w_in, width, n_pairs, fox, first_weights):
        def b(n, name, shape=(P, T)):
            return at(f"{tag}_{name}", list(shape), F32, B_OFF + 32768 + 4096 * n)
        q = [b(0, "q0"), b(1, "q1")]
        k = [b(2, "k0"), b(3, "k1")]
        v = [b(4, "v0", (P, TT, P)), b(5, "v1", (P, TT, P))]
        stage = b(6, "stage")
        logit = [b(7, "logit0"), b(8, "logit1")]
        prob = [b(9, "prob0"), b(10, "prob1")]
        extra = b(11, "extra", (P, 2, T))
        o_sb = b(13, "o", (P, TT, P))
        probt = [at(f"{tag}_probt{n}", [P, T], F32, T_OFF + 4096 * n) for n in range(2)]
        swap = at(f"{tag}_swap", [P, T], F32, T_OFF + 16384)
        raw, whi, wlo, zero = first_weights.raw[0], first_weights.whi, first_weights.wlo, first_weights.zero
        raw_in, w_full, split_hi = first_weights.raw_in[0], first_weights.w_full[0], first_weights.split_hi
        mask_b = at(f"{tag}_maskb", [P, P], BF16, C_OFF + 2688)
        ident_b = at(f"{tag}_identb", [P, P], BF16, C_OFF + 2944)
        mask_f = at(f"{tag}_maskf", [P, P], F32, C_OFF + 3520)
        small = at(f"{tag}_small", [P, 3, 16], F32, C_OFF + 3200)
        carrier = at(f"{tag}_carrier", [P, 16], F32, C_OFF + 3424)
        shift, den, rden = small[:, 0, :], small[:, 1, :], small[:, 2, :]
        wv = w_in.rearrange("(k p) n -> p k n", p=P)
        units = 2 * TT
        PROJ, OUT = 6, 7
        share = (3, 3, 2, 4, 4, 3, 3, 2, 4, 4, 3, 3, 2, 3, 3, 2)
        done_by = [sum(share[:u]) for u in range(units + 1)]
        ends = {u: done_by[u + 1] // KT - 1 for u in range(units) if done_by[u + 1] % KT == 0}
        rotations = {6: ("a", 0), 8: ("b", 0), 11: ("a", 1), 12: ("b", 1)}
        assert done_by[units] == 6 * KT
        q_scale = ATT_SCALE if fox else 1.0
        with ExitStack() as ctx:
            (proj, proj_read, v_turn, v_new,
             s_full, biased, probs, counted, turned, turned_read, o_full, o_ready, o_turn, y_ready,
             recips, mask_in, mask_ready, swapped, rot1, rot2, rot3, rot_zero) = sems(
                ctx, tag, "proj proj_read v_turn v_new "
                "s_full biased probs counted turned turned_read o_full o_ready o_turn "
                "y_ready recips mask_in mask_ready swapped rot1 rot2 rot3 rot_zero")
            gate_in = sems(ctx, tag, "gate0 gate1")
            rotary = None if fox else Rotary(ctx, tag)
            block = ctx.enter_context(nc.Block())

            def for_pairs(engine, pair_step):
                with engine.Fori(0, n_pairs // 2 - 1) as c:
                    pair_step(c * 2, 0, c * 2 + 1)
                    pair_step(c * 2 + 1, 1, c * 2 + 2)
                pair_step(n_pairs - 2, 0, n_pairs - 1)
                pair_step(n_pairs - 1, 1, None)

            def first(pair, u=0):
                return isinstance(pair, int) and pair == 0 and u == 0

            @block.sync
            def _(sp):
                def weights(pair):
                    for t in range(3):
                        col = sp.snap(pair * P + t * width)
                        sp.compute_val(col * 4)
                        sp.wait_ge(w_full, pair * 3 + t)
                        sp.dma_start(raw[:, :, :], wv[:, :, ds(col, P)]).then_inc(raw_in, 16)

                def gates(pair, e):
                    row = sp.snap(pair * 2 + e)
                    if not first(pair):
                        sp.wait_ge(biased, pair * units + (8 * e - 8))
                    sp.dma_start(extra[:, e, :], negc_dram[ds(row, 1), :].broadcast_to([P, T])
                                 ).then_inc(gate_in[e], 16)

                if fox:
                    gates(0, 0)
                    gates(0, 1)
                    sp.dma_start(mask_f[:, :], consts[:, K_CAUS:K_CAUS + P]).then_inc(mask_in, 16)
                else:
                    rotary.load(sp)
                    sp.dma_start(extra[:, :, :], dil).then_inc(mask_in, 16)
                weights(1)
                with sp.Fori(1, n_pairs - 1) as pair:
                    if fox:
                        gates(pair, 0)
                    weights(pair + 1)
                    if fox:
                        gates(pair, 1)
                if fox:
                    for e in range(2):
                        gates(n_pairs - 1, e)

            @block.gpsimd
            def _(pool):
                def split(pair, t):
                    pool.wait_ge(raw_in, (pair * 3 + t + 1) * 16)
                    split_weights(pool, raw[:, :, :], whi[t][:, :, :], wlo[t][:, :, :], zero,
                                  split_hi, pair * 3 + t + 1, w_full)
                with pool.Fori(1, n_pairs) as pair:
                    for t in range(3):
                        pool.wait_ge(proj, pair * 6 + (2 * t - 4))
                        split(pair, t)

            @block.tensor
            def _(pe):
                def fill(pair, lo, hi):
                    for step in range(lo, hi):
                        f, ch = step // KT, step % KT
                        t, h = f // 2, f % 2
                        if ch == 0:
                            if not h:
                                pe.wait_ge(w_full, pair * 3 + t + 1)
                            if not first(pair, f):
                                pe.wait_ge(proj_read, pair * 6 + f)
                            if f == 0 and not first(pair):
                                pe.wait_ge(y_ready, pair - 1)
                        mm = project_half(pe, psum[:, PROJ, :], whi[t], wlo[t], h_hi, h_lo, h, [ch])
                        if ch == KT - 1:
                            mm.then_inc(proj, 1)

                def turn_v(pair, before):
                    pe.wait_ge(proj_read, pair * 6 + 6)
                    if before is not None:
                        pe.wait_ge(turned_read, before * units + units)
                    for n in range(TT):
                        tr = pe.transpose(psum[:, 4 + n // 4, (n % 4) * P:(n % 4 + 1) * P],
                                          stage[:, n * P:(n + 1) * P], ident[:, :])
                    tr.then_inc(v_turn, 1)

                def scores(pair, par, u):
                    e, qt = u // TT, u % TT
                    if u == 0:
                        if fox:
                            pe.wait_ge(proj_read, pair * 6 + 4)
                        else:
                            pe.wait_ge(rot3, pair * 2 + 2)
                    if u >= 2 or not first(pair):
                        pe.wait_ge(biased, pair * units + (u - 1))
                    nk = (qt + 1) * P
                    rows = slice(e * HD, (e + 1) * HD)
                    for c in range(0, nk, HALF):
                        n = min(HALF, nk - c)
                        diag = fox and c + n == nk
                        mm = pe.matmul(psum[:, 2 * (u % 2) + c // HALF, 0:n], q[par][rows, qt * P:(qt + 1) * P],
                                       k[par][rows, c:c + n], start=True, stop=not diag)
                    if fox:
                        mm = pe.matmul(psum[:, 2 * (u % 2) + c // HALF, n - P:n], ident_b[:, :], mask_b[:, :],
                                       start=False, stop=True)
                    mm.then_inc(s_full, 1)

                def turn(pair, u):
                    pe.wait_ge(probs if fox else counted, pair * units + (u + 1))
                    pe.wait_ge(turned_read, pair * units + u)
                    if u == 0:
                        pe.wait_ge(v_new, pair + 1)
                    for n in range(u % TT + 1):
                        tr = pe.transpose(psum[:, 4 + n // 4, (n % 4) * P:(n % 4 + 1) * P],
                                          prob[u % 2][:, n * P:(n + 1) * P], ident[:, :])
                    tr.then_inc(turned, 1)

                def weigh(pair, par, u):
                    e, qt = u // TT, u % TT
                    pe.wait_ge(turned_read, pair * units + (u + 1))
                    pe.wait_ge(o_ready, pair * units + u)
                    if u == 0:
                        pe.wait_ge(y_ready, pair)
                    for n in range(qt + 1):
                        mm = pe.matmul(psum[:, OUT, 0:HD], probt[u % 2][:, n * P:(n + 1) * P],
                                       v[par][:, n, e * HD:(e + 1) * HD], start=(n == 0), stop=(n == qt))
                    mm.then_inc(o_full, 1)

                def pair_step(pair, par, following):
                    for u in range(units):
                        if u + 2 < units:
                            scores(pair, par, u + 2)
                        elif following is not None:
                            scores(following, 1 - par, u + 2 - units)
                        middle = done_by[u] + (share[u] + 1) // 2
                        if following is not None and u < units - 1:
                            fill(following, done_by[u], middle)
                        turn(pair, u)
                        if following is not None:
                            fill(following, middle if u < units - 1 else done_by[u], done_by[u + 1])
                        if u:
                            weigh(pair, par, u - 1)
                    weigh(pair, par, units - 1)
                    if following is not None:
                        turn_v(following, pair)
                    pe.wait_ge(o_ready, pair * units + units)
                    if following is not None:
                        pe.wait_ge(proj_read, following * 6 + 6)
                    for n in range(TT):
                        tr = pe.transpose(psum[:, PROJ + n // 4, (n % 4) * P:(n % 4 + 1) * P],
                                          o_sb[:, n, :], ident[:, :])
                    tr.then_inc(o_turn, 1)

                fill(0, 0, 4 * KT)
                if fox:
                    pe.wait_ge(mask_ready, 2)
                scores(0, 0, 0)
                scores(0, 0, 1)
                fill(0, 4 * KT, 6 * KT)
                turn_v(0, None)
                for_pairs(pe, pair_step)

            @block.scalar
            def _(act):
                def take(pair, par, f):
                    t, h = f // 2, f % 2
                    cols = slice(h * HALF, (h + 1) * HALF)
                    act.wait_ge(proj, pair * 6 + (f + 1))
                    dst = stage
                    if fox and t < 2:
                        dst = (q, k)[t][par]
                        if f == 0 and not first(pair):
                            act.wait_ge(s_full, (pair - 1) * units)
                    elif h == 0 and (fox or t == 0):
                        act.wait_ge(v_turn, pair)
                    elif h == 0:
                        act.wait_ge(rot1, pair * 2 + t)
                        act.wait_ge(swapped, pair * 128 + 64 * t)
                    act.activation(dst[:, cols], psum[:, PROJ, :], ACT.Copy,
                                   scale=(q_scale if t == 0 else 1.0)).then_inc(proj_read, 1)
                    if not fox and t < 2 and h:
                        act.wait_ge(proj_read, pair * 6 + (f + 1))
                        act.wait_ge(rot3, pair * 2 + t)
                        for to, of in ((0, 8), (8, 0), (64, 72), (72, 64)):
                            act.dma_start(swap[to:to + 8, :], stage[of:of + 8, :]).then_inc(swapped, 16)

                def take_v(pair, par):
                    act.wait_ge(v_turn, pair + 1)
                    if not first(pair):
                        act.wait_ge(o_full, (pair - 1) * units)
                    act.activation(v[par][:, :, :].rearrange("p n c -> p (n c)"),
                                   psum[:, 4:6, :].rearrange("p b n -> p (b n)"), ACT.Copy).then_inc(v_new, 1)

                def exp(pair, u):
                    nk = (u % TT + 1) * P
                    act.wait_ge(biased, pair * units + (u + 1))
                    if u == 1:
                        act.wait_ge(turned, pair * units)
                        act.wait_ge(o_ready, pair * units)
                    elif u or not first(pair):
                        act.wait_ge(turned, pair * units + (u - 1))
                        act.wait_ge(o_ready, pair * units + (u - 2))
                    act.activation(prob[u % 2][:, 0:nk], logit[u % 2][:, 0:nk], ACT.Exp, scale=-1.0,
                                   bias=shift[:, u:u + 1],
                                   **({"accum_out": den[:, u:u + 1]} if fox else {})).then_inc(probs, 1)

                def pair_step(pair, par, following):
                    for u in range(units):
                        if following is not None and u - 1 in ends:
                            take(following, 1 - par, ends[u - 1])
                        if u + 1 < units:
                            exp(pair, u + 1)
                        elif following is not None:
                            exp(following, 0)
                        act.wait_ge(turned, pair * units + (u + 1))
                        act.wait_ge(o_full, pair * units + max(u - 1, 0))
                        nk = (u % TT + 1) * P
                        act.activation(probt[u % 2][:, 0:nk],
                                       psum[:, 4:6, :].rearrange("p b n -> p (b n)")[:, 0:nk],
                                       ACT.Copy).then_inc(turned_read, 1)
                    if following is not None:
                        take(following, 1 - par, 5)
                        take_v(following, 1 - par)
                    act.wait_ge(o_turn, pair + 1)
                    act.activation(y_buf[:, pair, :], psum[:, PROJ:PROJ + 2, :].rearrange("p b n -> p (b n)"),
                                   ACT.Copy).then_inc(y_ready, 1)

                if fox:
                    act.wait_ge(mask_in, 16)
                    act.activation(mask_b[:, :], mask_f[:, :], ACT.Copy).then_inc(mask_ready, 1)
                    act.activation(ident_b[:, :], ident[:, :], ACT.Copy).then_inc(mask_ready, 1)
                else:
                    act.wait_ge(rot_zero, 1)
                for f in range(6):
                    take(0, 0, f)
                    if f == 1 and not fox:
                        rotary.sines(act)
                exp(0, 0)
                take_v(0, 0)
                for_pairs(act, pair_step)

            @block.vector
            def _(dve):
                def rotate_a(pair, par, t):
                    dve.wait_ge(proj_read, pair * 6 + (2 * t + 2))
                    if not first(pair):
                        dve.wait_ge(s_full, (pair - 1) * units)
                    dst = (q, k)[t][par]
                    dve.tensor_tensor(dst[:, :], stage[:, :], cos_t[:, :], ALU.mult).then_inc(rot1, 1)

                def rotate_b(pair, par, t):
                    dst = (q, k)[t][par]
                    dve.wait_ge(swapped, pair * 128 + 64 * (t + 1))
                    dve.tensor_tensor(swap[:, :], swap[:, :], sin_t[:, :], ALU.mult).then_inc(rot2, 1)
                    dve.wait_ge(rot2, pair * 2 + t + 1)
                    dve.wait_ge(rot1, pair * 2 + t + 1)
                    dve.tensor_tensor(dst[:, :], dst[:, :], swap[:, :], ALU.add).then_inc(rot3, 1)

                def bias(pair, u):
                    e, qt = u // TT, u % TT
                    nk = (qt + 1) * P
                    dve.wait_ge(s_full, pair * units + (u + 1))
                    if u >= 1:
                        dve.wait_ge(probs, pair * units + (u - 1))
                    elif not first(pair):
                        dve.wait_ge(probs, pair * units - 1)
                    if fox and qt == 0:
                        dve.wait_ge(gate_in[e], pair * 16 + 16)
                    if u == 0:
                        dve.wait_ge(mask_in, 16)
                    dve.memset(carrier[:, u:u + 1], 0.0)
                    more = extra[:, e, 0:nk] if fox else extra[:, 0, (TT - 1 - qt) * P:T]
                    s = psum[:, 2 * (u % 2):2 * (u % 2) + 2, :].rearrange("p b n -> p (b n)")[:, 0:nk]
                    dve.tensor_tensor_reduce(out=logit[u % 2][:, 0:nk], in0=s, in1=more,
                                             scale=(-1.0 if fox else -ATT_SCALE), scalar=3.0e38,
                                             op0=ALU.add, op1=ALU.min,
                                             accum_out=shift[:, u:u + 1]).then_inc(biased, 1)

                def count(pair, u):
                    qt = u % TT
                    nk = (qt + 1) * P
                    dve.wait_ge(probs, pair * units + (u + 1))
                    dve.tensor_tensor_reduce(out=prob[u % 2][:, 0:nk], in0=prob[u % 2][:, 0:nk],
                                             in1=extra[:, 1, (TT - 1 - qt) * P:T], scale=1.0, scalar=0.0,
                                             op0=ALU.mult, op1=ALU.add,
                                             accum_out=den[:, u:u + 1]).then_inc(counted, 1)

                def norm_out(pair, u):
                    e, qt = u // TT, u % TT
                    dve.wait_ge(probs if fox else counted, pair * units + (u + 1))
                    dve.reciprocal(rden[:, u:u + 1], den[:, u:u + 1]).then_inc(recips, 1)
                    dve.wait_ge(recips, pair * units + (u + 1))
                    if u == 0:
                        dve.wait_ge(o_turn, pair)
                    dve.wait_ge(o_full, pair * units + (u + 1))
                    dve.tensor_scalar(o_sb[:, qt, e * HD:(e + 1) * HD], psum[:, OUT, 0:HD],
                                      rden[:, u:u + 1], None, ALU.mult).then_inc(o_ready, 1)

                def pair_step(pair, par, following):
                    for u in range(units):
                        if not fox:
                            count(pair, u)
                        if u >= 2:
                            norm_out(pair, u - 2)
                        if u + 1 < units:
                            bias(pair, u + 1)
                        elif following is not None:
                            bias(following, 0)
                        if not fox and following is not None and u in rotations:
                            part, t = rotations[u]
                            (rotate_a if part == "a" else rotate_b)(following, 1 - par, t)
                    norm_out(pair, units - 2)
                    norm_out(pair, units - 1)

                if not fox:
                    dve.memset(swap[:, :], 0.0).then_inc(rot_zero, 1)
                    rotary.tables(dve)
                    for t in range(2):
                        rotate_a(0, 0, t)
                        rotate_b(0, 0, t)
                bias(0, 0)
                for_pairs(dve, pair_step)
    z_buf = at("z_buf", [P, RWKV_IN // P, T], F32, B_OFF + 32768)
    Z_R, Z_K, Z_V, Z_LO, Z_G = 0, RW_T, 2 * RW_T, 3 * RW_T, 3 * RW_T + 1
    cum_buf = at("cum_buf", [P, RW_T, T], F32, A_OFF)
    nkk_buf = at("nkk_buf", [P, RW_T, T], F32, A_OFF + 16384)
    bb_buf = at("bb_buf", [P, RW_T, T], F32, A_OFF + 32768)

    def rwkv_project(tag):
        n_pairs = RWKV_IN // P // 2
        raw = [at(f"{tag}_raw{j}", [P, KT, P], F32, W_OFF + 4096 * j) for j in range(2)]
        whi = [at(f"{tag}_whi{j}", [P, KT, P], F32R, W_OFF + 8192 + 4096 * j) for j in range(2)]
        wlo = [at(f"{tag}_wlo{j}", [P, KT, P], F32R, W_OFF + 16384 + 4096 * j) for j in range(2)]
        zero = at(f"{tag}_zero", [P, 8], F32, W_OFF + 24576)
        z = [at(f"{tag}_z{j}", [P, T + 1], F32, T_OFF + 4128 * j) for j in range(2)]
        diff = [at(f"{tag}_diff{j}", [P, T], F32, T_OFF + 8256 + 4096 * j) for j in range(2)]
        w = w_in0.rearrange("(k p) n -> p k n", p=P)
        with ExitStack() as ctx:
            zeroed, pads, split_hi = sems(ctx, tag, "zeroed pads split_hi")
            raw_in = sems(ctx, tag, "raw0 raw1")
            w_full = sems(ctx, tag, "wfull0 wfull1")
            ps_full = sems(ctx, tag, "psfull0 psfull1")
            evac = sems(ctx, tag, "evac0 evac1")
            diffed = sems(ctx, tag, "diffed0 diffed1")
            mixed = sems(ctx, tag, "mixed0 mixed1")
            block = ctx.enter_context(nc.Block())

            @block.sync
            def _(sp):
                with sp.Fori(0, n_pairs) as c:
                    for j in range(2):
                        col = sp.snap(c * (2 * P) + (j * P + FOX_IN))
                        sp.compute_val(col * 4)
                        sp.wait_ge(w_full[j], c)
                        sp.dma_start(raw[j][:, :, :], w[:, :, ds(col, P)]).then_inc(raw_in[j], 16)

            @block.gpsimd
            def _(pool):
                pool.memset(zero[:, :], 0.0).then_inc(zeroed, 1)
                pool.wait_ge(zeroed, 1)
                with pool.Fori(0, n_pairs) as c:
                    for j in range(2):
                        pool.wait_ge(ps_full[j], c * 2)
                        pool.wait_ge(raw_in[j], c * 16 + 16)
                        split_weights(pool, raw[j][:, :, :], whi[j][:, :, :], wlo[j][:, :, :], zero,
                                      split_hi, c * 2 + j + 1, w_full[j])

            @block.tensor
            def _(pe):
                with pe.Fori(0, n_pairs) as c:
                    for j in range(2):
                        for h in range(2):
                            pe.wait_ge(evac[j], c * 2)
                            pe.wait_ge(w_full[j], c + 1)
                            project_half(pe, psum[:, 2 * j + h, :], whi[j], wlo[j], h_hi, h_lo, h
                                         ).then_inc(ps_full[j], 1)

            @block.scalar
            def _(act):
                with act.Fori(0, n_pairs) as c:
                    for j in range(2):
                        act.wait_ge(mixed[j], c)
                        for h in range(2):
                            act.wait_ge(ps_full[j], c * 2 + h + 1)
                            act.activation(z[j][:, 1 + h * HALF:1 + (h + 1) * HALF], psum[:, 2 * j + h, :],
                                           ACT.Copy).then_inc(evac[j], 1)

            @block.vector
            def _(dve):
                for j in range(2):
                    dve.memset(z[j][:, 0:1], 0.0).then_inc(pads, 1)
                dve.wait_ge(pads, 2)
                with dve.Fori(0, n_pairs) as c:
                    for j in range(2):
                        dve.wait_ge(evac[j], c * 2 + 2)
                        dve.tensor_tensor(diff[j][:, :], z[j][:, 0:T], z[j][:, 1:T + 1],
                                          ALU.subtract).then_inc(diffed[j], 1)
                        dve.wait_ge(diffed[j], c + 1)
                        dve.scalar_tensor_tensor(z_buf[:, c * 2 + j, :], diff[j][:, :],
                                                 vec[:, ds(c * 2 + (j + V_MU), 1)], z[j][:, 1:T + 1],
                                                 ALU.mult, ALU.add).then_inc(mixed[j], 1)

    def rwkv_prepare(tag):
        lora = at(f"{tag}_lora", [P, RWKV_W], F32, W_OFF)
        blk = at(f"{tag}_blk", [P, P], F32, W_OFF + 2048)
        reset = at(f"{tag}_reset", [P, HALF], F32, W_OFF + 2560)
        neg = at(f"{tag}_neg", [P, 2, RW_T], F32, W_OFF + 4608)
        sq, sig, iclr, norm_, rnorm, fac = ([at(f"{tag}_{n}{s}", [P, HALF], F32, T_OFF - 20480 + 4096 * i + 2048 * s)
                                             for s in range(2)] for i, n in enumerate(
            "sq sig iclr norm rnorm fac".split()))
        blocks = 2 * RW_T
        with ExitStack() as ctx:
            (loaded, loras, squared, lora_ps, sum_ps, sigs, iclrs, floors, roots, recips, scans,
             nkks, bbs, facs, ks, negs) = sems(
                ctx, tag, "loaded loras squared lora_ps sum_ps sigs iclrs floors roots recips scans "
                "nkks bbs facs ks negs")
            block = ctx.enter_context(nc.Block())

            @block.sync
            def _(sp):
                sp.dma_start(lora[0:64, :], w2).then_inc(loaded, 16)
                sp.dma_start(lora[64:128, :], a2).then_inc(loaded, 16)
                sp.dma_start(blk[:, :], consts[:, K_BLK:K_BLK + P]).then_inc(loaded, 16)
                sp.dma_start(reset[:, :], consts[:, K_RESET:K_RESET + HALF]).then_inc(loaded, 16)

            def place(n):
                ct, h = n // 2, n % 2
                return ct, slice(h * HALF, (h + 1) * HALF), n % 2

            @block.tensor
            def _(pe):
                pe.wait_ge(loaded, 64)
                pe.wait_ge(loras, 1)
                for n in range(blocks):
                    ct, cols, s = place(n)
                    if n >= 2:
                        pe.wait_ge(sigs, n - 1)
                        pe.wait_ge(iclrs, n - 1)
                        pe.wait_ge(floors, n - 1)
                    pe.matmul(psum[:, s, :], lora[0:64, ct * P:(ct + 1) * P], z_buf[0:64, Z_LO, cols],
                              start=True, stop=True)
                    pe.matmul(psum[:, 2 + s, :], lora[64:128, ct * P:(ct + 1) * P], z_buf[64:128, Z_LO, cols],
                              start=True, stop=True).then_inc(lora_ps, 1)
                    pe.wait_ge(squared, n + 1)
                    pe.matmul(psum[:, 4 + s, :], blk[:, :], sq[s][:, :], start=True, stop=True).then_inc(sum_ps, 1)

            @block.scalar
            def _(act):
                act.activation(z_buf[0:64, Z_LO, :], z_buf[0:64, Z_LO, :], ACT.Tanh).then_inc(loras, 1)
                act.activation(z_buf[:, Z_G, :], z_buf[:, Z_G, :], ACT.Sigmoid)
                for n in range(blocks):
                    ct, cols, s = place(n)
                    if n >= 2:
                        act.wait_ge(sum_ps, n - 1)
                        act.wait_ge(scans, n - 1)
                        act.wait_ge(facs, n - 1)
                        act.wait_ge(bbs, n - 1)
                    act.activation(sq[s][:, :], z_buf[:, Z_K + ct, cols], ACT.Square,
                                   scale=vec[:, V_KK + ct:V_KK + ct + 1]).then_inc(squared, 1)
                    act.wait_ge(lora_ps, n + 1)
                    act.activation(sig[s][:, :], psum[:, s, :], ACT.Sigmoid,
                                   bias=vec[:, V_W0 + ct:V_W0 + ct + 1]).then_inc(sigs, 1)
                    act.activation(iclr[s][:, :], psum[:, 2 + s, :], ACT.Sigmoid,
                                   bias=vec[:, V_A0 + ct:V_A0 + ct + 1]).then_inc(iclrs, 1)
                    act.wait_ge(iclrs, n + 1)
                    act.wait_ge(negs, 2)
                    if n >= 2:
                        act.wait_ge(ks, n - 1)
                    act.activation(fac[s][:, :], iclr[s][:, :], ACT.Identity, scale=vec[:, V_KA + ct:V_KA + ct + 1],
                                   bias=neg[:, 1, ct:ct + 1]).then_inc(facs, 1)
                    act.wait_ge(floors, n + 1)
                    act.activation(norm_[s][:, :], norm_[s][:, :], ACT.Sqrt).then_inc(roots, 1)

            @block.vector
            def _(dve):
                dve.tensor_scalar(neg[:, 0, :], vec[:, V_KK:V_KK + RW_T], -1.0, None, ALU.mult).then_inc(negs, 1)
                dve.tensor_scalar(neg[:, 1, :], vec[:, V_KA:V_KA + RW_T], -1.0, 1.0, ALU.mult, ALU.add
                                  ).then_inc(negs, 1)
                dve.wait_ge(negs, 2)
                dve.wait_ge(loaded, 64)
                for n in range(blocks):
                    ct, cols, s = place(n)
                    dve.wait_ge(sum_ps, n + 1)
                    if n >= 2:
                        dve.wait_ge(recips, n - 1)
                    dve.tensor_scalar(norm_[s][:, :], psum[:, 4 + s, :], 1e-24, None, ALU.max).then_inc(floors, 1)
                    dve.wait_ge(sigs, n + 1)
                    dve.tensor_tensor_scan(cum_buf[:, ct, cols], reset[:, :], sig[s][:, :], 0.0,
                                           ALU.mult, ALU.add).then_inc(scans, 1)
                    dve.wait_ge(roots, n + 1)
                    dve.reciprocal(rnorm[s][:, :], norm_[s][:, :]).then_inc(recips, 1)
                    dve.wait_ge(recips, n + 1)
                    dve.scalar_tensor_tensor(nkk_buf[:, ct, cols], z_buf[:, Z_K + ct, cols], neg[:, 0, ct:ct + 1],
                                             rnorm[s][:, :], ALU.mult, ALU.mult).then_inc(nkks, 1)
                    dve.wait_ge(nkks, n + 1)
                    dve.wait_ge(iclrs, n + 1)
                    dve.scalar_tensor_tensor(bb_buf[:, ct, cols], nkk_buf[:, ct, cols], -1.0, iclr[s][:, :],
                                             ALU.mult, ALU.mult).then_inc(bbs, 1)

            @block.gpsimd
            def _(pool):
                for n in range(blocks):
                    ct, cols, s = place(n)
                    pool.wait_ge(facs, n + 1)
                    pool.wait_ge(squared, n + 1)
                    pool.wait_ge(nkks, n + 1)
                    pool.tensor_tensor(z_buf[:, Z_K + ct, cols], z_buf[:, Z_K + ct, cols], fac[s][:, :],
                                       ALU.mult).then_inc(ks, 1)

    def rwkv_chunks(tag):
        regions = [[W_OFF, C_OFF], [A_OFF + 49152, B_OFF], [B_OFF + 16384, B_OFF + 32768],
                   [C_OFF + 2432, C_OFF + 7928]]

        def buf(name, shape, nbytes, copies=0, dt=F32):
            if copies:
                return [buf(f"{name}{n}", shape, nbytes) for n in range(copies)]
            for region in regions:
                if region[0] + nbytes <= region[1]:
                    t = at(f"{tag}_{name}", shape, dt, region[0])
                    region[0] += nbytes
                    return t
            raise ValueError(f"no room for {name}: {regions}")
        mx = buf("mx", [P, 2, 2, 4 * P], 8192, 2)
        tok = buf("tok", [P, 4, RWKV_W], 8192, 2)
        ar = buf("ar", [P, RW_T, 2, P], 4096, 2)
        xs = buf("x", [P, 2, 2, 2 * P], 4096)
        mask_lev = buf("mlev", [P, 5, P], 2560)
        e_in = buf("ein", [P, RW_T, 2, CHUNK + 1], 2112, 2)
        e_neg = buf("eneg", [P, RW_T, P], 2048)
        bt = buf("bt", [P, RW_T, P], 2048, 2)
        kt = buf("kt", [P, RW_T, P], 2048, 2)
        kh = buf("kh", [P, RW_T, P], 2048)
        vt = buf("vt", [P, RW_T, P], 2048)
        lsb = buf("l", [P, 2, 2, P], 2048)
        zt = buf("zt", [P, 2, 2, P], 2048)
        pq = buf("pq", [P, 2, 2, P], 2048)
        mt = buf("mt", [P, 2, 2, P], 2048)
        st = buf("st", [P, RW_T, 2, HD], 2048)
        ysb = buf("y", [P, N_RWKV, HD], 2048)
        sqn = buf("sqn", [P, N_RWKV, HD], 2048)
        akv = buf("akv", [P, 2, 2, HD], 1024)
        gt = buf("gt", [P, 2, P], 1024)
        mask_ab = buf("mab", [P, 2 * P], 1024)
        mask_1 = buf("m1", [P, 2 * P], 1024)
        mask_l = buf("ml", [P, P], 512)
        id64 = buf("id64", [P, HD], 256)
        ident_b = buf("identb", [P, 2 * P], 512, dt=BF16)
        stat = buf("stat", [P, 3, N_RWKV], 96)
        carrier = buf("carrier", [P, 4], 16)
        bh = e_neg
        with ExitStack() as ctx:
            (consts_in, zeroed, exp_in, exp_neg, v_copied, prepared, hats, t_turned, toks,
             ab, mxs, ls, ones_in, x0a, x0, akv_ps, akv_sb, z_ps, zts, xx_ps, x_new, pq_ps, pqs, mn0_ps, mn_ps, gts, mts,
             y0_ps, ms0_ps, ms1_ps, st1s, st0s, ys, sums, centred, squares, varis, roots, rrs, normed,
             y_turned, y_out) = sems(
                ctx, tag, "consts_in zeroed exp_in exp_neg v_copied prepared hats t_turned toks "
                "ab mxs ls ones_in x0a x0 akv_ps akv_sb z_ps zts xx_ps x_new pq_ps pqs mn0_ps mn_ps gts mts "
                "y0_ps ms0_ps ms1_ps st1s st0s ys sums centred squares varis roots rrs normed "
                "y_turned y_out")
            block = ctx.enter_context(nc.Block())
            per_e = [slice(0, HD), slice(HD, P)]
            halves = "p (e t) -> p e t"

            def for_groups(engine, step):
                for g in range(2):
                    step(g, g, 0, 0, first=True)
                with engine.Fori(0, TT // 2 - 1) as c:
                    for m in range(4):
                        step(c * 4 + (2 + m), m % 2, c * 2 + (1 + m // 2), (1 + m // 2) % 2)
                for g in range(2):
                    step(2 * TT - 2 + g, g, TT - 1, (TT - 1) % 2, last=True)

            @block.sync
            def _(sp):
                for dst, col, n in ((mask_ab, K_AB, 2 * P), (mask_l, K_L, P), (mask_1, K_M1, 2 * P),
                                    (id64, K_ID64, HD)):
                    sp.dma_start(dst[:, :], consts[:, col:col + n]).then_inc(consts_in, 16)
                sp.dma_start(mask_lev[:, :, :], consts[:, K_LEV:K_LEV + 5 * P].rearrange("p (l n) -> p l n", l=5)
                             ).then_inc(consts_in, 16)

            @block.scalar
            def _(act):
                def wait_here(n):
                    act.activation(carrier[:, n:n + 1], cst[:, 1:2], ACT.Copy)

                def prepare(i, slot):
                    cols = ds(i * P, P)
                    if not isinstance(i, int) or i:
                        act.wait_ge(mts, i * 4 - 4)
                        act.wait_ge(prepared, i * 4)
                        act.wait_ge(t_turned, i * 4)
                    wait_here(0)
                    src = cum_buf[:, :, cols].rearrange("p c (j t) -> p c j t", j=2)
                    act.activation(e_in[slot][:, :, :, 1:CHUNK + 1], src, ACT.Exp, scale=-DECAY).then_inc(exp_in, 1)
                    act.activation(e_neg[:, :, :], cum_buf[:, :, cols], ACT.Exp, scale=DECAY).then_inc(exp_neg, 1)
                    act.activation(vt[:, :, :], z_buf[:, Z_V:Z_V + RW_T, cols], ACT.Copy).then_inc(v_copied, 1)

                def take_tok(i, slot, m):
                    act.wait_ge(t_turned, i * 4 + (m + 1))
                    act.activation(tok[slot][:, m, :], psum[:, m % 2, :], ACT.Copy).then_inc(toks, 1)

                def take_pq(G):
                    for s in range(2):
                        act.wait_ge(pq_ps, G * 2 + (s + 1))
                        act.activation(pq[:, s, :, :], psum[:, 2 + s, 0:2 * P].rearrange(halves, e=2),
                                       ACT.Copy).then_inc(pqs, 1)

                def take_y(G, g):
                    for s in range(2):
                        act.wait_ge(st0s, G * 2 + (s + 1))
                        act.activation(ysb[:, 4 * g + 2 * s:4 * g + 2 * s + 2, :],
                                       psum[:, 2 + s, 3 * P:4 * P].rearrange(halves, e=2), ACT.Copy
                                       ).then_inc(ys, 1)

                def norm_squares(i):
                    act.wait_ge(centred, i + 1)
                    act.wait_ge(y_turned, i)
                    act.activation(sqn[:, :, :], ysb[:, :, :], ACT.Square).then_inc(squares, 1)

                def norm_root(i):
                    act.wait_ge(varis, i + 1)
                    act.activation(stat[:, 2, :], stat[:, 1, :], ACT.Sqrt, scale=1.0 / HD, bias=cst[:, 1:2]
                                   ).then_inc(roots, 1)

                def take_out(i):
                    act.wait_ge(y_turned, i + 1)
                    wait_here(1)
                    act.activation(cum_buf[:, :, ds(i * P, P)], psum[:, 2, :].rearrange("p (c t) -> p c t", c=RW_T),
                                   ACT.Copy).then_inc(y_out, 1)

                def step(G, g, i, slot, first=False, last=False):
                    tail = not (first and g == 0)
                    norms = g == 1 and not first
                    prepares = g == 1 and not last
                    if tail:
                        take_pq(G - 1)
                    for lev in range(5):
                        for s in range(2):
                            act.wait_ge(xx_ps, G * 10 + (2 * lev + s + 1))
                            part = slice(0, 2 * P) if lev < 4 else slice(P, 2 * P)
                            act.activation(xs[:, s, :, part],
                                           psum[:, 5 + 2 * s, :].rearrange(halves, e=2)[:, :, part],
                                           ACT.Copy).then_inc(x_new, 1)
                        if lev == 1:
                            for s in range(2):
                                act.wait_ge(akv_ps, G * 2 + (s + 1))
                                act.activation(akv[:, s, :, :], psum[:, s, 0:P].rearrange(halves, e=2),
                                               ACT.Copy).then_inc(akv_sb, 1)
                        if prepares and lev == 0:
                            prepare(i + 1, 1 - slot)
                        if norms and lev == 0:
                            norm_squares(i - 1)
                        if norms and lev == 2:
                            norm_root(i - 1)
                        if prepares and lev == 3:
                            take_tok(i + 1, 1 - slot, 0)
                            take_tok(i + 1, 1 - slot, 1)
                    if prepares:
                        take_tok(i + 1, 1 - slot, 2)
                    if tail:
                        if norms:
                            act.wait_ge(normed, i)
                        take_y(G - 1, 1 - g)
                    if prepares:
                        take_tok(i + 1, 1 - slot, 3)
                    if norms:
                        take_out(i - 1)

                for n in range(2):
                    act.activation(ident_b[:, n * P:(n + 1) * P], ident[:, :], ACT.Copy).then_inc(ones_in, 1)
                prepare(0, 0)
                for m in range(4):
                    take_tok(0, 0, m)
                for_groups(act, step)
                take_pq(2 * TT - 1)
                take_y(2 * TT - 1, 1)
                norm_squares(TT - 1)
                norm_root(TT - 1)
                take_out(TT - 1)

            @block.gpsimd
            def _(pool):
                def split(a):
                    return a.rearrange("p c (j t) -> p c j t", j=2)

                def prepare(i, slot):
                    cols = ds(i * P, P)
                    pool.wait_ge(exp_neg, i + 1)
                    if not isinstance(i, int) or i:
                        pool.wait_ge(t_turned, i * 4)
                    pool.tensor_tensor(split(ar[slot][:, :, 0, :]), split(nkk_buf[:, :, cols]),
                                       e_in[slot][:, :, :, 0:CHUNK], ALU.mult).then_inc(prepared, 1)
                    pool.tensor_tensor(bt[slot][:, :, :], bb_buf[:, :, cols], e_neg[:, :, :], ALU.mult
                                       ).then_inc(prepared, 1)
                    pool.tensor_tensor(kt[slot][:, :, :], z_buf[:, Z_K:Z_K + RW_T, cols], e_neg[:, :, :], ALU.mult
                                       ).then_inc(prepared, 1)
                    w_end = e_in[slot][:, :, :, CHUNK:CHUNK + 1].broadcast_to([P, RW_T, 2, CHUNK])
                    for n, (dst, src) in enumerate(((bh, bt), (kh, kt))):
                        pool.wait_ge(prepared, i * 4 + 3)
                        pool.tensor_tensor(split(dst[:, :, :]), split(src[slot][:, :, :]), w_end, ALU.mult
                                           ).then_inc(hats, 1)
                    pool.tensor_tensor(split(ar[slot][:, :, 1, :]), split(z_buf[:, Z_R:Z_R + RW_T, cols]),
                                       e_in[slot][:, :, :, 1:CHUNK + 1], ALU.mult).then_inc(prepared, 1)

                def step(G, g, i, slot, first=False, last=False):
                    if g == 1 and not last:
                        prepare(i + 1, 1 - slot)

                pool.wait_ge(consts_in, 80)
                pool.wait_ge(zeroed, 4)
                prepare(0, 0)
                for_groups(pool, step)

            @block.vector
            def _(dve):
                def to_pair(mask):
                    return mask.rearrange(halves, e=1).broadcast_to([P, 2, P])

                def first_x(G, s):
                    n = G * 2 + s
                    own = psum[:, 4 + 2 * s:6 + 2 * s, 0:P]
                    dve.tensor_tensor(xs[:, s, :, 0:P], own, to_pair(mask_1[:, 0:P]), ALU.mult).then_inc(x0a, 1)
                    dve.tensor_tensor(lsb[:, s, :, :], own, to_pair(mask_l[:, :]), ALU.mult).then_inc(ls, 1)
                    dve.wait_ge(x0a, n * 2 + 2)
                    for m in (1, 0):
                        part = xs[:, s, :, m * P:(m + 1) * P]
                        dve.tensor_tensor(part, part, to_pair(ident[:, :]), ALU.add).then_inc(x0, 1)

                def first_x_t(G, s):
                    dve.wait_ge(ab, G * 2 + (s + 1))
                    if not isinstance(G, int) or G >= 1:
                        dve.wait_ge(pq_ps, G * 2 - 1 + s)
                    dve.tensor_tensor(xs[:, s, :, P:2 * P], psum[:, 0:2, 0:P], to_pair(mask_1[:, P:2 * P]),
                                      ALU.mult).then_inc(x0a, 1)

                def take_scores(G, g, s):
                    if not isinstance(G, int) or G >= 2:
                        dve.wait_ge(ms1_ps, G * 2 - 2)
                    dve.tensor_tensor(mx[g][:, s, :, :].rearrange("p e (m t) -> p (e m) t", m=2),
                                      psum[:, 0:2, :].rearrange("p e (m t) -> p (e m) t", m=2),
                                      mask_ab[:, :].rearrange(halves, e=1).broadcast_to([P, 4, 2 * P]),
                                      ALU.mult).then_inc(mxs, 1)

                def transfer(G, g, slot, s):
                    n, pr = G * 2 + s, 2 * g + s
                    dve.wait_ge(mn_ps, n + 1)
                    dve.tensor_tensor(gt[:, s, :], psum[:, 2 + s, 2 * P:3 * P], ar[slot][:, pr, 1, :], ALU.add
                                      ).then_inc(gts, 1)
                    for j in range(2):
                        for e in range(2):
                            ins = dve.scalar_tensor_tensor(
                                mt[per_e[e], s, j, per_e[e]], id64[per_e[e], :],
                                e_in[slot][per_e[e], pr, j, CHUNK:CHUNK + 1],
                                psum[per_e[e], 2 + s, j * P:j * P + HD], ALU.mult, ALU.add)
                    ins.then_inc(mts, 1)

                def state(G, g, s, j):
                    n, pr = G * 2 + s, 2 * g + s
                    dve.wait_ge((ms0_ps, ms1_ps)[j], n + 1)
                    dve.tensor_copy(st[:, pr, 1 - j, :], psum[:, 2 + s, j * P + HD:(j + 1) * P]
                                    ).then_inc((st1s, st0s)[j], 1)

                def norm_a(i):
                    dve.wait_ge(ys, i * 4 + 4)
                    dve.tensor_reduce(stat[:, 0, :], ysb[:, :, :], AX_X, ALU.add).then_inc(sums, 1)
                    dve.wait_ge(sums, i * 2 + 1)
                    dve.tensor_scalar(stat[:, 0, :], stat[:, 0, :], 1.0 / HD, None, ALU.mult).then_inc(sums, 1)
                    dve.wait_ge(sums, i * 2 + 2)
                    mean = stat[:, 0, :].rearrange("p (h o) -> p h o", o=1).broadcast_to([P, N_RWKV, HD])
                    dve.tensor_tensor(ysb[:, :, :], ysb[:, :, :], mean, ALU.subtract).then_inc(centred, 1)

                def norm_b(i):
                    dve.wait_ge(squares, i + 1)
                    dve.tensor_reduce(stat[:, 1, :], sqn[:, :, :], AX_X, ALU.add).then_inc(varis, 1)

                def norm_c(i):
                    dve.wait_ge(roots, i + 1)
                    dve.reciprocal(stat[:, 2, :], stat[:, 2, :]).then_inc(rrs, 1)
                    dve.wait_ge(rrs, i + 1)
                    rstd = stat[:, 2, :].rearrange("p (h o) -> p h o", o=1).broadcast_to([P, N_RWKV, HD])
                    dve.wait_ge(centred, i + 1)
                    dve.wait_ge(varis, i + 1)
                    dve.tensor_tensor(sqn[:, :, :], ysb[:, :, :], rstd, ALU.mult).then_inc(normed, 1)

                def step(G, g, i, slot, first=False, last=False):
                    tail = not (first and g == 0)
                    before = (G - 1, 1 - g, slot if g else 1 - slot)
                    norms = g == 1 and not first
                    first_x_t(G, 0)
                    take_scores(G, g, 0)
                    first_x(G, 0)
                    first_x_t(G, 1)
                    first_x(G, 1)
                    for lev in range(5):
                        for s in range(2):
                            dve.wait_ge(z_ps, G * 10 + (2 * lev + s + 1))
                            dve.tensor_tensor(
                                zt[:, s, :, :], psum[:, 4 + 2 * s, 0:2 * P].rearrange(halves, e=2),
                                to_pair(mask_lev[:, lev, :]), ALU.mult).then_inc(zts, 1)
                            if lev == 0 and s == 0:
                                take_scores(G, g, 1)
                                if tail:
                                    transfer(*before, 0)
                        if tail and lev == 1:
                            transfer(*before, 1)
                        if tail and lev == 2:
                            for s in range(2):
                                state(*before[:2], s, 0)
                        if tail and lev >= 3:
                            state(*before[:2], lev - 3, 1)
                        if norms:
                            if lev == 0:
                                norm_a(i - 1)
                            if lev == 1:
                                norm_b(i - 1)
                            if lev == 3:
                                norm_c(i - 1)

                for m in (st, mt):
                    dve.memset(m[:, :, :, :], 0.0).then_inc(zeroed, 1)
                for w in e_in:
                    dve.memset(w[:, :, :, 0:1], 1.0).then_inc(zeroed, 1)
                dve.wait_ge(zeroed, 4)
                dve.wait_ge(consts_in, 80)
                for_groups(dve, step)
                final = (2 * TT - 1, 1, (TT - 1) % 2)
                for s in range(2):
                    transfer(*final, s)
                for s in range(2):
                    state(*final[:2], s, 0)
                for s in range(2):
                    state(*final[:2], s, 1)
                norm_a(TT - 1)
                norm_b(TT - 1)
                norm_c(TT - 1)

            @block.tensor
            def _(pe):
                def mm(out, lhs, rhs, start=True, stop=True, **k):
                    return pe.matmul(out, lhs, rhs, start=start, stop=stop, **k)

                def turn_tok(i, slot, m):
                    src = (lambda ct: ar[slot][:, ct, 0, :], lambda ct: bh[:, ct, :],
                           lambda ct: kh[:, ct, :], lambda ct: vt[:, ct, :])[m]
                    ready, count = ((prepared, i * 4 + 1), (hats, i * 2 + 1), (hats, i * 2 + 2),
                                    (v_copied, i + 1))[m]
                    pe.wait_ge(ready, count)
                    if m >= 2:
                        pe.wait_ge(toks, i * 4 + (m - 1))
                    for ct in range(RW_T):
                        tr = pe.transpose(psum[:, m % 2, ct * P:(ct + 1) * P], src(ct), ident[:, :])
                    tr.then_inc(t_turned, 1)

                def scores(G, g, slot, s):
                    pr = 2 * g + s
                    for e in range(2):
                        rows = per_e[e]
                        both = ar[slot][rows, pr, :, :].rearrange("p m t -> p (m t)")
                        mm(psum[:, e, 0:2 * P], bt[slot][rows, pr, :], both)
                        mm(psum[:, e, 2 * P:4 * P], kt[slot][rows, pr, :], both)
                        last = mm(psum[:, 4 + 2 * s + e, 0:P], ar[slot][rows, pr, 0, :], bt[slot][rows, pr, :])
                    last.then_inc(ab, 1)

                def a_k_v(G, g, slot, s):
                    pr = 2 * g + s
                    pe.wait_ge(mxs, G * 2 + 2)
                    for e in range(2):
                        last = mm(psum[:, s, e * HD:(e + 1) * HD], mx[g][:, s, e, 2 * P:3 * P],
                                  tok[slot][:, 3, pr * P + e * HD:pr * P + (e + 1) * HD])
                    last.then_inc(akv_ps, 1)

                def solve(G, g, slot, s):
                    pr = 2 * g + s
                    pe.wait_ge(x_new, G * 10 + (8 + s + 1))
                    pe.wait_ge(akv_sb, G * 2 + (s + 1))
                    pe.wait_ge(ys, G * 2)
                    for e in range(2):
                        x_t = xs[:, s, e, P:2 * P]
                        mm(psum[:, 2 + s, e * P:e * P + HD], x_t,
                           tok[slot][:, 0, pr * P + e * HD:pr * P + (e + 1) * HD])
                        last = mm(psum[:, 2 + s, e * P + HD:(e + 1) * P], x_t, akv[:, s, e, :])
                    last.then_inc(pq_ps, 1)

                def moves(G, g, slot, s):
                    pr = 2 * g + s
                    pe.wait_ge(pqs, G * 2 + (s + 1))
                    for j in range(2):
                        if j:
                            pe.wait_ge(mn0_ps, G * 2 + (s + 1))
                        mm(psum[per_e[j], 2 + s, 2 * P:3 * P], pq[:, s, j, 0:HD], mx[g][:, s, j, P:2 * P],
                           start=(j == 0), stop=False, skip_group_check=True)
                        rows, to = per_e[j], j * P
                        for e in range(2):
                            c = slice(pr * P + e * HD, pr * P + (e + 1) * HD)
                            mm(psum[per_e[e], 2 + s, to:to + HD], pq[rows, s, e, 0:HD], tok[slot][rows, 1, c],
                               start=(j == 0 and e == 1), stop=False, skip_group_check=True)
                            mm(psum[per_e[e], 2 + s, to + HD:to + P], tok[slot][rows, 1, c], pq[rows, s, e, HD:P],
                               start=False, stop=False, skip_group_check=True)
                            last = mm(psum[per_e[e], 2 + s, to + HD:to + P], tok[slot][rows, 2, c],
                                      tok[slot][rows, 3, c], start=False, stop=False, skip_group_check=True)
                        last.then_inc((mn0_ps, mn_ps)[j], 1)

                def advance(G, g, s, j):
                    pr = 2 * g + s
                    mm(psum[:, 2 + s, j * P + HD:(j + 1) * P], mt[:, s, j, :], st[:, pr, j, :], start=False,
                       skip_group_check=True).then_inc((ms0_ps, ms1_ps)[j], 1)

                def outputs(G, g, slot, s):
                    pr = 2 * g + s
                    pe.wait_ge(gts, G * 2 + (s + 1))
                    pe.wait_ge(st1s, G * 2 + (s + 1))
                    for e in range(2):
                        if e:
                            pe.wait_ge(y0_ps, G * 2 + (s + 1))
                        out = psum[:, 2 + s, 3 * P + e * HD:3 * P + (e + 1) * HD]
                        mm(out, mx[g][:, s, e, P:2 * P], pq[:, s, e, HD:P], start=False, stop=False,
                           skip_group_check=True)
                        mm(out, mx[g][:, s, e, 3 * P:4 * P],
                           tok[slot][:, 3, pr * P + e * HD:pr * P + (e + 1) * HD],
                           start=False, stop=False, skip_group_check=True)
                        for j in range(2):
                            ins = mm(psum[per_e[j], 2 + s, 3 * P + e * HD:3 * P + (e + 1) * HD],
                                     gt[per_e[e], s, per_e[j]], st[per_e[e], pr, j, :], start=False,
                                     skip_group_check=True)
                        if e == 0:
                            ins.then_inc(y0_ps, 1)
                    advance(G, g, s, 1)

                def turn_out(i):
                    pe.wait_ge(normed, i + 1)
                    flat = sqn[:, :, :].rearrange("p h v -> p (h v)")
                    for ct in range(RW_T):
                        tr = pe.transpose(psum[:, 2, ct * P:(ct + 1) * P], flat[:, ct * P:(ct + 1) * P], ident[:, :])
                    tr.then_inc(y_turned, 1)

                def step(G, g, i, slot, first=False, last=False):
                    tail = not (first and g == 0)
                    before = (G - 1, 1 - g, slot if g else 1 - slot)
                    if g == 0:
                        pe.wait_ge(prepared, i * 4 + 4)
                        pe.wait_ge(toks, i * 4 + 4)
                    if tail:
                        pe.wait_ge(akv_sb, G * 2)
                        pe.wait_ge(x_new, G * 10 - 1)
                    scores(G, g, slot, 0)
                    if tail:
                        if g == 0 and not (isinstance(i, int) and i < 2):
                            pe.wait_ge(y_out, i - 1)
                        for s in range(2):
                            solve(*before, s)
                        moves(*before, 0)

                    def expand(lev, s):
                        if lev == 0:
                            pe.wait_ge(x0, (G * 2 + s) * 2 + 2)
                        mm(psum[:, 4 + 2 * s, 0:2 * P], ident_b[:, 0:P], ident_b[:, :], stop=False,
                           skip_group_check=True)
                        if lev:
                            pe.wait_ge(x_new, G * 10 + (2 * (lev - 1) + s + 1))
                        for e in range(2):
                            ins = mm(psum[:, 4 + 2 * s, e * P:(e + 1) * P], lsb[:, s, e, :],
                                     xs[:, s, e, P:2 * P], start=False, skip_group_check=True)
                        ins.then_inc(z_ps, 1)

                    def double(lev, s):
                        pe.wait_ge(zts, G * 10 + (2 * lev + s + 1))
                        for e in range(2):
                            if lev < 4:
                                mm(psum[:, 5 + 2 * s, e * 2 * P:e * 2 * P + P], zt[:, s, e, :], xs[:, s, e, 0:P])
                            ins = mm(psum[:, 5 + 2 * s, e * 2 * P + P:(e + 1) * 2 * P], xs[:, s, e, 0:P],
                                     zt[:, s, e, :])
                        ins.then_inc(xx_ps, 1)

                    pe.wait_ge(mxs, G * 2 + 1)
                    scores(G, g, slot, 1)
                    for s in range(2):
                        expand(0, s)
                        if tail and s == 0:
                            moves(*before, 1)
                        double(0, s)
                    for lev in range(1, 5):
                        for s in range(2):
                            expand(lev, s)
                        if lev == 1:
                            for s in range(2):
                                a_k_v(G, g, slot, s)
                        if lev == 2 and tail:
                            for s in range(2):
                                pe.wait_ge(mts, (G - 1) * 2 + (s + 1))
                                advance(*before[:2], s, 0)
                        if g == 1 and not last:
                            if lev == 3:
                                pe.wait_ge(akv_sb, G * 2 + 2)
                                turn_tok(i + 1, 1 - slot, 0)
                                turn_tok(i + 1, 1 - slot, 1)
                            if lev == 4:
                                turn_tok(i + 1, 1 - slot, 2)
                        if lev >= 3 and tail:
                            outputs(*before, lev - 3)
                        for s in range(2):
                            double(lev, s)
                    if g == 1 and not last:
                        turn_tok(i + 1, 1 - slot, 3)
                    if g == 1 and not first:
                        pe.wait_ge(ys, G * 2)
                        turn_out(i - 1)

                pe.wait_ge(zeroed, 4)
                pe.wait_ge(ones_in, 2)
                for m in range(4):
                    turn_tok(0, 0, m)
                for_groups(pe, step)
                final = (2 * TT - 1, 1, (TT - 1) % 2)
                pe.wait_ge(y_out, TT - 1)
                for s in range(2):
                    solve(*final, s)
                for s in range(2):
                    moves(*final, s)
                for s in range(2):
                    pe.wait_ge(mts, 2 * (2 * TT - 1) + s + 1)
                    advance(*final[:2], s, 0)
                for s in range(2):
                    outputs(*final, s)
                pe.wait_ge(ys, 4 * TT)
                turn_out(TT - 1)

    def rwkv_finish(tag):
        g2_sb = at(f"{tag}_g2", [P, RWKV_W], F32, W_OFF)
        blk = at(f"{tag}_blk", [P, P], F32, W_OFF + 2048)
        rk = [at(f"{tag}_rk{s}", [P, HALF], F32, T_OFF + 2048 * s) for s in range(2)]
        bonus = [at(f"{tag}_bonus{s}", [P, HALF], F32, T_OFF + 4096 + 2048 * s) for s in range(2)]
        with ExitStack() as ctx:
            loaded, rks, ps, scaled, bonuses, added, gated = sems(
                ctx, tag, "loaded rks ps scaled bonuses added gated")
            block = ctx.enter_context(nc.Block())

            @block.sync
            def _(sp):
                sp.dma_start(g2_sb[:, :], g2).then_inc(loaded, 16)
                sp.dma_start(blk[:, :], consts[:, K_BLK:K_BLK + P]).then_inc(loaded, 16)

            def place(n):
                ct, h = n // 2, n % 2
                return ct, slice(h * HALF, (h + 1) * HALF), n % 2

            @block.tensor
            def _(pe):
                pe.wait_ge(loaded, 32)
                for n in range(2 * RW_T):
                    ct, cols, s = place(n)
                    if n >= 2:
                        pe.wait_ge(gated, n - 1)
                    pe.matmul(psum[:, 2 + s, :], g2_sb[:, ct * P:(ct + 1) * P], z_buf[:, Z_G, cols],
                              start=True, stop=True)
                    pe.wait_ge(rks, n + 1)
                    pe.matmul(psum[:, s, :], blk[:, :], rk[s][:, :], start=True, stop=True).then_inc(ps, 1)

            @block.scalar
            def _(act):
                for n in range(2 * RW_T):
                    ct, cols, s = place(n)
                    y = y_buf[:, RW_T + ct, cols]
                    act.activation(y, cum_buf[:, ct, cols], ACT.Identity, scale=vec[:, V_LW + ct:V_LW + ct + 1],
                                   bias=vec[:, V_LB + ct:V_LB + ct + 1]).then_inc(scaled, 1)

            @block.vector
            def _(dve):
                def product(n):
                    ct, cols, s = place(n)
                    dve.wait_ge(ps, max(n - 1, 0))
                    dve.scalar_tensor_tensor(rk[s][:, :], z_buf[:, Z_R + ct, cols], vec[:, V_RK + ct:V_RK + ct + 1],
                                             z_buf[:, Z_K + ct, cols], ALU.mult, ALU.mult).then_inc(rks, 1)

                def gate(n):
                    ct, cols, s = place(n)
                    y = y_buf[:, RW_T + ct, cols]
                    dve.wait_ge(added, n + 1)
                    dve.tensor_tensor(y, y, psum[:, 2 + s, :], ALU.mult).then_inc(gated, 1)

                product(0)
                for n in range(2 * RW_T):
                    ct, cols, s = place(n)
                    if n + 1 < 2 * RW_T:
                        product(n + 1)
                    dve.wait_ge(ps, n + 1)
                    if n >= 2:
                        dve.wait_ge(added, n - 1)
                    dve.tensor_tensor(bonus[s][:, :], psum[:, s, :], z_buf[:, Z_V + ct, cols], ALU.mult
                                      ).then_inc(bonuses, 1)
                    if n:
                        gate(n - 1)
                gate(2 * RW_T - 1)

            @block.gpsimd
            def _(pool):
                for n in range(2 * RW_T):
                    ct, cols, s = place(n)
                    y = y_buf[:, RW_T + ct, cols]
                    pool.wait_ge(bonuses, n + 1)
                    pool.wait_ge(scaled, n + 1)
                    pool.tensor_tensor(y, y, bonus[s][:, :], ALU.add).then_inc(added, 1)
    setup()
    attention_cols = [[t * width for t in range(3)] for width in (FOX_W, D)]
    with ExitStack() as ctx:
        gate_w = FirstWeights(ctx, "fg", w_in0, [3 * FOX_W], B_OFF + 65536, False)
        fox_w = FirstWeights(ctx, "fw", w_in0, attention_cols[0], W_OFF, True)
        norm("n0", x, False, None, 0, gate_w)
        fox_gates("fg", gate_w, fox_w)
        attention("fox", w_in0, FOX_W, N_FOX // 2, True, fox_w)
    rwkv_project("rp")
    rwkv_prepare("rr")
    rwkv_chunks("rc")
    rwkv_finish("rf")
    clear_semaphores()
    down("o0", w_out0, y_buf, KT, 0)
    with ExitStack() as ctx:
        up_w = FirstWeights(ctx, "uw0", w_up[0], [0, D_FF], W_OFF, False)
        norm("n1", x, True, x_mid[0], 16, up_w)
        ffn_up("u0", 0, up_w)
    down("d0", w_down[0], g_buf, FT, 2)
    clear_semaphores()
    with ExitStack() as ctx:
        dil_w = FirstWeights(ctx, "dw", w_in1, attention_cols[1], W_OFF, True)
        norm("n2", x_mid[0], True, x_mid[1], 8, dil_w)
        attention("dil", w_in1, D, KT, False, dil_w)
    down("o1", w_out1, y_buf, KT, 1)
    clear_semaphores()
    with ExitStack() as ctx:
        up_w = FirstWeights(ctx, "uw1", w_up[1], [0, D_FF], W_OFF, False)
        norm("n3", x_mid[1], True, x_mid[2], 24, up_w)
        ffn_up("u1", 1, up_w)
    down("d1", w_down[1], g_buf, FT, 3)
    norm("n4", x_mid[2], True, out, None)
    top.close()


def kernel(**inputs):
    import concourse.bacc as _bacc
    from concourse.bass_utils import run_bass_kernel_spmd as _run

    def a(name):
        return np.ascontiguousarray(inputs[name])

    consts, dil = constants()
    vecs = np.concatenate([a(n).reshape(-1, P) for n in (
        "norm_mix_pre", "norm_ffn_pre", "rwkv_mu", "rwkv_w0", "rwkv_a0", "rwkv_k_k", "rwkv_k_a",
        "rwkv_r_k", "rwkv_ln_w", "rwkv_ln_b")])
    conv = np.concatenate([a("ffn_conv_w"), a("ffn_conv_b")[:, None]], 1)
    g_post = np.concatenate([a("norm_mix_post"), a("norm_ffn_post")])
    arrays = dict(
        x=a("x")[0], positions=a("positions"), g_post=g_post, vecs=vecs, conv=conv,
        w_in0=a("even_w_in")[0], w_out0=a("even_w_out")[0], w_in1=a("odd_w_in")[0], w_out1=a("odd_w_out")[0],
        w_up=a("ffn_w_up"), w_down=a("ffn_w_down"), forget_bias=a("fox_forget_bias").reshape(N_FOX, 1),
        w2=a("rwkv_w2")[0], a2=a("rwkv_a2")[0], g2=a("rwkv_g2")[0], consts=consts, dil=dil)
    nc = _bacc.Bacc("TRN2", target_bir_lowering=False, num_devices=1)
    args = {n: nc.dram_tensor(f"in_{n}", v.shape, mybir.dt.from_np(v.dtype), kind="ExternalInput").ap()
            for n, v in arrays.items()}
    args["out"] = nc.dram_tensor("out_x", [T, D], F32, kind="ExternalOutput").ap()
    build(nc, **args)
    r = _run(nc, [{f"in_{n}": v for n, v in arrays.items()}], core_ids=[0])
    return np.asarray(r.results[0]["out_x"]).reshape(1, T, D)
```
